# Optimizing a Trainium2 kernel written in Bass

```python
import math
import jax, jax.numpy as jnp
from jax import lax
import numpy as np

D_MODEL = 1024
BATCH = 1
SEQ = 2048
DEPTH = 1

HEAD_DIM = 64
DIFF_V_DIM = 2 * HEAD_DIM
DIFF_HEADS = D_MODEL // (2 * DIFF_V_DIM)
SB_HEAD_DIM = HEAD_DIM
SB_HEADS = D_MODEL // (2 * SB_HEAD_DIM)
MIX_WIDTH = DIFF_HEADS * DIFF_V_DIM + SB_HEADS * SB_HEAD_DIM
DIFF_QK = DIFF_HEADS * 2 * HEAD_DIM
DIFF_V = DIFF_HEADS * DIFF_V_DIM
SB_QKV = SB_HEADS * SB_HEAD_DIM
IN_COLS = 2 * DIFF_QK + DIFF_V + 3 * SB_QKV
ROPE_DIM = HEAD_DIM // 4
ROPE_THETA = 500000.0
D_FF = ((8 * D_MODEL // 3 + 255) // 256) * 256
Q_BLOCK = 128
NORM_EPS = 1e-5

kernel_name = "hybrid_diffattn_stickbreaking_swiglu"

def rmsnorm(x, g, eps=NORM_EPS):
    xf = x.astype(jnp.float32)
    y = xf * lax.rsqrt(jnp.mean(xf * xf, axis=-1, keepdims=True) + eps)
    return (y * g.astype(jnp.float32)).astype(x.dtype)

def partial_rope(t, positions):
    half = ROPE_DIM // 2
    inv_freq = ROPE_THETA ** (-jnp.arange(half, dtype=jnp.float32) / half)
    ang = positions.astype(jnp.float32)[..., None] * inv_freq
    cos = jnp.cos(ang)[:, :, None, :]
    sin = jnp.sin(ang)[:, :, None, :]
    tf = t.astype(jnp.float32)
    x1, x2, rest = tf[..., :half], tf[..., half:ROPE_DIM], tf[..., ROPE_DIM:]
    return jnp.concatenate([x1 * cos - x2 * sin, x2 * cos + x1 * sin, rest], axis=-1)

def to_blocks(t):
    b, s = t.shape[:2]
    return t.reshape(b, s // Q_BLOCK, Q_BLOCK, *t.shape[2:]).swapaxes(0, 1)

def from_blocks(t):
    nb, b, qb = t.shape[:3]
    return t.swapaxes(0, 1).reshape(b, nb * qb, *t.shape[3:])

def differential_attention(q, k, v, lam):
    b, s = q.shape[:2]
    scale = HEAD_DIM ** -0.5
    key_idx = jnp.arange(s)

    def block(args):
        qb, i = args
        sc = jnp.einsum('bqhd,bkhd->bhqk', qb, k) * scale
        q_idx = i * Q_BLOCK + jnp.arange(Q_BLOCK)
        causal = key_idx[None, :] <= q_idx[:, None]
        sc = jnp.where(causal, sc, -jnp.inf)
        p = jax.nn.softmax(sc, axis=-1).reshape(b, DIFF_HEADS, 2, Q_BLOCK, s)
        a = p[:, :, 0] - lam * p[:, :, 1]
        return jnp.einsum('bhqk,bkhd->bqhd', a, v)

    out = lax.map(block, (to_blocks(q), jnp.arange(s // Q_BLOCK)))
    return from_blocks(out)

def stick_breaking_attention(q, k, v):
    b, s = q.shape[:2]
    scale = SB_HEAD_DIM ** -0.5
    key_idx = jnp.arange(s)

    def block(args):
        qb, i = args
        z = jnp.einsum('bqhd,bkhd->bhqk', qb, k) * scale
        q_idx = i * Q_BLOCK + jnp.arange(Q_BLOCK)
        strict = key_idx[None, :] < q_idx[:, None]
        log_beta = jax.nn.log_sigmoid(z)
        log_1mb = jnp.where(strict, jax.nn.log_sigmoid(-z), 0.0)
        later = lax.cumsum(log_1mb, axis=3, reverse=True) - log_1mb
        a = jnp.where(strict, jnp.exp(log_beta + later), 0.0)
        return jnp.einsum('bhqk,bkhd->bqhd', a, v)

    out = lax.map(block, (to_blocks(q), jnp.arange(s // Q_BLOCK)))
    return from_blocks(out)

def setup_inputs(seed: int = 0) -> dict:
    key = jax.random.key(seed)
    ks = jax.random.split(key, 18)
    f32 = jnp.float32

    def nrm(k, shape, scale):
        return jax.random.normal(k, shape, f32) * scale

    def gain(k, shape):
        return 1.0 + 0.02 * jax.random.normal(k, shape, f32)

    x = jax.random.normal(ks[0], (BATCH, SEQ, D_MODEL), f32)
    offset = jax.random.randint(ks[1], (BATCH, 1), 0, 1024, dtype=jnp.int32)
    positions = offset + jnp.arange(SEQ, dtype=jnp.int32)[None, :]
    return {
        "x": x,
        "positions": positions,
        "norm_attn_g": gain(ks[2], (DEPTH, D_MODEL)),
        "w_in": nrm(ks[3], (DEPTH, D_MODEL, IN_COLS), D_MODEL ** -0.5),
        "lambda_q1": nrm(ks[4], (DEPTH, HEAD_DIM), 0.1),
        "lambda_k1": nrm(ks[5], (DEPTH, HEAD_DIM), 0.1),
        "lambda_q2": nrm(ks[6], (DEPTH, HEAD_DIM), 0.1),
        "lambda_k2": nrm(ks[7], (DEPTH, HEAD_DIM), 0.1),
        "diff_subln_g": gain(ks[8], (DEPTH, DIFF_V_DIM)),
        "sb_norm_g": gain(ks[9], (DEPTH, SB_HEAD_DIM)),
        "w_out": nrm(ks[10], (DEPTH, MIX_WIDTH, D_MODEL), MIX_WIDTH ** -0.5),
        "norm_ffn_g": gain(ks[11], (DEPTH, D_MODEL)),
        "w_gate": nrm(ks[12], (DEPTH, D_MODEL, D_FF), D_MODEL ** -0.5),
        "w_up": nrm(ks[13], (DEPTH, D_MODEL, D_FF), D_MODEL ** -0.5),
        "w_down": nrm(ks[14], (DEPTH, D_FF, D_MODEL), D_FF ** -0.5),
        "final_norm_g": gain(ks[15], (D_MODEL,)),
    }

def reference(x, positions, norm_attn_g, w_in, lambda_q1, lambda_k1, lambda_q2, lambda_k2,
              diff_subln_g, sb_norm_g, w_out, norm_ffn_g, w_gate, w_up, w_down, final_norm_g):
    b, s, _ = x.shape
    f32 = jnp.float32
    for layer in range(DEPTH):
        lambda_init = 0.8 - 0.6 * math.exp(-0.3 * layer)
        h = rmsnorm(x, norm_attn_g[layer])
        proj = h @ w_in[layer]
        o1 = DIFF_QK
        o2 = o1 + DIFF_QK
        o3 = o2 + DIFF_V
        o4 = o3 + SB_QKV
        o5 = o4 + SB_QKV
        dq = proj[..., :o1].reshape(b, s, 2 * DIFF_HEADS, HEAD_DIM)
        dk = proj[..., o1:o2].reshape(b, s, 2 * DIFF_HEADS, HEAD_DIM)
        dv = proj[..., o2:o3].reshape(b, s, DIFF_HEADS, DIFF_V_DIM).astype(f32)
        dq = partial_rope(dq, positions)
        dk = partial_rope(dk, positions)
        lam = (jnp.exp(jnp.sum(lambda_q1[layer].astype(f32) * lambda_k1[layer].astype(f32)))
               - jnp.exp(jnp.sum(lambda_q2[layer].astype(f32) * lambda_k2[layer].astype(f32)))
               + lambda_init)
        d_out = differential_attention(dq, dk, dv, lam)
        d_out = rmsnorm(d_out, diff_subln_g[layer]) * (1.0 - lambda_init)
        d_out = d_out.reshape(b, s, DIFF_V).astype(x.dtype)
        sq = proj[..., o3:o4].reshape(b, s, SB_HEADS, SB_HEAD_DIM).astype(f32)
        sk = proj[..., o4:o5].reshape(b, s, SB_HEADS, SB_HEAD_DIM).astype(f32)
        sv = proj[..., o5:].reshape(b, s, SB_HEADS, SB_HEAD_DIM).astype(f32)
        s_out = stick_breaking_attention(sq, sk, sv)
        s_out = rmsnorm(s_out, sb_norm_g[layer]).reshape(b, s, SB_QKV).astype(x.dtype)
        mix = jnp.concatenate([d_out, s_out], axis=-1)
        x = x + mix @ w_out[layer]
        h2 = rmsnorm(x, norm_ffn_g[layer])
        x = x + (jax.nn.silu(h2 @ w_gate[layer]) * (h2 @ w_up[layer])) @ w_down[layer]
    return rmsnorm(x, final_norm_g)


_drawn_inputs = setup_inputs


def setup_inputs(seed=0):
    import zlib

    import numpy as np

    out = dict(_drawn_inputs(seed))
    spreads = {}
    factors = {'lambda_k1': 3.969,
     'lambda_q2': 4.241,
     'diff_subln_g': 5.965,
     'sb_norm_g': 4.571,
     'norm_ffn_g': 4.836,
     'final_norm_g': 2.862}
    for name, (base, spread) in spreads.items():
        noise = np.random.default_rng([zlib.crc32(name.encode()), seed]).standard_normal(out[name].shape)
        drawn = base * np.exp(spread * noise) if base else spread * noise
        out[name] = __import__('jax').numpy.asarray(drawn.astype(out[name].dtype))
    for name, factor in factors.items():
        out[name] = (out[name] * factor).astype(out[name].dtype)
    return out
```

```python
import math
from contextlib import ExitStack

import numpy as np
import concourse.bass as bass
from concourse import mybir

F32 = mybir.dt.float32
F32R = mybir.dt.float32r
BF16 = mybir.dt.bfloat16
I32 = mybir.dt.int32
ALU = mybir.AluOpType
ACT = mybir.ActivationFunctionType
AX = mybir.AxisListType
ds = bass.ds

P = 128
SEQ = 2048
D_MODEL = 1024
HEAD_DIM = 64
D_FF = 2816
EPS = 1e-5
KC = D_MODEL // P
TOK_TILES = SEQ // P
BLK = 512
BLOCKS = SEQ // BLK
TPB = BLK // P
GROUP = 512
HEADS = GROUP // HEAD_DIM
QK_TILES = GROUP // P
COL = {"dq": 0, "dk": 512, "dv": 1024, "sq": 1536, "sk": 2048, "sv": 2560}
SCALE = HEAD_DIM ** -0.5
LAMBDA_INIT = 0.8 - 0.6 * math.exp(-0.3 * 0)


MAGIC = 1.5 * 2 ** 23


def two_pi_parts():
    first = 6.28125
    second = math.floor((2 * math.pi - first) * 2 ** 19) / 2 ** 19
    return first, second, 2 * math.pi - first - second


TWO_PI = two_pi_parts()


def link(eng, sem, value, instruction):
    instruction.then_inc(sem, 1)
    eng.wait_ge(sem, value)


def phase_norm(nc, x, g_row_dram, ident, hT_hi, hT_lo):
    ctx = ExitStack()
    with ctx:
        sb = lambda n, s, d=F32: ctx.enter_context(nc.sbuf_tensor(n, s, d))
        sem = lambda n: ctx.enter_context(nc.semaphore(n))
        xt = sb("a_x", [P, TOK_TILES, D_MODEL])
        g_row = sb("a_g", [P, D_MODEL])
        junk = sb("a_junk", [P, D_MODEL])
        sumsq = sb("a_sumsq", [P, TOK_TILES])
        var = sb("a_var", [P, TOK_TILES])
        lnv = sb("a_lnv", [P, TOK_TILES])
        y0 = sb("a_y0", [P, TOK_TILES])
        nt = sb("a_newton", [P, TOK_TILES])
        rstd = sb("a_rstd", [P, TOK_TILES])
        bank = [ctx.enter_context(nc.psum_tensor(f"a_ps{i}", [P, 512], F32)) for i in range(8)]
        x_loaded = [sem(f"a_x_loaded{g}") for g in range(BLOCKS)]
        g_loaded = sem("a_g_loaded")
        squared, var_ready, ln_ready, y0_ready = sem("a_squared"), sem("a_var"), sem("a_ln"), sem("a_y0")
        dve_chain, scaled, turned = sem("a_dve"), sem("a_scaled"), sem("a_turned")
        hi_ready, lo_ready, act_chain = sem("a_hi"), sem("a_lo"), sem("a_act")
        xs = x.rearrange("(g t p) n -> g p t n", t=TPB, p=P)
        block = ctx.enter_context(nc.Block())

        @block.sync
        def _(sp):
            for g in range(BLOCKS):
                sp.dma_start(xt[:, g * TPB:(g + 1) * TPB, :], xs[g]).then_inc(x_loaded[g], 16)
                if g == 0:
                    sp.dma_start(g_row[:], g_row_dram).then_inc(g_loaded, 16)

        @block.scalar
        def _(act):
            def stats(g):
                act.wait_ge(x_loaded[g], 16)
                for t in range(g * TPB, (g + 1) * TPB):
                    if t:
                        act.wait_ge(squared, t)
                    act.activation(junk[:], xt[:, t, :], ACT.Square,
                                   accum_out=sumsq[:, t:t + 1]).then_inc(squared, 1)
                own = slice(g * TPB, (g + 1) * TPB)
                act.wait_ge(var_ready, g + 1)
                act.activation(lnv[:, own], var[:, own], ACT.Ln).then_inc(ln_ready, 1)
                act.wait_ge(ln_ready, g + 1)
                act.activation(y0[:, own], lnv[:, own], ACT.Exp, scale=-0.5).then_inc(y0_ready, 1)

            stats(0)
            for g in range(BLOCKS):
                if g + 1 < BLOCKS:
                    stats(g + 1)
                for u in range(2 * TPB):
                    t, half = g * TPB + u // 2, u % 2
                    act.wait_ge(turned, 2 * t + half + 1)
                    act.activation(hT_hi[:, 4 * half:4 * half + 4, t * P:(t + 1) * P],
                                   bank[u][:].rearrange("p (k t) -> p k t", k=4), ACT.Copy)\
                       .then_inc(hi_ready, 1)

        @block.vector
        def _(dve):
            n = [0]

            def chain(instruction):
                n[0] += 1
                link(dve, dve_chain, n[0], instruction)

            def scale_rows(g):
                own = slice(g * TPB, (g + 1) * TPB)
                dve.wait_ge(squared, (g + 1) * TPB)
                dve.tensor_scalar(var[:, own], sumsq[:, own], 1.0 / D_MODEL, EPS, ALU.mult, ALU.add)\
                   .then_inc(var_ready, 1)
                dve.wait_ge(y0_ready, g + 1)
                chain(dve.tensor_tensor(nt[:, own], y0[:, own], y0[:, own], ALU.mult))
                chain(dve.tensor_tensor(nt[:, own], nt[:, own], var[:, own], ALU.mult))
                chain(dve.tensor_scalar(nt[:, own], nt[:, own], -0.5, 1.5, ALU.mult, ALU.add))
                chain(dve.tensor_tensor(rstd[:, own], nt[:, own], y0[:, own], ALU.mult))
                if g == 0:
                    dve.wait_ge(g_loaded, 16)
                for t in range(g * TPB, (g + 1) * TPB):
                    dve.scalar_tensor_tensor(out=xt[:, t, :], in0=xt[:, t, :], scalar=rstd[:, t:t + 1],
                                             in1=g_row[:], op0=ALU.mult, op1=ALU.mult).then_inc(scaled, 1)

            scale_rows(0)
            for g in range(BLOCKS):
                if g + 1 < BLOCKS:
                    scale_rows(g + 1)
                for u in range(2 * TPB):
                    t, half = g * TPB + u // 2, u % 2
                    dst = (slice(None), slice(4 * half, 4 * half + 4), slice(t * P, (t + 1) * P))
                    dve.wait_ge(hi_ready, 2 * t + half + 1)
                    dve.tensor_tensor(hT_lo[dst], bank[u][:].rearrange("p (k t) -> p k t", k=4),
                                      hT_hi[dst].bitcast(F32), ALU.subtract).then_inc(lo_ready, 1)

        @block.tensor
        def _(pe):
            for t in range(TOK_TILES):
                pe.wait_ge(scaled, t + 1)
                for half in range(2):
                    u = (2 * t + half) % 8
                    if 2 * t + half >= 8:
                        pe.wait_ge(lo_ready, 2 * t + half - 7)
                    for k in range(4):
                        c = 4 * half + k
                        mm = pe.transpose(bank[u][:, k * P:(k + 1) * P], xt[:, t, c * P:(c + 1) * P], ident[:])
                    mm.then_inc(turned, 1)


QK_ORDER = ["sq", "sk", "dq", "dk"]
PAIRS = QK_TILES // 2
ALL_PAIRS = len(QK_ORDER) * PAIRS


def phase_qk(nc, w_qk, positions, invf_dram, perm_dram, hT_hi, hT_lo, qk_scratch):
    ctx = ExitStack()
    with ctx:
        sb = lambda n, s, d=F32: ctx.enter_context(nc.sbuf_tensor(n, s, d))
        sem = lambda n: ctx.enter_context(nc.semaphore(n))
        w_raw = [sb(f"b_wraw{s}", [P, KC, P]) for s in range(2)]
        w_hi = [sb(f"b_whi{s}", [P, KC, P], F32R) for s in range(2)]
        w_lo = [sb(f"b_wlo{s}", [P, KC, P], F32R) for s in range(2)]
        out_hi = sb("b_ohi", [P, BLOCKS, BLK], F32R)
        out_lo = sb("b_olo", [P, BLOCKS, BLK], F32R)
        cosT, sinT = sb("b_cos", [P, SEQ]), sb("b_sin", [P, SEQ])
        raw_qk, turned = sb("b_rawqk", [P, 2, BLK]), sb("b_turned", [P, 2, BLK])
        turns, part = sb("b_turns", [P, SEQ // 2]), sb("b_part", [P, SEQ // 2])
        invf, perm = sb("b_invf", [P, 1]), sb("b_perm", [P, P])
        bank = [ctx.enter_context(nc.psum_tensor(f"b_ps{i}", [P, BLK], F32)) for i in range(BLOCKS)]
        rot_bank = [ctx.enter_context(nc.psum_tensor(f"b_rot{i}", [P, BLK], F32)) for i in range(2)]
        w_loaded = [sem(f"b_w_loaded{s}") for s in range(2)]
        hi_split, lo_split = sem("b_hi_split"), sem("b_lo_split")
        projected = sem("b_projected")
        hi_out = sem("b_hi_out")
        unit_done = sem("b_unit_done")
        raw_copied, rotated, summed = sem("b_raw"), sem("b_rotated"), sem("b_summed")
        dve_chain, pool_chain = sem("b_dve"), sem("b_pool")
        stored = [sem(f"b_stored{b}") for b in range(BLOCKS)]
        consts, table_ready = sem("b_const"), sem("b_table")
        first_rot = 2 * QK_TILES * BLOCKS

        def kinds(eng, n, kind, body):
            if kind != QK_ORDER[-1]:
                with eng.Fori(0, PAIRS) as i:
                    for s in range(2):
                        pair = i + n * PAIRS
                        body(pair * 2 + s, pair, s, kind, False)
            else:
                for i in range(PAIRS):
                    for s in range(2):
                        pair = n * PAIRS + i
                        body(2 * pair + s, pair, s, kind, 2 * i + s == QK_TILES - 1)

        block = ctx.enter_context(nc.Block())

        @block.sync
        def _(sp):
            def store(n, b):
                sp.wait_ge(unit_done, n * BLOCKS + (b + 5))
                for part_no, src in ((0, out_hi), (1, out_lo)):
                    sp.dma_start(qk_scratch[part_no, ds(n * P, P), b * BLK:(b + 1) * BLK],
                                 src[:, b, :].bitcast(F32)).then_inc(stored[b], 16)

            for s in range(2):
                sp.dma_start(w_raw[s][:], w_qk[s]).then_inc(w_loaded[s], 16)
            sp.dma_start(cosT[:].bitcast(I32), positions[0, :].partition_broadcast(P)).then_inc(consts, 16)
            sp.dma_start(invf[:], invf_dram).then_inc(consts, 16)
            sp.dma_start(perm[:], perm_dram).then_inc(consts, 16)
            with sp.Fori(0, ALL_PAIRS - 1) as pair:
                for s in range(2):
                    n = pair * 2 + s
                    sp.wait_ge(lo_split, n + 1)
                    sp.dma_start(w_raw[s][:], w_qk[ds(n + 2, 1)].rearrange("o p c n -> (o p) c n"))\
                      .then_inc(w_loaded[s], 16)
                    for b in range(BLOCKS):
                        store(n, b)
            for n in (2 * ALL_PAIRS - 2, 2 * ALL_PAIRS - 1):
                for b in range(BLOCKS):
                    store(n, b)
            for b in range(BLOCKS):
                sp.wait_ge(stored[b], 2 * ALL_PAIRS * 32)

        @block.gpsimd
        def _(pool):
            pool.wait_ge(consts, 48)
            step = [0]

            def chain(instruction):
                step[0] += 1
                link(pool, pool_chain, step[0], instruction)

            for cols in (slice(0, SEQ // 2), slice(SEQ // 2, SEQ)):
                cos, sin = cosT[:, cols], sinT[:, cols]
                chain(pool.tensor_copy(cos, cos.bitcast(I32)))
                chain(pool.tensor_scalar(cos, cos, invf[:, 0:1], 1.0, ALU.mult, ALU.mult))
                for table, quarter in ((sin, 0.0), (cos, 0.25)):
                    chain(pool.tensor_scalar(turns[:], cos, 1.0 / (2 * math.pi), quarter, ALU.mult, ALU.add))
                    chain(pool.tensor_scalar(turns[:], turns[:], MAGIC, -MAGIC, ALU.add, ALU.add))
                    chain(pool.tensor_scalar(part[:], turns[:], -TWO_PI[0], 1.0, ALU.mult, ALU.mult))
                    chain(pool.tensor_tensor(table, cos, part[:], ALU.add))
                    chain(pool.tensor_scalar(part[:], turns[:], -TWO_PI[1], 1.0, ALU.mult, ALU.mult))
                    chain(pool.tensor_tensor(table, table, part[:], ALU.add))
                    chain(pool.tensor_scalar(part[:], turns[:], -TWO_PI[2], quarter * 2 * math.pi,
                                             ALU.mult, ALU.add))
                    chain(pool.tensor_tensor(table, table, part[:], ALU.add))
                    chain(pool.tensor_scalar(table, table, 3.1415925, -3.1415925, ALU.min, ALU.max))

        @block.scalar
        def _(act):
            def split_hi(pair, s, tiles_done):
                act.wait_ge(w_loaded[s], pair * 16 + 16)
                act.wait_ge(projected, tiles_done * BLOCKS)
                act.activation(w_hi[s][:], w_raw[s][:], ACT.Copy).then_inc(hi_split, 1)

            def evac(n, pair, s, kind, last):
                scale = SCALE if kind[1] == "q" else 1.0
                for b in range(BLOCKS):
                    if b == 1 and not last:
                        split_hi(pair + s, 1 - s, n)
                    act.wait_ge(projected, n * BLOCKS + (b + 1))
                    if kind[0] == "s":
                        act.wait_ge(stored[b], n * 32)
                        act.activation(out_hi[:, b, :], bank[b][:], ACT.Copy, scale=scale).then_inc(hi_out, 1)
                    else:
                        act.activation(raw_qk[:, b % 2, :], bank[b][:], ACT.Copy, scale=scale)\
                           .then_inc(raw_copied, 1)
                        act.wait_ge(summed, n * BLOCKS + (b + 1 - first_rot))
                        act.wait_ge(stored[b], n * 32)
                        act.activation(out_hi[:, b, :], turned[:, b % 2, :], ACT.Copy).then_inc(hi_out, 1)

            for n, kind in enumerate(QK_ORDER):
                if n == 0:
                    split_hi(0, 0, 0)
                if kind == "dq":
                    act.wait_ge(pool_chain, 20 * 2)
                    act.activation(sinT[:], sinT[:], ACT.Sin).then_inc(table_ready, 1)
                    act.activation(cosT[:], cosT[:], ACT.Sin).then_inc(table_ready, 1)
                kinds(act, n, kind, evac)

        @block.vector
        def _(dve):
            def split_lo(n, s):
                dve.wait_ge(hi_split, n + 1)
                dve.tensor_tensor(w_lo[s][:], w_raw[s][:], w_hi[s][:].bitcast(F32), ALU.subtract)\
                   .then_inc(lo_split, 1)

            def evac(n, pair, s, kind, last):
                scale = SCALE if kind[1] == "q" else 1.0
                for b in range(BLOCKS):
                    if b == 1 and not last:
                        split_lo(n + 1, 1 - s)
                    hi = out_hi[:, b, :].bitcast(F32)
                    if kind[0] == "s":
                        dve.wait_ge(stored[b], n * 32)
                        dve.wait_ge(hi_out, n * BLOCKS + (b + 1))
                        dve.scalar_tensor_tensor(out=out_lo[:, b, :], in0=bank[b][:], scalar=scale, in1=hi,
                                                 op0=ALU.mult, op1=ALU.subtract).then_inc(unit_done, 1)
                    else:
                        rot = n * BLOCKS + (b - first_rot)
                        sin, cos = sinT[:, b * BLK:(b + 1) * BLK], cosT[:, b * BLK:(b + 1) * BLK]
                        slot = (slice(None), b % 2, slice(None))
                        dve.wait_ge(rotated, rot + 1)
                        link(dve, dve_chain, rot * 2 + 1,
                             dve.tensor_tensor(turned[slot], rot_bank[b % 2][:], sin, ALU.mult))
                        link(dve, dve_chain, rot * 2 + 2,
                             dve.tensor_tensor(raw_qk[slot], raw_qk[slot], cos, ALU.mult))
                        dve.tensor_tensor(turned[slot], turned[slot], raw_qk[slot], ALU.add).then_inc(summed, 1)
                        dve.wait_ge(summed, rot + 1)
                        dve.wait_ge(stored[b], n * 32)
                        dve.wait_ge(hi_out, n * BLOCKS + (b + 1))
                        dve.tensor_tensor(out_lo[:, b, :], turned[slot], hi, ALU.subtract).then_inc(unit_done, 1)

            dve.sem_inc(unit_done, BLOCKS)
            for n, kind in enumerate(QK_ORDER):
                if n == 0:
                    split_lo(0, 0)
                if kind == "dq":
                    dve.wait_ge(table_ready, 2)
                kinds(dve, n, kind, evac)

        @block.tensor
        def _(pe):
            def rotate(n, b):
                rot = n * BLOCKS + (b - first_rot)
                pe.wait_ge(raw_copied, rot + 1)
                pe.matmul(rot_bank[b % 2][:], perm[:], raw_qk[:, b % 2, :], start=True, stop=True)\
                  .then_inc(rotated, 1)

            def project(n, pair, s, kind, last):
                pe.wait_ge(lo_split, n + 1)
                for b in range(BLOCKS):
                    pe.wait_ge(unit_done, n * BLOCKS + (b + 1))
                    cols = slice(b * BLK, (b + 1) * BLK)
                    for c in range(KC):
                        for w, h in ((w_hi, hT_hi), (w_lo, hT_hi), (w_hi, hT_lo)):
                            mm = pe.matmul(bank[b][:], w[s][:, c, :], h[:, c, cols],
                                           start=(c == 0 and w is w_hi and h is hT_hi),
                                           stop=(c == KC - 1 and h is hT_lo))
                        if c == 2 and b and kind[0] == "d":
                            rotate(n, b - 1)
                    mm.then_inc(projected, 1)
                if kind[0] == "d":
                    rotate(n, BLOCKS - 1)

            for n, kind in enumerate(QK_ORDER):
                kinds(pe, n, kind, project)


def phase_v(nc, w_v, hT_hi, hT_lo, v_scratch):
    ctx = ExitStack()
    with ctx:
        sb = lambda n, s, d=F32: ctx.enter_context(nc.sbuf_tensor(n, s, d))
        sem = lambda n: ctx.enter_context(nc.semaphore(n))
        w_raw = [sb(f"c_wraw{s}", [P, GROUP]) for s in range(2)]
        w_hi, w_lo = sb("c_whi", [P, 2, KC, GROUP], F32R), sb("c_wlo", [P, 2, KC, GROUP], F32R)
        v_out = sb("c_out", [P, 4, GROUP])
        bank = [ctx.enter_context(nc.psum_tensor(f"c_ps{i}", [P, GROUP], F32)) for i in range(4)]
        w_loaded = [sem(f"c_w_loaded{s}") for s in range(2)]
        hi_split, lo_split = sem("c_hi_split"), sem("c_lo_split")
        projected, copied = sem("c_projected"), sem("c_copied")
        stored = [sem(f"c_stored{i}") for i in range(4)]
        block = ctx.enter_context(nc.Block())

        @block.sync
        def _(sp):
            for n in range(2 * KC):
                if n >= 2:
                    sp.wait_ge(lo_split, n - 1)
                sp.dma_start(w_raw[n % 2][:], w_v[n // KC, n % KC]).then_inc(w_loaded[n % 2], 16)
            with sp.Fori(0, 2) as group:
                for t in range(TOK_TILES):
                    sp.wait_ge(copied, group * TOK_TILES + (t + 5))
                    sp.dma_start(v_scratch[ds(group, 1), t * P:(t + 1) * P, :].rearrange("o p n -> (o p) n"),
                                 v_out[:, t % 4, :]).then_inc(stored[t % 4], 16)
            for i in range(4):
                sp.wait_ge(stored[i], 16 * 2 * TOK_TILES // 4)

        @block.vector
        def _(dve):
            for n in range(2 * KC):
                dve.wait_ge(hi_split, n + 1)
                dve.tensor_tensor(w_lo[:, n // KC, n % KC, :], w_raw[n % 2][:],
                                  w_hi[:, n // KC, n % KC, :].bitcast(F32), ALU.subtract).then_inc(lo_split, 1)

        @block.scalar
        def _(act):
            for n in range(2 * KC):
                act.wait_ge(w_loaded[n % 2], 16 * (n // 2 + 1))
                act.activation(w_hi[:, n // KC, n % KC, :], w_raw[n % 2][:], ACT.Copy).then_inc(hi_split, 1)
            act.sem_inc(copied, 4)
            with act.Fori(0, 2) as group:
                for t in range(TOK_TILES):
                    act.wait_ge(projected, group * TOK_TILES + (t + 1))
                    act.wait_ge(stored[t % 4], group * (16 * TOK_TILES // 4) + 16 * (t // 4))
                    act.activation(v_out[:, t % 4, :], bank[t % 4][:], ACT.Copy).then_inc(copied, 1)

        @block.tensor
        def _(pe):
            with pe.Fori(0, 2) as group:
                for t in range(TOK_TILES):
                    pe.wait_ge(copied, group * TOK_TILES + (t + 1))
                    for c in range(KC):
                        if t == 0:
                            pe.wait_ge(lo_split, group * KC + (c + 1))
                        for h, w in ((hT_hi, w_hi), (hT_lo, w_hi), (hT_hi, w_lo)):
                            mm = pe.matmul(bank[t % 4][:], h[:, c, t * P:(t + 1) * P],
                                           w[:, ds(group, 1), c, :].rearrange("p o n -> p (o n)"),
                                           start=(c == 0 and h is hT_hi and w is w_hi),
                                           stop=(c == KC - 1 and w is w_lo))
                    mm.then_inc(projected, 1)


CHUNK = 1024
CHUNK_TILES = CHUNK // P
KEY_PIECES = [0, 256, 768, 2048]
PIECE_OF_TILE = [next(p for p in range(3) if (i + 1) * P <= KEY_PIECES[p + 1]) for i in range(TOK_TILES)]


def chunks_of(i):
    return [(k, min(CHUNK_TILES, i + 1 - k)) for k in range(0, i + 1, CHUNK_TILES)]


def load_keys_values(sp, k_st, v_sb, qk_scratch, v_scratch, k_row, group, kv_loaded, pieces):
    for piece in pieces:
        if piece:
            sp.wait_ge(kv_loaded[piece - 1], 48)
        a, b = KEY_PIECES[piece], KEY_PIECES[piece + 1]
        for part in range(2):
            sp.dma_start(k_st[part * HEAD_DIM:(part + 1) * HEAD_DIM, :, a:b].bitcast(F32),
                         qk_scratch[part, k_row:k_row + GROUP, a:b].rearrange("(h r) t -> r h t", r=HEAD_DIM))\
              .then_inc(kv_loaded[piece], 16)
        sp.dma_start(v_sb[:, a // P:b // P, :], v_scratch[group, a:b, :].rearrange("(k p) n -> p k n", p=P))\
          .then_inc(kv_loaded[piece], 16)


def load_query(sp, q_slot, qk_scratch, q_row, head, i, q_loaded):
    for half in range(2):
        sp.dma_start(q_slot[half * HEAD_DIM:(half + 1) * HEAD_DIM, :, :].bitcast(F32),
                     qk_scratch[:, ds(head * HEAD_DIM + q_row, HEAD_DIM), i * P:(i + 1) * P]
                     .rearrange("l r t -> r l t")).then_inc(q_loaded, 16)


def score_matmuls(pe, z, q_slot, k_st, head, key_tile, tiles, diagonal, ident_bf, mask_bf):
    for first in range(0, tiles, 4):
        n = min(4, tiles - first)
        cols = ds(head * SEQ + (key_tile + first) * P, n * P)
        keys = k_st[:].rearrange("p h t -> p (h t)")[:, cols]
        out = z[:, first * P:(first + n) * P]
        pe.matmul(out, q_slot[:, 0, :], keys, start=True, stop=False)
        if diagonal and first + n == tiles:
            pe.matmul(out[:, (n - 1) * P:n * P], ident_bf[:], mask_bf[:], start=False, stop=False)
        mm = pe.matmul(out, q_slot[:, 1, :], keys, start=False, stop=True)
    return mm


NORM_SEMS = ["o_copied", "squared", "summed", "pool_chain", "normed_ready", "g_loaded"]


def norm_tiles(pool, S, stored, heads_out, normed, squares, g_rep, sumsq, var, rstd, exponent, dim, factor,
               mix_scratch, mix_col):
    by_head = lambda t: t.rearrange("p (h d) -> p h d", d=dim)
    link(pool, S["pool_chain"], 1, pool.memset(exponent[:], -0.5))
    pool.wait_ge(S["g_loaded"], 16)
    link(pool, S["pool_chain"], 2, pool.tensor_scalar(g_rep[:], g_rep[:], factor, 1.0, ALU.mult, ALU.mult))
    n = 2
    for i in range(TOK_TILES):
        src, dst = heads_out[:, i % 2, :], normed[:, i % 2, :]
        pool.wait_ge(S["o_copied"], i + 1)
        if i >= 1:
            pool.wait_ge(S["summed"], i)
        pool.tensor_tensor(squares[:], src, src, ALU.mult).then_inc(S["squared"], 1)
        if i >= 2:
            pool.wait_ge(stored[i % 2], 16 * (i // 2))
        link(pool, S["pool_chain"], n + 1, pool.tensor_tensor(dst, src, g_rep[:], ALU.mult))
        pool.wait_ge(S["summed"], i + 1)
        link(pool, S["pool_chain"], n + 2,
             pool.tensor_scalar(var[:], sumsq[:], 1.0 / dim, EPS, ALU.mult, ALU.add))
        link(pool, S["pool_chain"], n + 3, pool.tensor_tensor(rstd[:], var[:], exponent[:], ALU.pow))
        n += 3
        pool.tensor_tensor(by_head(dst), by_head(dst), rstd[:].unsqueeze(2).to_broadcast([P, GROUP // dim, dim]),
                           ALU.mult).then_inc(S["normed_ready"], 1)
        pool.wait_ge(S["normed_ready"], i + 1)
        pool.dma_start(mix_scratch[i * P:(i + 1) * P, mix_col:mix_col + GROUP], dst).then_inc(stored[i % 2], 16)
    for s in range(2):
        pool.wait_ge(stored[s], 16 * (TOK_TILES // 2))


def sum_squares(dve, S, sumsq, squares, dim, i):
    dve.wait_ge(S["squared"], i + 1)
    if i >= 1:
        dve.wait_ge(S["normed_ready"], i)
    dve.tensor_reduce(sumsq[:], squares[:].rearrange("p (h d) -> p h d", d=dim), AX.X, ALU.add)\
       .then_inc(S["summed"], 1)


def copy_heads(act, S, heads_out, o_bank, applied, i):
    act.wait_ge(S["applied"], applied)
    if i >= 2:
        act.wait_ge(S["normed_ready"], i - 1)
    act.activation(heads_out[:, i % 2, :], o_bank[i % 2][:], ACT.Copy).then_inc(S["o_copied"], 1)


def phase_stick_breaking(nc, qk_scratch, v_scratch, g_rep_dram, ident, ident_bf, mask_bf, mix_scratch):
    q_row, k_row = 0, GROUP
    dim = HEAD_DIM
    ctx = ExitStack()
    with ctx:
        sb = lambda n, s, d=F32: ctx.enter_context(nc.sbuf_tensor(n, s, d))
        sem = lambda n: ctx.enter_context(nc.semaphore(n))
        k_st = sb("e_k", [P, HEADS, SEQ], F32R)
        v_sb = sb("e_v", [P, TOK_TILES, GROUP])
        q_st = [sb(f"e_q{s}", [P, 2, P], F32R) for s in range(2)]
        work = [sb(f"e_work{s}", [P, CHUNK]) for s in range(2)]
        attn = [sb(f"e_attn{s}", [P, CHUNK]) for s in range(2)]
        attn_t = [sb(f"e_attn_t{s}", [P, CHUNK]) for s in range(2)]
        carry = sb("e_carry", [P, 1])
        heads_out, normed = sb("e_heads", [P, 2, GROUP]), sb("e_normed", [P, 2, GROUP])
        squares = sb("e_squares", [P, GROUP])
        g_rep = sb("e_g", [P, GROUP])
        sumsq, var, rstd, exponent = (sb(f"e_{n}", [P, HEADS]) for n in ("sumsq", "var", "rstd", "exponent"))
        z = [ctx.enter_context(nc.psum_tensor(f"e_z{s}", [P, CHUNK], F32)) for s in range(2)]
        t_bank = ctx.enter_context(nc.psum_tensor("e_t", [P, CHUNK], F32))
        o_bank = [ctx.enter_context(nc.psum_tensor(f"e_o{s}", [P, GROUP], F32)) for s in range(2)]
        kv_loaded = [sem(f"e_kv{p}") for p in range(3)]
        q_loaded = [sem(f"e_q_loaded{s}") for s in range(2)]
        names = ["scored", "exped", "clipped", "logged", "plused", "scanned", "carried", "subbed", "attn_done",
                 "transposed", "evacuated", "applied"]
        S = {n: sem(f"e_{n}") for n in names + NORM_SEMS}
        stored = [sem(f"e_stored{s}") for s in range(2)]

        pairs_of = [HEADS // 2 * len(chunks_of(i)) for i in range(TOK_TILES)]
        first_step = [2 * sum(pairs_of[:i]) for i in range(TOK_TILES + 1)]

        def step(i, pair, s):
            chunks = chunks_of(i)
            two = len(chunks) == 2
            key_tile, tiles = chunks[1 - s] if two else chunks[0]
            return dict(i=i, s=s, g=pair * 2 + (first_step[i] + s), pair=pair + first_step[i] // 2,
                        head=pair if two else pair * 2 + s, key_tile=key_tile, tiles=tiles, width=tiles * P,
                        diagonal=key_tile + tiles == i + 1, opens=not two or s == 0, closes=not two or s == 1,
                        first=(i == 0 and s == 0), two=two)

        def schedule(eng, body, tile_end):
            late = [None, None]
            for i in range(TOK_TILES):
                a, b = step(i, 0, 0), step(i, 0, 1)
                body(a, late[1], late[0])
                body(b, a, late[1])
                if i:
                    tile_end(i - 1)
                def one(pair):
                    before = [step(i, pair - 1, s) for s in range(2)]
                    now = [step(i, pair, s) for s in range(2)]
                    body(now[0], before[1], before[0])
                    body(now[1], now[0], before[1])

                if i == 0:
                    for pair in range(1, pairs_of[i]):
                        one(pair)
                else:
                    with eng.Fori(1, pairs_of[i]) as pair:
                        one(pair)
                late = [step(i, pairs_of[i] - 1, s) for s in range(2)]
            body(None, late[1], late[0])
            body(None, None, late[1])
            tile_end(TOK_TILES - 1)

        block = ctx.enter_context(nc.Block())

        @block.sync
        def _(sp):
            def body(cur, prev, prev2):
                if cur is None:
                    return
                if prev2 is not None:
                    sp.wait_ge(S["scored"], cur["g"] - 1)
                load_query(sp, q_st[cur["s"]], qk_scratch, q_row, cur["head"], cur["i"], q_loaded[cur["s"]])
                if cur["first"] and prev is None:
                    load_keys_values(sp, k_st, v_sb, qk_scratch, v_scratch, k_row, 1, kv_loaded, [0])
                    sp.dma_start(g_rep[:], g_rep_dram).then_inc(S["g_loaded"], 16)

            def tile_end(i):
                pass

            schedule(sp, body, tile_end)

        @block.tensor
        def _(pe):
            def body(cur, prev, prev2):
                if cur is not None:
                    if cur["s"] == 0 and (cur["i"] == 0 or PIECE_OF_TILE[cur["i"]] != PIECE_OF_TILE[cur["i"] - 1]) \
                            and (prev is None or prev["i"] != cur["i"]):
                        pe.wait_ge(kv_loaded[PIECE_OF_TILE[cur["i"]]], 48)
                    pe.wait_ge(q_loaded[cur["s"]], cur["pair"] * 32 + 32)
                    if prev2 is not None:
                        pe.wait_ge(S["subbed"], cur["g"] - 1)
                    score_matmuls(pe, z[cur["s"]], q_st[cur["s"]], k_st, cur["head"], cur["key_tile"],
                                  cur["tiles"], cur["diagonal"], ident_bf, mask_bf).then_inc(S["scored"], 1)
                if prev2 is not None:
                    pe.wait_ge(S["attn_done"], prev2["g"] + 1)
                    for j in range(prev2["tiles"]):
                        mm = pe.transpose(t_bank[:, j * P:(j + 1) * P], attn[prev2["s"]][:, j * P:(j + 1) * P], ident[:])
                    mm.then_inc(S["transposed"], 1)
                    o = o_bank[prev2["i"] % 2]
                    pe.wait_ge(S["evacuated"], prev2["g"] + 1)
                    if prev2["i"] >= 2 and prev2["s"] == 0:
                        pe.wait_ge(S["o_copied"], prev2["i"] - 1)
                    for j in range(prev2["tiles"]):
                        mm = pe.matmul(o[:, ds(prev2["head"] * dim, dim)], attn_t[prev2["s"]][:, j * P:(j + 1) * P],
                                       v_sb[:, prev2["key_tile"] + j, ds(prev2["head"] * dim, dim)],
                                       start=(prev2["opens"] and j == 0),
                                       stop=(prev2["closes"] and j == prev2["tiles"] - 1))
                    mm.then_inc(S["applied"], 1)

            schedule(pe, body, lambda i: None)

        @block.scalar
        def _(act):
            def body(cur, prev, prev2):
                if cur is not None:
                    w, s = cur["width"], cur["s"]
                    act.wait_ge(S["scored"], cur["g"] + 1)
                    if prev2 is not None:
                        act.wait_ge(S["attn_done"], cur["g"] - 1)
                    act.activation(work[s][:, 0:w], z[s][:, 0:w], ACT.Exp).then_inc(S["exped"], 1)
                if prev2 is not None:
                    act.wait_ge(S["transposed"], prev2["g"] + 1)
                    act.wait_ge(S["applied"], s_before(prev2))
                    act.activation(attn_t[prev2["s"]][:, 0:prev2["width"]], t_bank[:, 0:prev2["width"]], ACT.Copy)\
                       .then_inc(S["evacuated"], 1)
                if cur is not None:
                    act.wait_ge(S["clipped"], cur["g"] + 1)
                    act.activation(work[s][:, 0:w], work[s][:, 0:w], ACT.Ln, bias=1.0).then_inc(S["logged"], 1)
                if prev is not None:
                    w = prev["width"]
                    act.wait_ge(S["subbed"], prev["g"] + 1)
                    if prev2 is not None:
                        act.wait_ge(S["transposed"], s_before(prev))
                    act.activation(attn[prev["s"]][:, 0:w], work[prev["s"]][:, 0:w], ACT.Exp)\
                       .then_inc(S["attn_done"], 1)

            def s_before(step):
                g = step["g"]
                return max(g - 1, 0) if isinstance(g, int) else g - 1

            def tile_end(i):
                copy_heads(act, S, heads_out, o_bank, first_step[i + 1], i)

            act.preload_act_table_set("natural_log_exp_and_others")
            schedule(act, body, tile_end)

        @block.vector
        def _(dve):
            def sums(i):
                sum_squares(dve, S, sumsq, squares, dim, i)

            def body(cur, prev, prev2):
                if cur is not None and cur["s"] == 0 and cur["i"] >= 2 and prev["i"] != cur["i"]:
                    sums(cur["i"] - 2)
                if prev is not None:
                    w, t = prev["width"], work[prev["s"]]
                    back = t[:, 0:w][:, ::-1]
                    dve.wait_ge(S["plused"], prev["g"] + 1)
                    lower = prev["two"] and prev["s"] == 1
                    if lower:
                        dve.wait_ge(S["carried"], (prev["pair"] + 1) - first_step[CHUNK_TILES] // 2)
                    dve.tensor_tensor_scan(back, back, back, carry[:, 0:1] if lower else 0.0,
                                           ALU.add, ALU.bypass).then_inc(S["scanned"], 1)
                    if prev["two"] and prev["s"] == 0:
                        dve.wait_ge(S["scanned"], prev["g"] + 1)
                        dve.tensor_copy(carry[:, 0:1], t[:, 0:1]).then_inc(S["carried"], 1)
                if cur is not None:
                    w, t = cur["width"], work[cur["s"]]
                    dve.wait_ge(S["exped"], cur["g"] + 1)
                    dve.tensor_scalar(t[:, 0:w], t[:, 0:w], 2.0 ** 60, None, ALU.min).then_inc(S["clipped"], 1)
                if prev is not None:
                    w, t = prev["width"], work[prev["s"]]
                    dve.wait_ge(S["scanned"], prev["g"] + 1)
                    if prev["two"] and prev["s"] == 0:
                        dve.wait_ge(S["carried"], (prev["pair"] + 1) - first_step[CHUNK_TILES] // 2)
                    dve.tensor_tensor(t[:, 0:w], z[prev["s"]][:, 0:w], t[:, 0:w], ALU.subtract)\
                       .then_inc(S["subbed"], 1)
                if cur is not None:
                    w, t = cur["width"], work[cur["s"]]
                    dve.wait_ge(S["logged"], cur["g"] + 1)
                    dve.tensor_tensor(t[:, 0:w], z[cur["s"]][:, 0:w], t[:, 0:w], ALU.max).then_inc(S["plused"], 1)

            schedule(dve, body, lambda i: None)
            sums(TOK_TILES - 2)
            sums(TOK_TILES - 1)

        @block.gpsimd
        def _(pool):
            load_keys_values(pool, k_st, v_sb, qk_scratch, v_scratch, k_row, 1, kv_loaded, [1, 2])
            norm_tiles(pool, S, stored, heads_out, normed, squares, g_rep, sumsq, var, rstd, exponent,
                       dim, 1.0, mix_scratch, GROUP)


def phase_differential(nc, qk_scratch, v_scratch, lambdas_dram, g_rep_dram, ident, ident_bf, mask_bf, mix_scratch):
    q_row, k_row = 2 * GROUP, 3 * GROUP
    dim = 2 * HEAD_DIM
    ctx = ExitStack()
    with ctx:
        sb = lambda n, s, d=F32: ctx.enter_context(nc.sbuf_tensor(n, s, d))
        sem = lambda n: ctx.enter_context(nc.semaphore(n))
        k_st = sb("d_k", [P, HEADS, SEQ], F32R)
        v_sb = sb("d_v", [P, TOK_TILES, GROUP])
        q_st = [sb(f"d_q{s}", [P, 2, P], F32R) for s in range(2)]
        probs = [sb(f"d_probs{k}", [P, CHUNK]) for k in range(4)]
        attn = [sb(f"d_attn{u}", [P, CHUNK]) for u in range(2)]
        attn_t = [sb(f"d_attn_t{u}", [P, CHUNK]) for u in range(2)]
        row_max, neg_max, row_sum = sb("d_max", [P, 4]), sb("d_negmax", [P, 4]), sb("d_sum", [P, 4])
        neg_all, shift, weight = sb("d_negall", [P, 2]), sb("d_shift", [P, 4]), sb("d_weight", [P, 4])
        total, inverse, factor = sb("d_total", [P, 4]), sb("d_inverse", [P, 4]), sb("d_factor", [P, 4])
        sign = sb("d_sign", [P, 4])
        lambdas, lam_prod = sb("d_lambdas", [P, 4, HEAD_DIM]), sb("d_lamprod", [P, 2, HEAD_DIM])
        lam_dot, lam_exp = sb("d_lamdot", [P, 2]), sb("d_lamexp", [P, 2])
        heads_out, normed = sb("d_heads", [P, 2, GROUP]), sb("d_normed", [P, 2, GROUP])
        squares, g_rep = sb("d_squares", [P, GROUP]), sb("d_g", [P, GROUP])
        sumsq, var, rstd, exponent = (sb(f"d_{n}", [P, GROUP // dim]) for n in ("sumsq", "var", "rstd", "exponent"))
        z = [ctx.enter_context(nc.psum_tensor(f"d_z{s}", [P, CHUNK], F32)) for s in range(2)]
        t_bank = ctx.enter_context(nc.psum_tensor("d_t", [P, CHUNK], F32))
        o_bank = [ctx.enter_context(nc.psum_tensor(f"d_o{s}", [P, GROUP], F32)) for s in range(2)]
        kv_loaded = [sem(f"d_kv{p}") for p in range(3)]
        q_loaded = [sem(f"d_q_loaded{s}") for s in range(2)]
        names = ["scored", "reduced", "maxed", "exped", "shifted", "weighed", "stats_chain", "combined",
                 "transposed", "evacuated", "applied", "lambda_loaded", "lambda_ready", "lambda_chain"]
        S = {n: sem(f"d_{n}") for n in names + NORM_SEMS}
        stored = [sem(f"d_stored{s}") for s in range(2)]

        two = [len(chunks_of(i)) == 2 for i in range(TOK_TILES)]
        quads_of = [4 if two[i] else 2 for i in range(TOK_TILES)]
        first_quad = [sum(quads_of[:i]) for i in range(TOK_TILES + 1)]
        stat_steps = [8 if two[i] else 4 for i in range(TOK_TILES)]
        first_stat = [sum(stat_steps[j] * quads_of[j] for j in range(i)) for i in range(TOK_TILES)]

        def quad(i, q):
            return dict(i=i, q=q, n=q + first_quad[i])

        def step(Q, k):
            i = Q["i"]
            key_tile, tiles = chunks_of(i)[k % 2] if two[i] else chunks_of(i)[0]
            return dict(i=i, s=k % 2, g=Q["n"] * 4 + k, map=Q["q"] * 2 + k // 2 if two[i] else Q["q"] * 4 + k,
                        key_tile=key_tile, tiles=tiles, width=tiles * P, diagonal=key_tile + tiles == i + 1)

        def unit(Q, u):
            i = Q["i"]
            key_tile, tiles = chunks_of(i)[u] if two[i] else chunks_of(i)[0]
            return dict(i=i, u=u, a=Q["n"] * 2 + u, head=Q["q"] if two[i] else Q["q"] * 2 + u,
                        key_tile=key_tile, tiles=tiles, width=tiles * P,
                        maps=(u, 2 + u) if two[i] else (2 * u, 2 * u + 1),
                        opens=not two[i] or u == 0, closes=not two[i] or u == 1)

        def schedule(eng, body, tile_end):
            last = None
            for i in range(TOK_TILES):
                body(quad(i, 0), last)
                if i:
                    tile_end(i - 1)
                if i == 0:
                    for q in range(1, quads_of[i]):
                        body(quad(i, q), quad(i, q - 1))
                else:
                    with eng.Fori(1, quads_of[i]) as q:
                        body(quad(i, q), quad(i, q - 1))
                last = quad(i, quads_of[i] - 1)
            body(None, last)
            tile_end(TOK_TILES - 1)

        block = ctx.enter_context(nc.Block())

        @block.sync
        def _(sp):
            def body(cur, prev):
                if cur is None:
                    return
                for k in range(4):
                    t = step(cur, k)
                    if prev is not None or k >= 2:
                        sp.wait_ge(S["scored"], t["g"] - 1)
                    load_query(sp, q_st[t["s"]], qk_scratch, q_row, t["map"], t["i"], q_loaded[t["s"]])
                    if prev is None and k == 0:
                        load_keys_values(sp, k_st, v_sb, qk_scratch, v_scratch, k_row, 0, kv_loaded, [0])
                        sp.dma_start(lambdas[:], lambdas_dram).then_inc(S["lambda_loaded"], 16)
                        sp.dma_start(g_rep[:], g_rep_dram).then_inc(S["g_loaded"], 16)

            schedule(sp, body, lambda i: None)

        @block.tensor
        def _(pe):
            def scores(cur, k):
                t = step(cur, k)
                pe.wait_ge(q_loaded[t["s"]], cur["n"] * 64 + 32 * (k // 2 + 1))
                if not isinstance(t["g"], int) or t["g"] >= 2:
                    pe.wait_ge(S["exped"], t["g"] - 1)
                score_matmuls(pe, z[t["s"]], q_st[t["s"]], k_st, t["map"], t["key_tile"], t["tiles"],
                              t["diagonal"], ident_bf, mask_bf).then_inc(S["scored"], 1)

            def turn(prev, n):
                t = unit(prev, n)
                pe.wait_ge(S["combined"], t["a"] + 1)
                pe.wait_ge(S["evacuated"], t["a"])
                for j in range(t["tiles"]):
                    mm = pe.transpose(t_bank[:, j * P:(j + 1) * P], attn[n][:, j * P:(j + 1) * P], ident[:])
                mm.then_inc(S["transposed"], 1)

            def apply(prev, n):
                t = unit(prev, n)
                o = o_bank[t["i"] % 2]
                pe.wait_ge(S["evacuated"], t["a"] + 1)
                if t["i"] >= 2 and n == 0:
                    pe.wait_ge(S["o_copied"], t["i"] - 1)
                for j in range(t["tiles"]):
                    mm = pe.matmul(o[:, ds(t["head"] * dim, dim)], attn_t[n][:, j * P:(j + 1) * P],
                                   v_sb[:, t["key_tile"] + j, ds(t["head"] * dim, dim)],
                                   start=(t["opens"] and j == 0), stop=(t["closes"] and j == t["tiles"] - 1))
                mm.then_inc(S["applied"], 1)

            def body(cur, prev):
                if cur is not None:
                    piece = PIECE_OF_TILE[cur["i"]]
                    if prev is None or (prev["i"] != cur["i"] and piece != PIECE_OF_TILE[prev["i"]]):
                        pe.wait_ge(kv_loaded[piece], 48)
                for k in range(4):
                    if cur is not None:
                        scores(cur, k)
                    if prev is not None and k:
                        (turn, apply, apply)[k - 1](prev, (0, 0, 1)[k - 1])
                    if prev is not None and k == 2:
                        turn(prev, 1)

            schedule(pe, body, lambda i: None)

        @block.scalar
        def _(act):
            def exponentials(cur, k):
                t = step(cur, k)
                act.wait_ge(S["maxed"], t["g"] + 1)
                act.wait_ge(S["combined"], cur["n"] * 2)
                act.activation(probs[k][:, 0:t["width"]], z[t["s"]][:, 0:t["width"]], ACT.Exp,
                               bias=neg_max[:, k:k + 1], accum_out=row_sum[:, k:k + 1]).then_inc(S["exped"], 1)

            def evacuate(prev, n):
                t = unit(prev, n)
                act.wait_ge(S["transposed"], t["a"] + 1)
                if not isinstance(t["a"], int) or t["a"] >= 2:
                    act.wait_ge(S["applied"], t["a"] - 1)
                act.activation(attn_t[n][:, 0:t["width"]], t_bank[:, 0:t["width"]], ACT.Copy)\
                   .then_inc(S["evacuated"], 1)

            def body(cur, prev):
                if prev is not None and two[prev["i"]]:
                    number = prev["n"] + 1 - first_quad[CHUNK_TILES]
                    act.wait_ge(S["shifted"], number)
                    act.activation(weight[:], shift[:], ACT.Exp).then_inc(S["weighed"], 1)
                for k in range(4):
                    if cur is not None:
                        exponentials(cur, k)
                    if prev is not None and k < 2:
                        evacuate(prev, k)

            act.preload_act_table_set("natural_log_exp_and_others")
            act.wait_ge(S["lambda_ready"], 1)
            act.activation(lam_exp[:], lam_dot[:], ACT.Exp).then_inc(S["lambda_ready"], 1)
            schedule(act, body, lambda i: copy_heads(act, S, heads_out, o_bank, 2 * first_quad[i + 1], i))

        @block.vector
        def _(dve):
            def factors(prev):
                i = prev["i"]
                base = prev["q"] * stat_steps[i] + first_stat[i]
                dve.wait_ge(S["exped"], prev["n"] * 4 + 4)
                if not two[i]:
                    link(dve, S["stats_chain"], base + 1, dve.reciprocal(inverse[:], row_sum[:]))
                    link(dve, S["stats_chain"], base + 2,
                         dve.tensor_tensor(factor[:], inverse[:], sign[:], ALU.mult))
                    return base + 2
                by_map = lambda t: t[:].rearrange("p (m c) -> p m c", c=2)
                wide = lambda t: t[:, 0:2].unsqueeze(2).to_broadcast([P, 2, 2])
                number = prev["n"] + 1 - first_quad[CHUNK_TILES]
                link(dve, S["stats_chain"], base + 1,
                     dve.tensor_tensor(neg_all[:], neg_max[:, 0:4:2], neg_max[:, 1:4:2], ALU.min))
                dve.tensor_tensor(by_map(shift), wide(neg_all), by_map(neg_max), ALU.subtract)\
                   .then_inc(S["shifted"], 1)
                dve.wait_ge(S["weighed"], number)
                link(dve, S["stats_chain"], base + 2, dve.tensor_tensor(total[:], row_sum[:], weight[:], ALU.mult))
                link(dve, S["stats_chain"], base + 3,
                     dve.tensor_tensor(inverse[:, 0:2], total[:, 0:4:2], total[:, 1:4:2], ALU.add))
                link(dve, S["stats_chain"], base + 4, dve.reciprocal(inverse[:, 2:4], inverse[:, 0:2]))
                link(dve, S["stats_chain"], base + 5,
                     dve.tensor_tensor(inverse[:, 0:2], inverse[:, 2:4], sign[:, 0:2], ALU.mult))
                link(dve, S["stats_chain"], base + 6,
                     dve.tensor_tensor(by_map(factor), by_map(weight), wide(inverse), ALU.mult))
                return base + 6

            def body(cur, prev):
                if prev is not None:
                    count = factors(prev)
                    for n in range(2):
                        t = unit(prev, n)
                        w, (one, other) = t["width"], t["maps"]
                        link(dve, S["stats_chain"], count + 1 + n,
                             dve.tensor_scalar(probs[other][:, 0:w], probs[other][:, 0:w],
                                               factor[:, other:other + 1], None, ALU.mult))
                        if not isinstance(t["a"], int) or t["a"] >= 2:
                            dve.wait_ge(S["transposed"], t["a"] - 1)
                        dve.scalar_tensor_tensor(out=attn[n][:, 0:w], in0=probs[one][:, 0:w],
                                                 scalar=factor[:, one:one + 1], in1=probs[other][:, 0:w],
                                                 op0=ALU.mult, op1=ALU.add).then_inc(S["combined"], 1)
                if cur is not None:
                    for k in range(4):
                        t = step(cur, k)
                        dve.wait_ge(S["scored"], t["g"] + 1)
                        dve.tensor_reduce(row_max[:, k:k + 1], z[t["s"]][:, 0:t["width"]], AX.X, ALU.max)\
                           .then_inc(S["reduced"], 1)
                        dve.wait_ge(S["reduced"], t["g"] + 1)
                        dve.tensor_scalar(neg_max[:, k:k + 1], row_max[:, k:k + 1], -1.0, None, ALU.mult)\
                           .then_inc(S["maxed"], 1)
                    if prev is not None and prev["i"] != cur["i"] and cur["i"] >= 2:
                        sum_squares(dve, S, sumsq, squares, dim, cur["i"] - 2)

            dve.wait_ge(S["lambda_loaded"], 16)
            pairs = lambdas[:].rearrange("p (m s) d -> p m s d", s=2)
            n = S["lambda_chain"]
            link(dve, n, 1, dve.memset(sign[:], 1.0))
            link(dve, n, 2, dve.tensor_tensor(lam_prod[:], pairs[:, :, 0, :], pairs[:, :, 1, :], ALU.mult))
            dve.tensor_reduce(lam_dot[:], lam_prod[:], AX.X, ALU.add).then_inc(S["lambda_ready"], 1)
            dve.wait_ge(S["lambda_ready"], 2)
            link(dve, n, 3, dve.tensor_tensor(lam_dot[:, 0:1], lam_exp[:, 1:2], lam_exp[:, 0:1], ALU.subtract))
            for k in (1, 3):
                link(dve, n, 3 + (k + 1) // 2,
                     dve.tensor_scalar(sign[:, k:k + 1], lam_dot[:, 0:1], -LAMBDA_INIT, None, ALU.add))
            schedule(dve, body, lambda i: None)
            for i in (TOK_TILES - 2, TOK_TILES - 1):
                sum_squares(dve, S, sumsq, squares, dim, i)

        @block.gpsimd
        def _(pool):
            load_keys_values(pool, k_st, v_sb, qk_scratch, v_scratch, k_row, 0, kv_loaded, [1, 2])
            norm_tiles(pool, S, stored, heads_out, normed, squares, g_rep, sumsq, var, rstd, exponent,
                       dim, 1.0 - LAMBDA_INIT, mix_scratch, 0)


FT = D_FF // P
OUT_ITEMS = 2 * KC // 2
GATE_ITEM = OUT_ITEMS
DOWN_ITEM = OUT_ITEMS + 2 * FT
ITEMS = DOWN_ITEM + 2 * FT // 2
HALF = D_MODEL // 2


def phase_ffn(nc, x, mix_scratch, w_stream, g_ffn_dram, g_final_dram, ident, out):
    assert ITEMS % 2 == 0 and FT % 2 == 0
    ctx = ExitStack()
    with ctx:
        sb = lambda n, s, d=F32: ctx.enter_context(nc.sbuf_tensor(n, s, d))
        sem = lambda n: ctx.enter_context(nc.semaphore(n))
        w_raw = [sb(f"f_wraw{s}", [P, D_MODEL]) for s in range(2)]
        w_hi = [sb(f"f_whi{s}", [P, D_MODEL], F32R) for s in range(2)]
        w_lo = [sb(f"f_wlo{s}", [P, D_MODEL], F32R) for s in range(2)]
        natural = sb("f_natural", [P, TPB, D_MODEL])
        turned_hi, turned_lo = sb("f_thi", [P, KC, BLK], F32R), sb("f_tlo", [P, KC, BLK], F32R)
        x_in, x_sum = sb("f_xin", [P, TPB, D_MODEL]), sb("f_xsum", [P, TPB, D_MODEL])
        act_hi, act_lo = sb("f_ahi", [P, FT, BLK], F32R), sb("f_alo", [P, FT, BLK], F32R)
        gated = sb("f_gated", [P, 2, BLK])
        g_final, g_ffn = sb("f_gfinal", [P, D_MODEL]), sb("f_gffn", [P, KC])
        sumsq, var, rstd, exponent = (sb(f"f_{n}", [P, TPB]) for n in ("sumsq", "var", "rstd", "exponent"))
        bank = [ctx.enter_context(nc.psum_tensor(f"f_ps{i}", [P, BLK], F32)) for i in range(8)]
        w_loaded = [sem(f"f_w_loaded{s}") for s in range(2)]
        names = ["consts", "mix_loaded", "x_loaded", "mix_turned", "mix_hi", "mix_lo", "hi_split", "lo_split",
                 "multiplied", "x1_half", "squared", "var_ready", "powered", "scaled", "h2_turned", "h2_hi",
                 "h2_lo", "silued", "producted", "act_hi", "act_lo", "x2_half", "final", "stored", "pool_chain"]
        S = {n: sem(f"f_{n}") for n in names}
        x_blocks = x.rearrange("(b t p) n -> b p t n", t=TPB, p=P)
        mix_blocks = mix_scratch.rearrange("(b t p) n -> b p t n", t=TPB, p=P)
        out_blocks = out.rearrange("(b t p) n -> b p t n", t=TPB, p=P)
        one = lambda ap: ap.rearrange("o p t n -> (o p) t n")
        done = lambda b, j: b * ITEMS + (j + 2)
        block = ctx.enter_context(nc.Block())

        @block.sync
        def _(sp):
            for s in range(2):
                sp.dma_start(w_raw[s][:], w_stream[s]).then_inc(w_loaded[s], 16)
            sp.dma_start(g_final[:], g_final_dram).then_inc(S["consts"], 16)
            sp.dma_start(g_ffn[:], g_ffn_dram).then_inc(S["consts"], 16)
            with sp.Fori(0, BLOCKS) as b:
                sp.wait_ge(S["h2_turned"], b * KC)
                sp.dma_start(natural[:], one(mix_blocks[ds(b, 1)])).then_inc(S["mix_loaded"], 16)
                sp.wait_ge(S["x1_half"], b * (2 * TPB))
                sp.dma_start(x_in[:], one(x_blocks[ds(b, 1)])).then_inc(S["x_loaded"], 16)
                with sp.Fori(0, ITEMS // 2) as pair:
                    for s in range(2):
                        sp.wait_ge(S["lo_split"], b * ITEMS + pair * 2 + (s + 1))
                        sp.dma_start(w_raw[s][:], w_stream[ds(pair * 2 + (s + 2), 1)]
                                     .rearrange("o p n -> (o p) n")).then_inc(w_loaded[s], 16)
            for s in range(2):
                sp.wait_ge(w_loaded[s], 16 * (BLOCKS * ITEMS // 2 + 1))

        @block.gpsimd
        def _(pool):
            pool.memset(exponent[:], -0.5).then_inc(S["pool_chain"], 1)
            pool.wait_ge(S["pool_chain"], 1)
            with pool.Fori(0, BLOCKS) as b:
                for which in range(2):
                    pool.wait_ge(S["var_ready"], b * 2 + (which + 1))
                    pool.tensor_tensor(rstd[:], var[:], exponent[:], ALU.pow).then_inc(S["powered"], 1)
                for t in range(TPB):
                    pool.wait_ge(S["final"], b * TPB + (t + 1))
                    pool.dma_start(out_blocks[ds(b, 1), :, t, :].rearrange("o p n -> (o p) n"),
                                   x_sum[:, t, :]).then_inc(S["stored"], 16)
            pool.wait_ge(S["stored"], 16 * BLOCKS * TPB)

        @block.scalar
        def _(act):
            def split_hi(b, j):
                s = j % 2
                act.wait_ge(w_loaded[s], b * (ITEMS // 2 * 16) + (j // 2 + 1) * 16)
                act.wait_ge(S["multiplied"], b * ITEMS + j)
                act.activation(w_hi[s][:], w_raw[s][:], ACT.Copy).then_inc(S["hi_split"], 1)

            def squares(b, which, source):
                for t in range(TPB):
                    act.wait_ge(S[source], b * (2 * TPB) + (TPB + t + 1))
                    if which or t:
                        act.wait_ge(S["squared"], b * (2 * TPB) + (which * TPB + t))
                    act.activation(junk, x_sum[:, t, :], ACT.Square, accum_out=sumsq[:, t:t + 1])\
                       .then_inc(S["squared"], 1)

            junk = act_hi[:, 0:2, :].rearrange("p a n -> p (a n)")
            act.preload_act_table_set("silu_and_others")
            split_hi(0, 0)
            act.wait_ge(S["consts"], 32)
            with act.Fori(0, BLOCKS) as b:
                for k in range(KC):
                    act.wait_ge(S["mix_turned"], b * KC + (k + 1))
                    act.activation(turned_hi[:, k, :], bank[k][:], ACT.Copy).then_inc(S["mix_hi"], 1)
                for j in range(OUT_ITEMS):
                    split_hi(b, j + 1)
                squares(b, 0, "x1_half")
                for k in range(KC):
                    act.wait_ge(S["h2_turned"], b * KC + (k + 1))
                    act.activation(turned_hi[:, k, :], bank[k][:], ACT.Copy, scale=g_ffn[:, k:k + 1])\
                       .then_inc(S["h2_hi"], 1)
                with act.Fori(0, FT // 2) as pair:
                    for e in range(2):
                        item = b * ITEMS + pair * 4 + (GATE_ITEM + 2 * e)
                        f = b * FT + pair * 2 + e
                        for n in (1, 2):
                            s = n % 2
                            loads = b * (ITEMS // 2 * 16) + pair * 32 + ((GATE_ITEM + 2 * e + n) // 2 + 1) * 16
                            act.wait_ge(w_loaded[s], loads)
                            act.wait_ge(S["multiplied"], item + n)
                            act.activation(w_hi[s][:], w_raw[s][:], ACT.Copy).then_inc(S["hi_split"], 1)
                            if n == 1:
                                act.wait_ge(S["multiplied"], item + 2)
                                act.wait_ge(S["act_lo"], f)
                                act.activation(gated[:, e, :], bank[2 * e][:], ACT.Silu)\
                                   .then_inc(S["silued"], 1)
                        act.wait_ge(S["producted"], f + 2)
                        act.activation(act_hi[:, ds(pair * 2 + e, 1), :].rearrange("p o n -> p (o n)"),
                                       gated[:, e, :], ACT.Copy).then_inc(S["act_hi"], 1)
                for j in range(DOWN_ITEM, ITEMS):
                    split_hi(b, j + 1)
                squares(b, 1, "x2_half")

        @block.vector
        def _(dve):
            def split_lo(s, number):
                dve.wait_ge(S["hi_split"], number + 1)
                dve.tensor_tensor(w_lo[s][:], w_raw[s][:], w_hi[s][:].bitcast(F32), ALU.subtract)\
                   .then_inc(S["lo_split"], 1)

            def add_half(b, item, half, first_bank, inc, source):
                cols = slice(half * HALF, (half + 1) * HALF)
                dve.wait_ge(S["multiplied"], done(b, item))
                for t in range(TPB):
                    dve.tensor_tensor(x_sum[:, t, cols], bank[first_bank + t][:], source[:, t, cols], ALU.add)\
                       .then_inc(S[inc], 1)

            def variance(b, which):
                dve.wait_ge(S["squared"], b * (2 * TPB) + (which + 1) * TPB)
                dve.wait_ge(S["powered"], b * 2 + which)
                dve.tensor_scalar(var[:], sumsq[:], 1.0 / D_MODEL, EPS, ALU.mult, ALU.add).then_inc(S["var_ready"], 1)
                dve.wait_ge(S["powered"], b * 2 + (which + 1))

            split_lo(0, 0)
            dve.sem_inc(S["producted"], 1)
            with dve.Fori(0, BLOCKS) as b:
                for k in range(KC):
                    dve.wait_ge(S["mix_hi"], b * KC + (k + 1))
                    dve.tensor_tensor(turned_lo[:, k, :], bank[k][:], turned_hi[:, k, :].bitcast(F32),
                                      ALU.subtract).then_inc(S["mix_lo"], 1)
                for j in range(OUT_ITEMS):
                    split_lo((j + 1) % 2, b * ITEMS + (j + 1))
                    if j == OUT_ITEMS // 2 - 1:
                        dve.wait_ge(S["x_loaded"], b * 16 + 16)
                        dve.wait_ge(S["stored"], b * (16 * TPB))
                    if j == OUT_ITEMS // 2:
                        add_half(b, OUT_ITEMS // 2 - 1, 0, 0, "x1_half", x_in)
                add_half(b, OUT_ITEMS - 1, 1, 4, "x1_half", x_in)
                variance(b, 0)
                for t in range(TPB):
                    dve.tensor_scalar(natural[:, t, :], x_sum[:, t, :], rstd[:, t:t + 1], None, ALU.mult)\
                       .then_inc(S["scaled"], 1)
                for k in range(KC):
                    dve.wait_ge(S["h2_hi"], b * KC + (k + 1))
                    dve.scalar_tensor_tensor(out=turned_lo[:, k, :], in0=bank[k][:], scalar=g_ffn[:, k:k + 1],
                                             in1=turned_hi[:, k, :].bitcast(F32), op0=ALU.mult,
                                             op1=ALU.subtract).then_inc(S["h2_lo"], 1)
                with dve.Fori(0, FT // 2) as pair:
                    for e in range(2):
                        item = b * ITEMS + pair * 4 + (GATE_ITEM + 2 * e)
                        f = b * FT + pair * 2 + e
                        split_lo(1, item + 1)
                        split_lo(0, item + 2)
                        dve.wait_ge(S["multiplied"], item + 3)
                        dve.wait_ge(S["silued"], f + 1 + 1)
                        dve.tensor_tensor(gated[:, e, :], bank[2 * e + 1][:], gated[:, e, :], ALU.mult)\
                           .then_inc(S["producted"], 1)
                        dve.wait_ge(S["act_hi"], f + 1)
                        here = (slice(None), ds(pair * 2 + e, 1), slice(None))
                        flat = lambda t: t.rearrange("p o n -> p (o n)")
                        dve.tensor_tensor(flat(act_lo[here]), gated[:, e, :], flat(act_hi[here]).bitcast(F32),
                                          ALU.subtract).then_inc(S["act_lo"], 1)
                for j in range(DOWN_ITEM, ITEMS):
                    split_lo((j + 1) % 2, b * ITEMS + (j + 1))
                    if j == DOWN_ITEM + FT // 2:
                        add_half(b, DOWN_ITEM + FT // 2 - 1, 0, 4, "x2_half", x_sum)
                add_half(b, ITEMS - 1, 1, 0, "x2_half", x_sum)
                variance(b, 1)
                for t in range(TPB):
                    dve.scalar_tensor_tensor(out=x_sum[:, t, :], in0=x_sum[:, t, :], scalar=rstd[:, t:t + 1],
                                             in1=g_final[:], op0=ALU.mult, op1=ALU.mult).then_inc(S["final"], 1)

        @block.tensor
        def _(pe):
            def passes(s, chunk, left_hi, left_lo, outs, start, stop):
                cols = slice(chunk * HALF, (chunk + 1) * HALF)
                for t in range(TPB):
                    tok = slice(t * P, (t + 1) * P)
                    for n, (a, w) in enumerate(((left_hi, w_hi), (left_lo, w_hi), (left_hi, w_lo))):
                        mm = pe.matmul(bank[outs + t][:], a[:, tok], w[s][:, cols],
                                       start=(start and n == 0), stop=(stop and n == 2))
                return mm

            pe.sem_inc(S["multiplied"], 1)
            pe.sem_inc(S["silued"], 1)
            with pe.Fori(0, BLOCKS) as b:
                pe.wait_ge(S["mix_loaded"], b * 16 + 16)
                pe.wait_ge(S["x2_half"], b * (2 * TPB))
                for k in range(KC):
                    for t in range(TPB):
                        mm = pe.transpose(bank[k][:, t * P:(t + 1) * P], natural[:, t, k * P:(k + 1) * P], ident[:])
                    mm.then_inc(S["mix_turned"], 1)
                for j in range(OUT_ITEMS):
                    pe.wait_ge(S["lo_split"], b * ITEMS + (j + 1))
                    if j in (0, 2):
                        pe.wait_ge(S["mix_lo"], b * KC + 4 * (j // 2 + 1))
                    half, first = divmod(j, OUT_ITEMS // 2)
                    for n in range(2):
                        c = 2 * first + n
                        mm = passes(j % 2, n, turned_hi[:, c, :], turned_lo[:, c, :], 4 * half, c == 0, c == KC - 1)
                    mm.then_inc(S["multiplied"], 1)
                for t in range(TPB):
                    pe.wait_ge(S["scaled"], b * TPB + (t + 1))
                    for k in range(KC):
                        mm = pe.transpose(bank[k][:, t * P:(t + 1) * P], natural[:, t, k * P:(k + 1) * P], ident[:])
                        if t == TPB - 1:
                            mm.then_inc(S["h2_turned"], 1)
                with pe.Fori(0, FT // 2) as pair:
                    for e in range(2):
                        f = b * FT + pair * 2 + e
                        for n in range(2):
                            pe.wait_ge(S["lo_split"], b * ITEMS + pair * 4 + (GATE_ITEM + 2 * e + n + 1))
                            pe.wait_ge(S["producted" if n else "silued"], f)
                            for c in range(KC):
                                if e == 0 and n == 0:
                                    pe.wait_ge(S["h2_lo"], b * KC + (c + 1))
                                w = slice(c * P, (c + 1) * P)
                                for m, (a, h) in enumerate(((w_hi, turned_hi), (w_lo, turned_hi), (w_hi, turned_lo))):
                                    mm = pe.matmul(bank[2 * e + n][:], a[n][:, w], h[:, c, :],
                                                   start=(c == 0 and m == 0), stop=(c == KC - 1 and m == 2))
                            mm.then_inc(S["multiplied"], 1)
                for j in range(DOWN_ITEM, ITEMS):
                    pe.wait_ge(S["lo_split"], b * ITEMS + (j + 1))
                    half, first = divmod(j - DOWN_ITEM, FT // 2)
                    if half == 0:
                        pe.wait_ge(S["act_lo"], b * FT + (2 * first + 2))
                    for n in range(2):
                        f = 2 * first + n
                        mm = passes(j % 2, n, act_hi[:, f, :], act_lo[:, f, :], 4 * (1 - half), f == 0, f == FT - 1)
                    mm.then_inc(S["multiplied"], 1)



def build_program(nc, D, out):
    qk_scratch = nc.dram_tensor("qk_scratch", [2, len(QK_ORDER) * GROUP, SEQ], F32).ap()
    v_scratch = nc.dram_tensor("v_scratch", [2, SEQ, GROUP], F32).ap()
    mix_scratch = nc.dram_tensor("mix_scratch", [SEQ, D_MODEL], F32).ap()
    ctx = ExitStack()
    with ctx:
        sb = lambda n, s, d=F32: ctx.enter_context(nc.sbuf_tensor(n, s, d))
        ident = sb("ident_sb", [P, P])
        loaded, cast = ctx.enter_context(nc.semaphore("m_loaded")), ctx.enter_context(nc.semaphore("m_cast"))
        with nc.sbuf_tensor("hT_hi", [P, KC, SEQ], F32R) as hT_hi, nc.sbuf_tensor("hT_lo", [P, KC, SEQ], F32R) as hT_lo:
            with nc.Block() as block:
                @block.sync
                def _(sp):
                    sp.dma_start(ident[:], D["ident"]).then_inc(loaded, 16)
                    sp.wait_ge(loaded, 16)
            phase_norm(nc, D["x"], D["g_attn"][0].partition_broadcast(P), ident, hT_hi, hT_lo)
            phase_qk(nc, D["w_qk"], D["positions"], D["inv_freq"], D["rotary"], hT_hi, hT_lo, qk_scratch)
            phase_v(nc, D["w_v"], hT_hi, hT_lo, v_scratch)
        with ExitStack() as masks:
            small = lambda n, d: masks.enter_context(nc.sbuf_tensor(n, [P, P], d))
            ident_bf, raw = small("ident_bf", BF16), small("mask_raw", F32)
            raw_strict, causal, strict = small("mask_raw_strict", F32), small("causal", BF16), small("strict", BF16)
            with nc.Block() as block:
                @block.sync
                def _(sp):
                    sp.dma_start(raw[:], D["causal_mask"]).then_inc(loaded, 16)
                    sp.dma_start(raw_strict[:], D["strict_mask"]).then_inc(loaded, 16)

                @block.vector
                def _(dve):
                    dve.wait_ge(loaded, 48)
                    dve.tensor_copy(ident_bf[:], ident[:]).then_inc(cast, 1)
                    dve.tensor_copy(causal[:], raw[:]).then_inc(cast, 1)
                    dve.tensor_copy(strict[:], raw_strict[:]).then_inc(cast, 1)
                    dve.wait_ge(cast, 3)
            phase_differential(nc, qk_scratch, v_scratch, D["lambdas"].partition_broadcast(P),
                               D["g_diff"][0].partition_broadcast(P), ident, ident_bf, causal, mix_scratch)
            phase_stick_breaking(nc, qk_scratch, v_scratch, D["g_stick"][0].partition_broadcast(P), ident,
                                 ident_bf, strict, mix_scratch)
        phase_ffn(nc, D["x"], mix_scratch, D["w_stream"], D["g_ffn"], D["g_final"][0].partition_broadcast(P),
                  ident, out)


def host_arrays(x, positions, norm_attn_g, w_in, lambda_q1, lambda_k1, lambda_q2, lambda_k2, diff_subln_g,
                sb_norm_g, w_out, norm_ffn_g, w_gate, w_up, w_down, final_norm_g):
    chunked = w_in[0].reshape(KC, P, -1)
    w_qk = np.stack([chunked[:, :, COL[kind] + f * P:COL[kind] + (f + 1) * P].transpose(1, 0, 2)
                     for kind in QK_ORDER for f in range(QK_TILES)])
    w_v = np.stack([chunked[:, :, COL[kind]:COL[kind] + GROUP] for kind in ("dv", "sv")])

    def natural(w):
        return w.reshape(-1, 2, P, 2, HALF).transpose(3, 0, 2, 1, 4).reshape(-1, P, D_MODEL)

    def by_tile(w):
        return w.reshape(KC, P, FT, P).transpose(2, 1, 0, 3).reshape(FT, P, D_MODEL)

    gate_up = np.stack([by_tile(w_gate[0]), by_tile(w_up[0])], 1).reshape(2 * FT, P, D_MODEL)
    items = [natural(w_out[0]), gate_up, natural(w_down[0])]
    w_stream = np.concatenate(items + [items[0][:2]])

    half = HEAD_DIM // 8
    inv_freq = np.zeros((P, 1), np.float32)
    rotary = np.zeros((P, P), np.float32)
    for first in range(0, P, HEAD_DIM):
        for i in range(half):
            inv_freq[first + i] = inv_freq[first + half + i] = np.float32(500000.0) ** np.float32(-i / half)
            rotary[first + half + i, first + i] = -1.0
            rotary[first + i, first + half + i] = 1.0
    row, col = np.arange(P)[:, None], np.arange(P)[None, :]
    return dict(
        x=x[0], positions=positions, g_attn=norm_attn_g, w_qk=w_qk, w_v=w_v, w_stream=w_stream,
        lambdas=np.concatenate([lambda_q1, lambda_k1, lambda_q2, lambda_k2]),
        g_diff=np.tile(diff_subln_g, (1, GROUP // (2 * HEAD_DIM))), g_stick=np.tile(sb_norm_g, (1, HEADS)),
        g_ffn=norm_ffn_g.reshape(KC, P).transpose(1, 0), g_final=final_norm_g.reshape(1, D_MODEL),
        inv_freq=inv_freq, rotary=rotary, ident=np.eye(P, dtype=np.float32),
        causal_mask=np.where(col > row, -1e30, 0.0).astype(np.float32),
        strict_mask=np.where(col >= row, -1e30, 0.0).astype(np.float32))


def kernel(**inputs):
    from concourse import bacc
    from concourse.bass_utils import run_bass_kernel_spmd

    arrays = {n: np.ascontiguousarray(a) for n, a in host_arrays(**{k: np.asarray(v) for k, v in inputs.items()}).items()}
    nc = bacc.Bacc("TRN2", target_bir_lowering=False, num_devices=1)
    dram = {n: nc.dram_tensor("in_" + n, a.shape, mybir.dt.from_np(a.dtype), kind="ExternalInput").ap() for n, a in arrays.items()}
    out = nc.dram_tensor("out", [SEQ, D_MODEL], F32, kind="ExternalOutput").ap()
    build_program(nc, dram, out)
    result = run_bass_kernel_spmd(nc, [{"in_" + n: a for n, a in arrays.items()}], core_ids=[0])
    return result.results[0]["out"].reshape(1, SEQ, D_MODEL)
```

```python
import math
from contextlib import ExitStack

import numpy as np
import concourse.bass as bass
from concourse import mybir

F32 = mybir.dt.float32
F32R = mybir.dt.float32r
BF16 = mybir.dt.bfloat16
I32 = mybir.dt.int32
ALU = mybir.AluOpType
ACT = mybir.ActivationFunctionType
AX = mybir.AxisListType
ds = bass.ds

P = 128
SEQ = 2048
D_MODEL = 1024
HEAD_DIM = 64
D_FF = 2816
EPS = 1e-5
KC = D_MODEL // P
TOK_TILES = SEQ // P
BLK = 512
BLOCKS = SEQ // BLK
TPB = BLK // P
GROUP = 512
HEADS = GROUP // HEAD_DIM
QK_TILES = GROUP // P
COL = {"dq": 0, "dk": 512, "dv": 1024, "sq": 1536, "sk": 2048, "sv": 2560}
SCALE = HEAD_DIM ** -0.5
LAMBDA_INIT = 0.8 - 0.6 * math.exp(-0.3 * 0)


MAGIC = 1.5 * 2 ** 23


def two_pi_parts():
    first = 6.28125
    second = math.floor((2 * math.pi - first) * 2 ** 19) / 2 ** 19
    return first, second, 2 * math.pi - first - second


TWO_PI = two_pi_parts()


def link(eng, sem, value, instruction):
    instruction.then_inc(sem, 1)
    eng.wait_ge(sem, value)


def phase_norm(nc, x, g_row_dram, ident, hT_hi, hT_lo):
    ctx = ExitStack()
    with ctx:
        sb = lambda n, s, d=F32: ctx.enter_context(nc.sbuf_tensor(n, s, d))
        sem = lambda n: ctx.enter_context(nc.semaphore(n))
        xt = sb("a_x", [P, TOK_TILES, D_MODEL])
        g_row = sb("a_g", [P, D_MODEL])
        junk = sb("a_junk", [P, D_MODEL])
        sumsq = sb("a_sumsq", [P, TOK_TILES])
        var = sb("a_var", [P, TOK_TILES])
        lnv = sb("a_lnv", [P, TOK_TILES])
        y0 = sb("a_y0", [P, TOK_TILES])
        nt = sb("a_newton", [P, TOK_TILES])
        rstd = sb("a_rstd", [P, TOK_TILES])
        bank = [ctx.enter_context(nc.psum_tensor(f"a_ps{i}", [P, 512], F32)) for i in range(8)]
        x_loaded = [sem(f"a_x_loaded{g}") for g in range(BLOCKS)]
        g_loaded = sem("a_g_loaded")
        squared, var_ready, ln_ready, y0_ready = sem("a_squared"), sem("a_var"), sem("a_ln"), sem("a_y0")
        dve_chain, scaled, turned = sem("a_dve"), sem("a_scaled"), sem("a_turned")
        hi_ready, lo_ready, act_chain = sem("a_hi"), sem("a_lo"), sem("a_act")
        xs = x.rearrange("(g t p) n -> g p t n", t=TPB, p=P)
        block = ctx.enter_context(nc.Block())

        @block.sync
        def _(sp):
            for g in range(BLOCKS):
                sp.dma_start(xt[:, g * TPB:(g + 1) * TPB, :], xs[g]).then_inc(x_loaded[g], 16)
                if g == 0:
                    sp.dma_start(g_row[:], g_row_dram).then_inc(g_loaded, 16)

        @block.scalar
        def _(act):
            def stats(g):
                act.wait_ge(x_loaded[g], 16)
                for t in range(g * TPB, (g + 1) * TPB):
                    if t:
                        act.wait_ge(squared, t)
                    act.activation(junk[:], xt[:, t, :], ACT.Square,
                                   accum_out=sumsq[:, t:t + 1]).then_inc(squared, 1)
                own = slice(g * TPB, (g + 1) * TPB)
                act.wait_ge(var_ready, g + 1)
                act.activation(lnv[:, own], var[:, own], ACT.Ln).then_inc(ln_ready, 1)
                act.wait_ge(ln_ready, g + 1)
                act.activation(y0[:, own], lnv[:, own], ACT.Exp, scale=-0.5).then_inc(y0_ready, 1)

            stats(0)
            for g in range(BLOCKS):
                if g + 1 < BLOCKS:
                    stats(g + 1)
                for u in range(2 * TPB):
                    t, half = g * TPB + u // 2, u % 2
                    act.wait_ge(turned, 2 * t + half + 1)
                    act.activation(hT_hi[:, 4 * half:4 * half + 4, t * P:(t + 1) * P],
                                   bank[u][:].rearrange("p (k t) -> p k t", k=4), ACT.Copy)\
                       .then_inc(hi_ready, 1)

        @block.vector
        def _(dve):
            n = [0]

            def chain(instruction):
                n[0] += 1
                link(dve, dve_chain, n[0], instruction)

            def scale_rows(g):
                own = slice(g * TPB, (g + 1) * TPB)
                dve.wait_ge(squared, (g + 1) * TPB)
                dve.tensor_scalar(var[:, own], sumsq[:, own], 1.0 / D_MODEL, EPS, ALU.mult, ALU.add)\
                   .then_inc(var_ready, 1)
                dve.wait_ge(y0_ready, g + 1)
                chain(dve.tensor_tensor(nt[:, own], y0[:, own], y0[:, own], ALU.mult))
                chain(dve.tensor_tensor(nt[:, own], nt[:, own], var[:, own], ALU.mult))
                chain(dve.tensor_scalar(nt[:, own], nt[:, own], -0.5, 1.5, ALU.mult, ALU.add))
                chain(dve.tensor_tensor(rstd[:, own], nt[:, own], y0[:, own], ALU.mult))
                if g == 0:
                    dve.wait_ge(g_loaded, 16)
                for t in range(g * TPB, (g + 1) * TPB):
                    dve.scalar_tensor_tensor(out=xt[:, t, :], in0=xt[:, t, :], scalar=rstd[:, t:t + 1],
                                             in1=g_row[:], op0=ALU.mult, op1=ALU.mult).then_inc(scaled, 1)

            scale_rows(0)
            for g in range(BLOCKS):
                if g + 1 < BLOCKS:
                    scale_rows(g + 1)
                for u in range(2 * TPB):
                    t, half = g * TPB + u // 2, u % 2
                    dst = (slice(None), slice(4 * half, 4 * half + 4), slice(t * P, (t + 1) * P))
                    dve.wait_ge(hi_ready, 2 * t + half + 1)
                    dve.tensor_tensor(hT_lo[dst], bank[u][:].rearrange("p (k t) -> p k t", k=4),
                                      hT_hi[dst].bitcast(F32), ALU.subtract).then_inc(lo_ready, 1)

        @block.tensor
        def _(pe):
            for t in range(TOK_TILES):
                pe.wait_ge(scaled, t + 1)
                for half in range(2):
                    u = (2 * t + half) % 8
                    if 2 * t + half >= 8:
                        pe.wait_ge(lo_ready, 2 * t + half - 7)
                    for k in range(4):
                        c = 4 * half + k
                        mm = pe.transpose(bank[u][:, k * P:(k + 1) * P], xt[:, t, c * P:(c + 1) * P], ident[:])
                    mm.then_inc(turned, 1)


QK_ORDER = ["sq", "sk", "dq", "dk"]
PAIRS = QK_TILES // 2
ALL_PAIRS = len(QK_ORDER) * PAIRS


def phase_qk(nc, w_qk, positions, invf_dram, perm_dram, hT_hi, hT_lo, qk_scratch):
    ctx = ExitStack()
    with ctx:
        sb = lambda n, s, d=F32: ctx.enter_context(nc.sbuf_tensor(n, s, d))
        sem = lambda n: ctx.enter_context(nc.semaphore(n))
        w_raw = [sb(f"b_wraw{s}", [P, KC, P]) for s in range(2)]
        w_hi = [sb(f"b_whi{s}", [P, KC, P], F32R) for s in range(2)]
        w_lo = [sb(f"b_wlo{s}", [P, KC, P], F32R) for s in range(2)]
        out_hi = sb("b_ohi", [P, BLOCKS, BLK], F32R)
        out_lo = sb("b_olo", [P, BLOCKS, BLK], F32R)
        cosT, sinT = sb("b_cos", [P, SEQ]), sb("b_sin", [P, SEQ])
        raw_qk, turned = sb("b_rawqk", [P, 2, BLK]), sb("b_turned", [P, 2, BLK])
        turns, part = sb("b_turns", [P, SEQ // 2]), sb("b_part", [P, SEQ // 2])
        invf, perm = sb("b_invf", [P, 1]), sb("b_perm", [P, P])
        bank = [ctx.enter_context(nc.psum_tensor(f"b_ps{i}", [P, BLK], F32)) for i in range(BLOCKS)]
        rot_bank = [ctx.enter_context(nc.psum_tensor(f"b_rot{i}", [P, BLK], F32)) for i in range(2)]
        w_loaded = [sem(f"b_w_loaded{s}") for s in range(2)]
        hi_split, lo_split = sem("b_hi_split"), sem("b_lo_split")
        projected = sem("b_projected")
        hi_out = sem("b_hi_out")
        unit_done = sem("b_unit_done")
        raw_copied, rotated, summed = sem("b_raw"), sem("b_rotated"), sem("b_summed")
        dve_chain, pool_chain = sem("b_dve"), sem("b_pool")
        stored = [sem(f"b_stored{b}") for b in range(BLOCKS)]
        consts, table_ready = sem("b_const"), sem("b_table")
        first_rot = 2 * QK_TILES * BLOCKS

        def kinds(eng, n, kind, body):
            if kind != QK_ORDER[-1]:
                with eng.Fori(0, PAIRS) as i:
                    for s in range(2):
                        pair = i + n * PAIRS
                        body(pair * 2 + s, pair, s, kind, False)
            else:
                for i in range(PAIRS):
                    for s in range(2):
                        pair = n * PAIRS + i
                        body(2 * pair + s, pair, s, kind, 2 * i + s == QK_TILES - 1)

        block = ctx.enter_context(nc.Block())

        @block.sync
        def _(sp):
            def store(n, b):
                sp.wait_ge(unit_done, n * BLOCKS + (b + 5))
                for part_no, src in ((0, out_hi), (1, out_lo)):
                    sp.dma_start(qk_scratch[part_no, ds(n * P, P), b * BLK:(b + 1) * BLK],
                                 src[:, b, :].bitcast(F32)).then_inc(stored[b], 16)

            for s in range(2):
                sp.dma_start(w_raw[s][:], w_qk[s]).then_inc(w_loaded[s], 16)
            sp.dma_start(cosT[:].bitcast(I32), positions[0, :].partition_broadcast(P)).then_inc(consts, 16)
            sp.dma_start(invf[:], invf_dram).then_inc(consts, 16)
            sp.dma_start(perm[:], perm_dram).then_inc(consts, 16)
            with sp.Fori(0, ALL_PAIRS - 1) as pair:
                for s in range(2):
                    n = pair * 2 + s
                    sp.wait_ge(lo_split, n + 1)
                    sp.dma_start(w_raw[s][:], w_qk[ds(n + 2, 1)].rearrange("o p c n -> (o p) c n"))\
                      .then_inc(w_loaded[s], 16)
                    for b in range(BLOCKS):
                        store(n, b)
            for n in (2 * ALL_PAIRS - 2, 2 * ALL_PAIRS - 1):
                for b in range(BLOCKS):
                    store(n, b)
            for b in range(BLOCKS):
                sp.wait_ge(stored[b], 2 * ALL_PAIRS * 32)

        @block.gpsimd
        def _(pool):
            pool.wait_ge(consts, 48)
            step = [0]

            def chain(instruction):
                step[0] += 1
                link(pool, pool_chain, step[0], instruction)

            for cols in (slice(0, SEQ // 2), slice(SEQ // 2, SEQ)):
                cos, sin = cosT[:, cols], sinT[:, cols]
                chain(pool.tensor_copy(cos, cos.bitcast(I32)))
                chain(pool.tensor_scalar(cos, cos, invf[:, 0:1], 1.0, ALU.mult, ALU.mult))
                for table, quarter in ((sin, 0.0), (cos, 0.25)):
                    chain(pool.tensor_scalar(turns[:], cos, 1.0 / (2 * math.pi), quarter, ALU.mult, ALU.add))
                    chain(pool.tensor_scalar(turns[:], turns[:], MAGIC, -MAGIC, ALU.add, ALU.add))
                    chain(pool.tensor_scalar(part[:], turns[:], -TWO_PI[0], 1.0, ALU.mult, ALU.mult))
                    chain(pool.tensor_tensor(table, cos, part[:], ALU.add))
                    chain(pool.tensor_scalar(part[:], turns[:], -TWO_PI[1], 1.0, ALU.mult, ALU.mult))
                    chain(pool.tensor_tensor(table, table, part[:], ALU.add))
                    chain(pool.tensor_scalar(part[:], turns[:], -TWO_PI[2], quarter * 2 * math.pi,
                                             ALU.mult, ALU.add))
                    chain(pool.tensor_tensor(table, table, part[:], ALU.add))
                    chain(pool.tensor_scalar(table, table, 3.1415925, -3.1415925, ALU.min, ALU.max))

        @block.scalar
        def _(act):
            def split_hi(pair, s, tiles_done):
                act.wait_ge(w_loaded[s], pair * 16 + 16)
                act.wait_ge(projected, tiles_done * BLOCKS)
                act.activation(w_hi[s][:], w_raw[s][:], ACT.Copy).then_inc(hi_split, 1)

            def evac(n, pair, s, kind, last):
                scale = SCALE if kind[1] == "q" else 1.0
                for b in range(BLOCKS):
                    if b == 1 and not last:
                        split_hi(pair + s, 1 - s, n)
                    act.wait_ge(projected, n * BLOCKS + (b + 1))
                    if kind[0] == "s":
                        act.wait_ge(stored[b], n * 32)
                        act.activation(out_hi[:, b, :], bank[b][:], ACT.Copy, scale=scale).then_inc(hi_out, 1)
                    else:
                        act.activation(raw_qk[:, b % 2, :], bank[b][:], ACT.Copy, scale=scale)\
                           .then_inc(raw_copied, 1)
                        act.wait_ge(summed, n * BLOCKS + (b + 1 - first_rot))
                        act.wait_ge(stored[b], n * 32)
                        act.activation(out_hi[:, b, :], turned[:, b % 2, :], ACT.Copy).then_inc(hi_out, 1)

            for n, kind in enumerate(QK_ORDER):
                if n == 0:
                    split_hi(0, 0, 0)
                if kind == "dq":
                    act.wait_ge(pool_chain, 20 * 2)
                    act.activation(sinT[:], sinT[:], ACT.Sin).then_inc(table_ready, 1)
                    act.activation(cosT[:], cosT[:], ACT.Sin).then_inc(table_ready, 1)
                kinds(act, n, kind, evac)

        @block.vector
        def _(dve):
            def split_lo(n, s):
                dve.wait_ge(hi_split, n + 1)
                dve.tensor_tensor(w_lo[s][:], w_raw[s][:], w_hi[s][:].bitcast(F32), ALU.subtract)\
                   .then_inc(lo_split, 1)

            def evac(n, pair, s, kind, last):
                scale = SCALE if kind[1] == "q" else 1.0
                for b in range(BLOCKS):
                    if b == 1 and not last:
                        split_lo(n + 1, 1 - s)
                    hi = out_hi[:, b, :].bitcast(F32)
                    if kind[0] == "s":
                        dve.wait_ge(stored[b], n * 32)
                        dve.wait_ge(hi_out, n * BLOCKS + (b + 1))
                        dve.scalar_tensor_tensor(out=out_lo[:, b, :], in0=bank[b][:], scalar=scale, in1=hi,
                                                 op0=ALU.mult, op1=ALU.subtract).then_inc(unit_done, 1)
                    else:
                        rot = n * BLOCKS + (b - first_rot)
                        sin, cos = sinT[:, b * BLK:(b + 1) * BLK], cosT[:, b * BLK:(b + 1) * BLK]
                        slot = (slice(None), b % 2, slice(None))
                        dve.wait_ge(rotated, rot + 1)
                        link(dve, dve_chain, rot * 2 + 1,
                             dve.tensor_tensor(turned[slot], rot_bank[b % 2][:], sin, ALU.mult))
                        link(dve, dve_chain, rot * 2 + 2,
                             dve.tensor_tensor(raw_qk[slot], raw_qk[slot], cos, ALU.mult))
                        dve.tensor_tensor(turned[slot], turned[slot], raw_qk[slot], ALU.add).then_inc(summed, 1)
                        dve.wait_ge(summed, rot + 1)
                        dve.wait_ge(stored[b], n * 32)
                        dve.wait_ge(hi_out, n * BLOCKS + (b + 1))
                        dve.tensor_tensor(out_lo[:, b, :], turned[slot], hi, ALU.subtract).then_inc(unit_done, 1)

            dve.sem_inc(unit_done, BLOCKS)
            for n, kind in enumerate(QK_ORDER):
                if n == 0:
                    split_lo(0, 0)
                if kind == "dq":
                    dve.wait_ge(table_ready, 2)
                kinds(dve, n, kind, evac)

        @block.tensor
        def _(pe):
            def rotate(n, b):
                rot = n * BLOCKS + (b - first_rot)
                pe.wait_ge(raw_copied, rot + 1)
                pe.matmul(rot_bank[b % 2][:], perm[:], raw_qk[:, b % 2, :], start=True, stop=True)\
                  .then_inc(rotated, 1)

            def project(n, pair, s, kind, last):
                pe.wait_ge(lo_split, n + 1)
                for b in range(BLOCKS):
                    pe.wait_ge(unit_done, n * BLOCKS + (b + 1))
                    cols = slice(b * BLK, (b + 1) * BLK)
                    for c in range(KC):
                        for w, h in ((w_hi, hT_hi), (w_lo, hT_hi), (w_hi, hT_lo)):
                            mm = pe.matmul(bank[b][:], w[s][:, c, :], h[:, c, cols],
                                           start=(c == 0 and w is w_hi and h is hT_hi),
                                           stop=(c == KC - 1 and h is hT_lo))
                        if c == 2 and b and kind[0] == "d":
                            rotate(n, b - 1)
                    mm.then_inc(projected, 1)
                if kind[0] == "d":
                    rotate(n, BLOCKS - 1)

            for n, kind in enumerate(QK_ORDER):
                kinds(pe, n, kind, project)


def phase_v(nc, w_v, hT_hi, hT_lo, v_scratch):
    ctx = ExitStack()
    with ctx:
        sb = lambda n, s, d=F32: ctx.enter_context(nc.sbuf_tensor(n, s, d))
        sem = lambda n: ctx.enter_context(nc.semaphore(n))
        w_raw = [sb(f"c_wraw{s}", [P, GROUP]) for s in range(2)]
        w_hi, w_lo = sb("c_whi", [P, 2, KC, GROUP], F32R), sb("c_wlo", [P, 2, KC, GROUP], F32R)
        v_out = sb("c_out", [P, 4, GROUP])
        bank = [ctx.enter_context(nc.psum_tensor(f"c_ps{i}", [P, GROUP], F32)) for i in range(4)]
        w_loaded = [sem(f"c_w_loaded{s}") for s in range(2)]
        hi_split, lo_split = sem("c_hi_split"), sem("c_lo_split")
        projected, copied = sem("c_projected"), sem("c_copied")
        stored = [sem(f"c_stored{i}") for i in range(4)]
        block = ctx.enter_context(nc.Block())

        @block.sync
        def _(sp):
            for n in range(2 * KC):
                if n >= 2:
                    sp.wait_ge(lo_split, n - 1)
                sp.dma_start(w_raw[n % 2][:], w_v[n // KC, n % KC]).then_inc(w_loaded[n % 2], 16)
            with sp.Fori(0, 2) as group:
                for t in range(TOK_TILES):
                    sp.wait_ge(copied, group * TOK_TILES + (t + 5))
                    sp.dma_start(v_scratch[ds(group, 1), t * P:(t + 1) * P, :].rearrange("o p n -> (o p) n"),
                                 v_out[:, t % 4, :]).then_inc(stored[t % 4], 16)
            for i in range(4):
                sp.wait_ge(stored[i], 16 * 2 * TOK_TILES // 4)

        @block.vector
        def _(dve):
            for n in range(2 * KC):
                dve.wait_ge(hi_split, n + 1)
                dve.tensor_tensor(w_lo[:, n // KC, n % KC, :], w_raw[n % 2][:],
                                  w_hi[:, n // KC, n % KC, :].bitcast(F32), ALU.subtract).then_inc(lo_split, 1)

        @block.scalar
        def _(act):
            for n in range(2 * KC):
                act.wait_ge(w_loaded[n % 2], 16 * (n // 2 + 1))
                act.activation(w_hi[:, n // KC, n % KC, :], w_raw[n % 2][:], ACT.Copy).then_inc(hi_split, 1)
            act.sem_inc(copied, 4)
            with act.Fori(0, 2) as group:
                for t in range(TOK_TILES):
                    act.wait_ge(projected, group * TOK_TILES + (t + 1))
                    act.wait_ge(stored[t % 4], group * (16 * TOK_TILES // 4) + 16 * (t // 4))
                    act.activation(v_out[:, t % 4, :], bank[t % 4][:], ACT.Copy).then_inc(copied, 1)

        @block.tensor
        def _(pe):
            with pe.Fori(0, 2) as group:
                for t in range(TOK_TILES):
                    pe.wait_ge(copied, group * TOK_TILES + (t + 1))
                    for c in range(KC):
                        if t == 0:
                            pe.wait_ge(lo_split, group * KC + (c + 1))
                        for h, w in ((hT_hi, w_hi), (hT_lo, w_hi), (hT_hi, w_lo)):
                            mm = pe.matmul(bank[t % 4][:], h[:, c, t * P:(t + 1) * P],
                                           w[:, ds(group, 1), c, :].rearrange("p o n -> p (o n)"),
                                           start=(c == 0 and h is hT_hi and w is w_hi),
                                           stop=(c == KC - 1 and w is w_lo))
                    mm.then_inc(projected, 1)


CHUNK = 1024
CHUNK_TILES = CHUNK // P
KEY_PIECES = [0, 256, 768, 2048]
PIECE_OF_TILE = [next(p for p in range(3) if (i + 1) * P <= KEY_PIECES[p + 1]) for i in range(TOK_TILES)]


def chunks_of(i):
    return [(k, min(CHUNK_TILES, i + 1 - k)) for k in range(0, i + 1, CHUNK_TILES)]


def load_keys_values(sp, k_st, v_sb, qk_scratch, v_scratch, k_row, group, kv_loaded, pieces):
    for piece in pieces:
        if piece:
            sp.wait_ge(kv_loaded[piece - 1], 48)
        a, b = KEY_PIECES[piece], KEY_PIECES[piece + 1]
        for part in range(2):
            sp.dma_start(k_st[part * HEAD_DIM:(part + 1) * HEAD_DIM, :, a:b].bitcast(F32),
                         qk_scratch[part, k_row:k_row + GROUP, a:b].rearrange("(h r) t -> r h t", r=HEAD_DIM))\
              .then_inc(kv_loaded[piece], 16)
        sp.dma_start(v_sb[:, a // P:b // P, :], v_scratch[group, a:b, :].rearrange("(k p) n -> p k n", p=P))\
          .then_inc(kv_loaded[piece], 16)


def load_query(sp, q_slot, qk_scratch, q_row, head, i, q_loaded):
    for half in range(2):
        sp.dma_start(q_slot[half * HEAD_DIM:(half + 1) * HEAD_DIM, :, :].bitcast(F32),
                     qk_scratch[:, ds(head * HEAD_DIM + q_row, HEAD_DIM), i * P:(i + 1) * P]
                     .rearrange("l r t -> r l t")).then_inc(q_loaded, 16)


def score_matmuls(pe, z, q_slot, k_st, head, key_tile, tiles, diagonal, ident_bf, mask_bf):
    for first in range(0, tiles, 4):
        n = min(4, tiles - first)
        cols = ds(head * SEQ + (key_tile + first) * P, n * P)
        keys = k_st[:].rearrange("p h t -> p (h t)")[:, cols]
        out = z[:, first * P:(first + n) * P]
        pe.matmul(out, q_slot[:, 0, :], keys, start=True, stop=False)
        if diagonal and first + n == tiles:
            pe.matmul(out[:, (n - 1) * P:n * P], ident_bf[:], mask_bf[:], start=False, stop=False)
        mm = pe.matmul(out, q_slot[:, 1, :], keys, start=False, stop=True)
    return mm


NORM_SEMS = ["o_copied", "squared", "summed", "pool_chain", "normed_ready", "g_loaded"]


def norm_tiles(pool, S, stored, heads_out, normed, squares, g_rep, sumsq, var, rstd, exponent, dim, factor,
               mix_scratch, mix_col):
    by_head = lambda t: t.rearrange("p (h d) -> p h d", d=dim)
    link(pool, S["pool_chain"], 1, pool.memset(exponent[:], -0.5))
    pool.wait_ge(S["g_loaded"], 16)
    link(pool, S["pool_chain"], 2, pool.tensor_scalar(g_rep[:], g_rep[:], factor, 1.0, ALU.mult, ALU.mult))
    n = 2
    for i in range(TOK_TILES):
        src, dst = heads_out[:, i % 2, :], normed[:, i % 2, :]
        pool.wait_ge(S["o_copied"], i + 1)
        if i >= 1:
            pool.wait_ge(S["summed"], i)
        pool.tensor_tensor(squares[:], src, src, ALU.mult).then_inc(S["squared"], 1)
        if i >= 2:
            pool.wait_ge(stored[i % 2], 16 * (i // 2))
        link(pool, S["pool_chain"], n + 1, pool.tensor_tensor(dst, src, g_rep[:], ALU.mult))
        pool.wait_ge(S["summed"], i + 1)
        link(pool, S["pool_chain"], n + 2,
             pool.tensor_scalar(var[:], sumsq[:], 1.0 / dim, EPS, ALU.mult, ALU.add))
        link(pool, S["pool_chain"], n + 3, pool.tensor_tensor(rstd[:], var[:], exponent[:], ALU.pow))
        n += 3
        pool.tensor_tensor(by_head(dst), by_head(dst), rstd[:].unsqueeze(2).to_broadcast([P, GROUP // dim, dim]),
                           ALU.mult).then_inc(S["normed_ready"], 1)
        pool.wait_ge(S["normed_ready"], i + 1)
        pool.dma_start(mix_scratch[i * P:(i + 1) * P, mix_col:mix_col + GROUP], dst).then_inc(stored[i % 2], 16)
    for s in range(2):
        pool.wait_ge(stored[s], 16 * (TOK_TILES // 2))


def sum_squares(dve, S, sumsq, squares, dim, i):
    dve.wait_ge(S["squared"], i + 1)
    if i >= 1:
        dve.wait_ge(S["normed_ready"], i)
    dve.tensor_reduce(sumsq[:], squares[:].rearrange("p (h d) -> p h d", d=dim), AX.X, ALU.add)\
       .then_inc(S["summed"], 1)


def copy_heads(act, S, heads_out, o_bank, applied, i):
    act.wait_ge(S["applied"], applied)
    if i >= 2:
        act.wait_ge(S["normed_ready"], i - 1)
    act.activation(heads_out[:, i % 2, :], o_bank[i % 2][:], ACT.Copy).then_inc(S["o_copied"], 1)


def phase_stick_breaking(nc, qk_scratch, v_scratch, g_rep_dram, ident, mask, mix_scratch):
    q_row, k_row = 0, GROUP
    dim = HEAD_DIM
    ctx = ExitStack()
    with ctx:
        sb = lambda n, s, d=F32: ctx.enter_context(nc.sbuf_tensor(n, s, d))
        sem = lambda n: ctx.enter_context(nc.semaphore(n))
        k_st = sb("e_k", [P, HEADS, SEQ], F32R)
        v_sb = sb("e_v", [P, TOK_TILES, GROUP])
        q_st = [sb(f"e_q{s}", [P, 2, P], F32R) for s in range(2)]
        work = [sb(f"e_work{s}", [P, CHUNK]) for s in range(2)]
        attn = [sb(f"e_attn{s}", [P, CHUNK]) for s in range(2)]
        attn_t = [sb(f"e_attn_t{s}", [P, CHUNK]) for s in range(2)]
        carry = sb("e_carry", [P, 1])
        heads_out, normed = sb("e_heads", [P, 2, GROUP]), sb("e_normed", [P, 2, GROUP])
        squares = sb("e_squares", [P, GROUP])
        g_rep = sb("e_g", [P, GROUP])
        sumsq, var, rstd, exponent = (sb(f"e_{n}", [P, HEADS]) for n in ("sumsq", "var", "rstd", "exponent"))
        z = [ctx.enter_context(nc.psum_tensor(f"e_z{s}", [P, CHUNK], F32)) for s in range(2)]
        t_bank = ctx.enter_context(nc.psum_tensor("e_t", [P, CHUNK], F32))
        o_bank = [ctx.enter_context(nc.psum_tensor(f"e_o{s}", [P, GROUP], F32)) for s in range(2)]
        kv_loaded = [sem(f"e_kv{p}") for p in range(3)]
        q_loaded = [sem(f"e_q_loaded{s}") for s in range(2)]
        names = ["scored", "exped", "clipped_half", "clipped", "logged_half", "logged", "plused", "masked", "linked", "scanned", "attn_done",
                 "transposed", "evacuated", "applied", "var_ready", "powered"]
        S = {n: sem(f"e_{n}") for n in names + ["norm_chain", "o_copied", "normed_ready", "g_loaded", "pool_chain"]}
        stored = [sem(f"e_stored{s}") for s in range(2)]

        pairs_of = [HEADS // 2 * len(chunks_of(i)) for i in range(TOK_TILES)]
        first_step = [2 * sum(pairs_of[:i]) for i in range(TOK_TILES + 1)]

        split = first_step[CHUNK_TILES]

        FIRST_HALVED = 3
        halved_before = first_step[FIRST_HALVED]

        def step(i, pair, s):
            chunks = chunks_of(i)
            two = len(chunks) == 2
            key_tile, tiles = chunks[1 - s] if two else chunks[0]
            return dict(i=i, s=s, g=pair * 2 + (first_step[i] + s), pair=pair + first_step[i] // 2,
                        head=pair if two else pair * 2 + s, key_tile=key_tile, tiles=tiles, width=tiles * P,
                        diagonal=key_tile + tiles == i + 1,
                        peeled=isinstance(pair, int),
                        half=tiles * P // 2 if i >= FIRST_HALVED else 0,
                        masks=(pair + (first_step[i] - split) // 2) + (split + 1) if two else
                        pair * 2 + (first_step[i] + s + 1), opens=not two or s == 0, closes=not two or s == 1,
                        first=(i == 0 and s == 0), two=two)

        def schedule(eng, body, tile_end):
            late = [None] * 4
            for i in range(TOK_TILES):
                for pair in range(2 if i else pairs_of[0]):
                    for s in range(2):
                        now = step(i, pair, s)
                        body(now, *late)
                        late = [now] + late[:3]
                if i:
                    tile_end(i - 1)
                    with eng.Fori(2, pairs_of[i]) as pair:
                        now = [step(i, pair + k // 2, k % 2) for k in (1, 0, -1, -2, -3, -4)]
                        body(*now[1:6])
                        body(*now[0:5])
                    late = [step(i, pairs_of[i] + k // 2, k % 2) for k in (-1, -2, -3, -4)]
            for n in range(4):
                body(*[None] * (n + 1), *late[:4 - n])
            tile_end(TOK_TILES - 1)

        block = ctx.enter_context(nc.Block())

        @block.sync
        def _(sp):
            def body(cur, prev, prev2, prev3, prev4):
                if cur is None:
                    return
                if prev2 is not None:
                    sp.wait_ge(S["scored"], cur["g"] - 1)
                load_query(sp, q_st[cur["s"]], qk_scratch, q_row, cur["head"], cur["i"], q_loaded[cur["s"]])
                if cur["first"] and prev is None:
                    load_keys_values(sp, k_st, v_sb, qk_scratch, v_scratch, k_row, 1, kv_loaded, [0])
                    sp.dma_start(g_rep[:], g_rep_dram).then_inc(S["g_loaded"], 16)

            schedule(sp, body, lambda i: None)

        @block.tensor
        def _(pe):
            def body(cur, prev, prev2, prev3, prev4):
                if cur is not None:
                    if cur["s"] == 0 and (cur["i"] == 0 or PIECE_OF_TILE[cur["i"]] != PIECE_OF_TILE[cur["i"] - 1]) \
                            and (prev is None or prev["i"] != cur["i"]):
                        pe.wait_ge(kv_loaded[PIECE_OF_TILE[cur["i"]]], 48)
                    pe.wait_ge(q_loaded[cur["s"]], cur["pair"] * 32 + 32)
                    if prev2 is not None:
                        pe.wait_ge(S["scanned"], cur["g"] - 1)
                    score_matmuls(pe, z[cur["s"]], q_st[cur["s"]], k_st, cur["head"], cur["key_tile"],
                                  cur["tiles"], False, None, None).then_inc(S["scored"], 1)
                if prev3 is not None:
                    pe.wait_ge(S["attn_done"], prev3["g"] + 1)
                    if prev4 is not None:
                        pe.wait_ge(S["evacuated"], prev3["g"])
                    for j in range(prev3["tiles"]):
                        mm = pe.transpose(t_bank[:, j * P:(j + 1) * P], attn[prev3["s"]][:, j * P:(j + 1) * P], ident[:])
                    mm.then_inc(S["transposed"], 1)
                if prev4 is not None:
                    o = o_bank[prev4["i"] % 2]
                    pe.wait_ge(S["evacuated"], prev4["g"] + 1)
                    if prev4["i"] >= 2 and prev4["s"] == 0:
                        pe.wait_ge(S["o_copied"], prev4["i"] - 1)
                    for j in range(prev4["tiles"]):
                        mm = pe.matmul(o[:, ds(prev4["head"] * dim, dim)], attn_t[prev4["s"]][:, j * P:(j + 1) * P],
                                       v_sb[:, prev4["key_tile"] + j, ds(prev4["head"] * dim, dim)],
                                       start=(prev4["opens"] and j == 0),
                                       stop=(prev4["closes"] and j == prev4["tiles"] - 1))
                    mm.then_inc(S["applied"], 1)

            schedule(pe, body, lambda i: None)

        @block.scalar
        def _(act):
            def body(cur, prev, prev2, prev3, prev4):
                if prev is not None:
                    w, h, t = prev["width"], prev["half"], work[prev["s"]]
                    if h:
                        act.wait_ge(S["clipped_half"], prev["g"] + 1 - halved_before)
                        act.activation(t[:, 0:h], t[:, 0:h], ACT.Ln, bias=1.0).then_inc(S["logged_half"], 1)
                    act.wait_ge(S["clipped"], prev["g"] + 1)
                    act.activation(t[:, h:w], t[:, h:w], ACT.Ln, bias=1.0).then_inc(S["logged"], 1)
                if prev2 is not None:
                    w, s = prev2["width"], prev2["s"]
                    act.wait_ge(S["scanned"], prev2["g"] + 1)
                    if prev4 is not None:
                        act.wait_ge(S["transposed"], prev2["g"] - 1)
                    act.activation(attn[s][:, 0:w], work[s][:, 0:w], ACT.Exp, scale=-1.0)\
                       .then_inc(S["attn_done"], 1)
                if cur is not None:
                    w, s = cur["width"], cur["s"]
                    act.wait_ge(S["scored"], cur["g"] + 1)
                    if prev2 is not None:
                        act.wait_ge(S["attn_done"], cur["g"] - 1)
                    act.activation(work[s][:, 0:w], z[s][:, 0:w], ACT.Exp, scale=-1.0).then_inc(S["exped"], 1)
                if prev3 is not None:
                    w, s = prev3["width"], prev3["s"]
                    act.wait_ge(S["transposed"], prev3["g"] + 1)
                    if not isinstance(prev3["g"], int) or prev3["g"] >= 2:
                        act.wait_ge(S["applied"], prev3["g"] - 1)
                    act.activation(attn_t[s][:, 0:w], t_bank[:, 0:w], ACT.Copy).then_inc(S["evacuated"], 1)

            def tile_end(i):
                copy_heads(act, S, heads_out, o_bank, first_step[i + 1], i)

            act.preload_act_table_set("natural_log_exp_and_others")
            schedule(act, body, tile_end)

        @block.vector
        def _(dve):
            by_head = lambda t: t.rearrange("p (h d) -> p h d", d=dim)

            def norm(i, stage):
                src, dst = heads_out[:, i % 2, :], normed[:, i % 2, :]
                chain = S["norm_chain"]
                if stage == 0:
                    dve.wait_ge(S["o_copied"], i + 1)
                    link(dve, chain, 4 * i + 1, dve.tensor_tensor(squares[:], src, src, ALU.mult))
                elif stage == 1:
                    link(dve, chain, 4 * i + 2, dve.tensor_reduce(sumsq[:], by_head(squares[:]), AX.X, ALU.add))
                    dve.tensor_scalar(var[:], sumsq[:], 1.0 / dim, EPS, ALU.mult, ALU.add)\
                       .then_inc(S["var_ready"], 1)
                elif stage == 2:
                    dve.wait_ge(S["powered"], i + 1)
                    link(dve, chain, 4 * i + 3,
                         dve.tensor_tensor(by_head(squares[:]), by_head(src),
                                           rstd[:].unsqueeze(2).to_broadcast([P, HEADS, dim]), ALU.mult))
                else:
                    if i == 0:
                        dve.wait_ge(S["g_loaded"], 16)
                    if i >= 2:
                        dve.wait_ge(stored[i % 2], 16 * (i // 2))
                    link(dve, chain, 4 * i + 4, dve.tensor_tensor(dst, squares[:], g_rep[:], ALU.mult))
                    dve.sem_inc(S["normed_ready"], 1)

            def body(cur, prev, prev2, prev3, prev4):
                if cur is None:
                    return
                s, w = cur["s"], cur["width"]
                t, scores = work[s], z[s]
                h = cur["half"]
                dve.wait_ge(S["exped"], cur["g"] + 1)
                if h:
                    dve.tensor_scalar(t[:, 0:h], t[:, 0:h], 2.0 ** 60, None, ALU.min).then_inc(S["clipped_half"], 1)
                dve.tensor_scalar(t[:, h:w], t[:, h:w], 2.0 ** 60, None, ALU.min).then_inc(S["clipped"], 1)
                if cur["diagonal"]:
                    own = scores[:, w - P:w]
                    link(dve, S["masked"], cur["masks"], dve.tensor_tensor(own, own, mask[:], ALU.add))
                def plus(cols):
                    return dve.scalar_tensor_tensor(out=t[:, cols], in0=scores[:, cols], scalar=-1.0, in1=t[:, cols],
                                                    op0=ALU.mult, op1=ALU.max)
                if h:
                    dve.wait_ge(S["logged_half"], cur["g"] + 1 - halved_before)
                    plus(slice(0, h))
                dve.wait_ge(S["logged"], cur["g"] + 1)
                plus(slice(h, w)).then_inc(S["plused"], 1)
                dve.wait_ge(S["plused"], cur["g"] + 1)
                links = (cur["pair"] - first_step[CHUNK_TILES] // 2) * 2
                last = t[:, w - 1:w]
                if cur["two"] and s == 1:
                    dve.wait_ge(S["scanned"], cur["g"])
                    link(dve, S["linked"], links + 2, dve.tensor_tensor(last, last, carry[:], ALU.add))
                back = t[:, 0:w - 1][:, ::-1]
                scan = dve.tensor_tensor_scan(back, scores[:, 1:w][:, ::-1], back, last, ALU.add, ALU.add)
                if cur["two"] and s == 0:
                    link(dve, S["linked"], links + 1, scan)
                    dve.tensor_tensor(carry[:], scores[:, 0:1], t[:, 0:1], ALU.add).then_inc(S["scanned"], 1)
                else:
                    scan.then_inc(S["scanned"], 1)
                if cur["i"] >= 2 and cur["peeled"]:
                    norm(cur["i"] - 2, cur["g"] - first_step[cur["i"]])

            schedule(dve, body, lambda i: None)
            for i in (TOK_TILES - 2, TOK_TILES - 1):
                for stage in range(4):
                    norm(i, stage)

        @block.gpsimd
        def _(pool):
            load_keys_values(pool, k_st, v_sb, qk_scratch, v_scratch, k_row, 1, kv_loaded, [1, 2])
            link(pool, S["pool_chain"], 1, pool.memset(exponent[:], -0.5))

            def power(i):
                pool.wait_ge(S["var_ready"], i + 1)
                pool.tensor_tensor(rstd[:], var[:], exponent[:], ALU.pow).then_inc(S["powered"], 1)

            for i in range(TOK_TILES):
                power(i)
                pool.wait_ge(S["normed_ready"], i + 1)
                pool.dma_start(mix_scratch[i * P:(i + 1) * P, GROUP:2 * GROUP], normed[:, i % 2, :])\
                    .then_inc(stored[i % 2], 16)
            for s in range(2):
                pool.wait_ge(stored[s], 16 * (TOK_TILES // 2))


def phase_differential(nc, qk_scratch, v_scratch, lambdas_dram, g_rep_dram, ident, ident_bf, mask_bf, mix_scratch):
    q_row, k_row = 2 * GROUP, 3 * GROUP
    dim = 2 * HEAD_DIM
    ctx = ExitStack()
    with ctx:
        sb = lambda n, s, d=F32: ctx.enter_context(nc.sbuf_tensor(n, s, d))
        sem = lambda n: ctx.enter_context(nc.semaphore(n))
        k_st = sb("d_k", [P, HEADS, SEQ], F32R)
        v_sb = sb("d_v", [P, TOK_TILES, GROUP])
        q_st = [sb(f"d_q{s}", [P, 2, P], F32R) for s in range(2)]
        probs = [sb(f"d_probs{k}", [P, CHUNK]) for k in range(4)]
        attn = [sb(f"d_attn{u}", [P, CHUNK]) for u in range(2)]
        attn_t = [sb(f"d_attn_t{u}", [P, CHUNK]) for u in range(2)]
        row_max, neg_max, row_sum = sb("d_max", [P, 4]), sb("d_negmax", [P, 4]), sb("d_sum", [P, 4])
        neg_all, shift, weight = sb("d_negall", [P, 2]), sb("d_shift", [P, 4]), sb("d_weight", [P, 4])
        total, inverse, factor = sb("d_total", [P, 4]), sb("d_inverse", [P, 4]), sb("d_factor", [P, 4])
        sign = sb("d_sign", [P, 4])
        lambdas, lam_prod = sb("d_lambdas", [P, 4, HEAD_DIM]), sb("d_lamprod", [P, 2, HEAD_DIM])
        lam_dot, lam_exp = sb("d_lamdot", [P, 2]), sb("d_lamexp", [P, 2])
        heads_out, normed = sb("d_heads", [P, 2, GROUP]), sb("d_normed", [P, 2, GROUP])
        squares, g_rep = sb("d_squares", [P, GROUP]), sb("d_g", [P, GROUP])
        sumsq, var, rstd, exponent = (sb(f"d_{n}", [P, GROUP // dim]) for n in ("sumsq", "var", "rstd", "exponent"))
        z = [ctx.enter_context(nc.psum_tensor(f"d_z{s}", [P, CHUNK], F32)) for s in range(2)]
        t_bank = ctx.enter_context(nc.psum_tensor("d_t", [P, CHUNK], F32))
        o_bank = [ctx.enter_context(nc.psum_tensor(f"d_o{s}", [P, GROUP], F32)) for s in range(2)]
        kv_loaded = [sem(f"d_kv{p}") for p in range(3)]
        q_loaded = [sem(f"d_q_loaded{s}") for s in range(2)]
        names = ["scored", "reduced", "maxed", "exped", "shifted", "weighed", "stats_chain", "combined",
                 "transposed", "evacuated", "applied", "lambda_loaded", "lambda_ready", "lambda_chain"]
        S = {n: sem(f"d_{n}") for n in names + NORM_SEMS}
        stored = [sem(f"d_stored{s}") for s in range(2)]

        two = [len(chunks_of(i)) == 2 for i in range(TOK_TILES)]
        quads_of = [4 if two[i] else 2 for i in range(TOK_TILES)]
        first_quad = [sum(quads_of[:i]) for i in range(TOK_TILES + 1)]
        stat_steps = [8 if two[i] else 4 for i in range(TOK_TILES)]
        first_stat = [sum(stat_steps[j] * quads_of[j] for j in range(i)) for i in range(TOK_TILES)]

        def quad(i, q):
            return dict(i=i, q=q, n=q + first_quad[i])

        def step(Q, k):
            i = Q["i"]
            key_tile, tiles = chunks_of(i)[k % 2] if two[i] else chunks_of(i)[0]
            return dict(i=i, s=k % 2, g=Q["n"] * 4 + k, map=Q["q"] * 2 + k // 2 if two[i] else Q["q"] * 4 + k,
                        key_tile=key_tile, tiles=tiles, width=tiles * P, diagonal=key_tile + tiles == i + 1)

        def unit(Q, u):
            i = Q["i"]
            key_tile, tiles = chunks_of(i)[u] if two[i] else chunks_of(i)[0]
            return dict(i=i, u=u, a=Q["n"] * 2 + u, head=Q["q"] if two[i] else Q["q"] * 2 + u,
                        key_tile=key_tile, tiles=tiles, width=tiles * P,
                        maps=(u, 2 + u) if two[i] else (2 * u, 2 * u + 1),
                        opens=not two[i] or u == 0, closes=not two[i] or u == 1)

        def schedule(eng, body, tile_end):
            late = [None, None]
            for i in range(TOK_TILES):
                for q in range(2):
                    now = quad(i, q)
                    body(now, *late)
                    late = [now, late[0]]
                if i:
                    tile_end(i - 1)
                if quads_of[i] > 2:
                    with eng.Fori(2, quads_of[i]) as q:
                        body(*[quad(i, q - k) for k in range(3)])
                    late = [quad(i, quads_of[i] - 1 - k) for k in range(2)]
            body(None, *late)
            body(None, None, late[0])
            tile_end(TOK_TILES - 1)

        block = ctx.enter_context(nc.Block())

        @block.sync
        def _(sp):
            def body(cur, prev, prev2):
                if cur is None:
                    return
                for k in range(4):
                    t = step(cur, k)
                    if prev is not None or k >= 2:
                        sp.wait_ge(S["scored"], t["g"] - 1)
                    load_query(sp, q_st[t["s"]], qk_scratch, q_row, t["map"], t["i"], q_loaded[t["s"]])
                    if prev is None and k == 0:
                        load_keys_values(sp, k_st, v_sb, qk_scratch, v_scratch, k_row, 0, kv_loaded, [0])
                        sp.dma_start(lambdas[:], lambdas_dram).then_inc(S["lambda_loaded"], 16)
                        sp.dma_start(g_rep[:], g_rep_dram).then_inc(S["g_loaded"], 16)

            schedule(sp, body, lambda i: None)

        @block.tensor
        def _(pe):
            def scores(cur, k):
                t = step(cur, k)
                pe.wait_ge(q_loaded[t["s"]], cur["n"] * 64 + 32 * (k // 2 + 1))
                if not isinstance(t["g"], int) or t["g"] >= 2:
                    pe.wait_ge(S["exped"], t["g"] - 1)
                score_matmuls(pe, z[t["s"]], q_st[t["s"]], k_st, t["map"], t["key_tile"], t["tiles"],
                              t["diagonal"], ident_bf, mask_bf).then_inc(S["scored"], 1)

            def turn(prev, n):
                t = unit(prev, n)
                pe.wait_ge(S["combined"], t["a"] + 1)
                pe.wait_ge(S["evacuated"], t["a"])
                for j in range(t["tiles"]):
                    mm = pe.transpose(t_bank[:, j * P:(j + 1) * P], attn[n][:, j * P:(j + 1) * P], ident[:])
                mm.then_inc(S["transposed"], 1)

            def apply(prev, n):
                t = unit(prev, n)
                o = o_bank[t["i"] % 2]
                pe.wait_ge(S["evacuated"], t["a"] + 1)
                if t["i"] >= 2 and n == 0:
                    pe.wait_ge(S["o_copied"], t["i"] - 1)
                for j in range(t["tiles"]):
                    mm = pe.matmul(o[:, ds(t["head"] * dim, dim)], attn_t[n][:, j * P:(j + 1) * P],
                                   v_sb[:, t["key_tile"] + j, ds(t["head"] * dim, dim)],
                                   start=(t["opens"] and j == 0), stop=(t["closes"] and j == t["tiles"] - 1))
                mm.then_inc(S["applied"], 1)

            def body(cur, prev, prev2):
                if cur is not None:
                    piece = PIECE_OF_TILE[cur["i"]]
                    if prev is None or (prev["i"] != cur["i"] and piece != PIECE_OF_TILE[prev["i"]]):
                        pe.wait_ge(kv_loaded[piece], 48)
                    scores(cur, 0)
                    scores(cur, 1)
                if prev2 is not None:
                    apply(prev2, 1)
                if prev is not None:
                    turn(prev, 0)
                if cur is not None:
                    scores(cur, 2)
                if prev is not None:
                    apply(prev, 0)
                if cur is not None:
                    scores(cur, 3)
                if prev is not None:
                    turn(prev, 1)

            schedule(pe, body, lambda i: None)

        @block.scalar
        def _(act):
            def exponentials(cur, prev, k):
                t = step(cur, k)
                act.wait_ge(S["maxed"], t["g"] + 1)
                if prev is not None:
                    user = next(u for u in range(2) if k in unit(prev, u)["maps"])
                    act.wait_ge(S["combined"], prev["n"] * 2 + (user + 1))
                act.activation(probs[k][:, 0:t["width"]], z[t["s"]][:, 0:t["width"]], ACT.Exp,
                               bias=neg_max[:, k:k + 1], accum_out=row_sum[:, k:k + 1]).then_inc(S["exped"], 1)

            def evacuate(prev, n):
                t = unit(prev, n)
                act.wait_ge(S["transposed"], t["a"] + 1)
                if not isinstance(t["a"], int) or t["a"] >= 2:
                    act.wait_ge(S["applied"], t["a"] - 1)
                act.activation(attn_t[n][:, 0:t["width"]], t_bank[:, 0:t["width"]], ACT.Copy)\
                   .then_inc(S["evacuated"], 1)

            def body(cur, prev, prev2):
                if prev is not None and two[prev["i"]]:
                    number = prev["n"] + 1 - first_quad[CHUNK_TILES]
                    act.wait_ge(S["shifted"], number)
                    act.activation(weight[:], shift[:], ACT.Exp).then_inc(S["weighed"], 1)
                if prev2 is not None:
                    evacuate(prev2, 1)
                if cur is not None:
                    exponentials(cur, prev, 0)
                if prev is not None:
                    evacuate(prev, 0)
                if cur is not None:
                    for k in (1, 2, 3):
                        exponentials(cur, prev, k)

            act.preload_act_table_set("natural_log_exp_and_others")
            act.wait_ge(S["lambda_ready"], 1)
            act.activation(lam_exp[:], lam_dot[:], ACT.Exp).then_inc(S["lambda_ready"], 1)
            schedule(act, body, lambda i: copy_heads(act, S, heads_out, o_bank, 2 * first_quad[i + 1], i))

        @block.vector
        def _(dve):
            def maximum(cur, k):
                t = step(cur, k)
                dve.wait_ge(S["scored"], t["g"] + 1)
                dve.tensor_reduce(row_max[:, k:k + 1], z[t["s"]][:, 0:t["width"]], AX.X, ALU.max)\
                   .then_inc(S["reduced"], 1)
                dve.wait_ge(S["reduced"], t["g"] + 1)
                dve.tensor_scalar(neg_max[:, k:k + 1], row_max[:, k:k + 1], -1.0, None, ALU.mult)\
                   .then_inc(S["maxed"], 1)

            def factors(cur, prev):
                i = prev["i"]
                base = prev["q"] * stat_steps[i] + first_stat[i]
                if not two[i]:
                    if cur is not None:
                        maximum(cur, 0)
                    dve.wait_ge(S["exped"], prev["n"] * 4 + 4)
                    link(dve, S["stats_chain"], base + 1, dve.reciprocal(inverse[:], row_sum[:]))
                    link(dve, S["stats_chain"], base + 2,
                         dve.tensor_tensor(factor[:], inverse[:], sign[:], ALU.mult))
                    return base + 2
                by_map = lambda t: t[:].rearrange("p (m c) -> p m c", c=2)
                wide = lambda t: t[:, 0:2].unsqueeze(2).to_broadcast([P, 2, 2])
                number = prev["n"] + 1 - first_quad[CHUNK_TILES]
                dve.wait_ge(S["maxed"], prev["n"] * 4 + 4)
                link(dve, S["stats_chain"], base + 1,
                     dve.tensor_tensor(neg_all[:], neg_max[:, 0:4:2], neg_max[:, 1:4:2], ALU.min))
                dve.tensor_tensor(by_map(shift), wide(neg_all), by_map(neg_max), ALU.subtract)\
                   .then_inc(S["shifted"], 1)
                dve.wait_ge(S["shifted"], number)
                if cur is not None:
                    maximum(cur, 0)
                dve.wait_ge(S["exped"], prev["n"] * 4 + 4)
                dve.wait_ge(S["weighed"], number)
                link(dve, S["stats_chain"], base + 2, dve.tensor_tensor(total[:], row_sum[:], weight[:], ALU.mult))
                link(dve, S["stats_chain"], base + 3,
                     dve.tensor_tensor(inverse[:, 0:2], total[:, 0:4:2], total[:, 1:4:2], ALU.add))
                link(dve, S["stats_chain"], base + 4, dve.reciprocal(inverse[:, 2:4], inverse[:, 0:2]))
                link(dve, S["stats_chain"], base + 5,
                     dve.tensor_tensor(inverse[:, 0:2], inverse[:, 2:4], sign[:, 0:2], ALU.mult))
                link(dve, S["stats_chain"], base + 6,
                     dve.tensor_tensor(by_map(factor), by_map(weight), wide(inverse), ALU.mult))
                return base + 6

            def combine(prev, n, count):
                t = unit(prev, n)
                w, (one, other) = t["width"], t["maps"]
                link(dve, S["stats_chain"], count + 1 + n,
                     dve.tensor_scalar(probs[other][:, 0:w], probs[other][:, 0:w],
                                       factor[:, other:other + 1], None, ALU.mult))
                if not isinstance(t["a"], int) or t["a"] >= 2:
                    dve.wait_ge(S["transposed"], t["a"] - 1)
                dve.scalar_tensor_tensor(out=attn[n][:, 0:w], in0=probs[one][:, 0:w],
                                         scalar=factor[:, one:one + 1], in1=probs[other][:, 0:w],
                                         op0=ALU.mult, op1=ALU.add).then_inc(S["combined"], 1)

            def body(cur, prev, prev2):
                count = None
                if prev is not None:
                    count = factors(cur, prev)
                    combine(prev, 0, count)
                elif cur is not None:
                    maximum(cur, 0)
                if cur is not None:
                    maximum(cur, 1)
                if prev is not None:
                    combine(prev, 1, count)
                if cur is not None:
                    maximum(cur, 2)
                    maximum(cur, 3)
                    if prev is not None and prev["i"] != cur["i"] and cur["i"] >= 2:
                        sum_squares(dve, S, sumsq, squares, dim, cur["i"] - 2)

            dve.wait_ge(S["lambda_loaded"], 16)
            pairs = lambdas[:].rearrange("p (m s) d -> p m s d", s=2)
            n = S["lambda_chain"]
            link(dve, n, 1, dve.memset(sign[:], 1.0))
            link(dve, n, 2, dve.tensor_tensor(lam_prod[:], pairs[:, :, 0, :], pairs[:, :, 1, :], ALU.mult))
            dve.tensor_reduce(lam_dot[:], lam_prod[:], AX.X, ALU.add).then_inc(S["lambda_ready"], 1)
            dve.wait_ge(S["lambda_ready"], 2)
            link(dve, n, 3, dve.tensor_tensor(lam_dot[:, 0:1], lam_exp[:, 1:2], lam_exp[:, 0:1], ALU.subtract))
            for k in (1, 3):
                link(dve, n, 3 + (k + 1) // 2,
                     dve.tensor_scalar(sign[:, k:k + 1], lam_dot[:, 0:1], -LAMBDA_INIT, None, ALU.add))
            schedule(dve, body, lambda i: None)
            for i in (TOK_TILES - 2, TOK_TILES - 1):
                sum_squares(dve, S, sumsq, squares, dim, i)

        @block.gpsimd
        def _(pool):
            load_keys_values(pool, k_st, v_sb, qk_scratch, v_scratch, k_row, 0, kv_loaded, [1, 2])
            norm_tiles(pool, S, stored, heads_out, normed, squares, g_rep, sumsq, var, rstd, exponent,
                       dim, 1.0 - LAMBDA_INIT, mix_scratch, 0)


FT = D_FF // P
OUT_ITEMS = 2 * KC // 2
GATE_ITEM = OUT_ITEMS
DOWN_ITEM = OUT_ITEMS + 2 * FT
ITEMS = DOWN_ITEM + 2 * FT // 2
HALF = D_MODEL // 2


def phase_ffn(nc, x, mix_scratch, w_stream, g_ffn_dram, g_final_dram, ident, out):
    assert ITEMS % 2 == 0 and FT % 2 == 0
    ctx = ExitStack()
    with ctx:
        sb = lambda n, s, d=F32: ctx.enter_context(nc.sbuf_tensor(n, s, d))
        sem = lambda n: ctx.enter_context(nc.semaphore(n))
        w_raw = [sb(f"f_wraw{s}", [P, D_MODEL]) for s in range(2)]
        w_hi = [sb(f"f_whi{s}", [P, D_MODEL], F32R) for s in range(2)]
        w_lo = [sb(f"f_wlo{s}", [P, D_MODEL], F32R) for s in range(2)]
        natural = sb("f_natural", [P, TPB, D_MODEL])
        turned_hi, turned_lo = sb("f_thi", [P, KC, BLK], F32R), sb("f_tlo", [P, KC, BLK], F32R)
        x_in, x_sum = sb("f_xin", [P, TPB, D_MODEL]), sb("f_xsum", [P, TPB, D_MODEL])
        act_hi, act_lo = sb("f_ahi", [P, FT, BLK], F32R), sb("f_alo", [P, FT, BLK], F32R)
        gated = sb("f_gated", [P, 2, BLK])
        g_final, g_ffn = sb("f_gfinal", [P, D_MODEL]), sb("f_gffn", [P, KC])
        sumsq, var, rstd, exponent = (sb(f"f_{n}", [P, TPB]) for n in ("sumsq", "var", "rstd", "exponent"))
        bank = [ctx.enter_context(nc.psum_tensor(f"f_ps{i}", [P, BLK], F32)) for i in range(8)]
        w_loaded = [sem(f"f_w_loaded{s}") for s in range(2)]
        names = ["consts", "mix_loaded", "x_loaded", "mix_turned", "mix_hi", "mix_lo", "hi_split", "lo_split",
                 "multiplied", "x1_half", "squared", "var_ready", "powered", "scaled", "h2_turned", "h2_hi",
                 "h2_lo", "silued", "producted", "act_hi", "act_lo", "x2_half", "final", "stored", "pool_chain"]
        S = {n: sem(f"f_{n}") for n in names}
        x_blocks = x.rearrange("(b t p) n -> b p t n", t=TPB, p=P)
        mix_blocks = mix_scratch.rearrange("(b t p) n -> b p t n", t=TPB, p=P)
        out_blocks = out.rearrange("(b t p) n -> b p t n", t=TPB, p=P)
        one = lambda ap: ap.rearrange("o p t n -> (o p) t n")
        done = lambda b, j: b * ITEMS + (j + 2)
        block = ctx.enter_context(nc.Block())

        @block.sync
        def _(sp):
            for s in range(2):
                sp.dma_start(w_raw[s][:], w_stream[s]).then_inc(w_loaded[s], 16)
            sp.dma_start(g_final[:], g_final_dram).then_inc(S["consts"], 16)
            sp.dma_start(g_ffn[:], g_ffn_dram).then_inc(S["consts"], 16)
            with sp.Fori(0, BLOCKS) as b:
                sp.wait_ge(S["h2_turned"], b * KC)
                sp.dma_start(natural[:], one(mix_blocks[ds(b, 1)])).then_inc(S["mix_loaded"], 16)
                sp.wait_ge(S["x1_half"], b * (2 * TPB))
                sp.dma_start(x_in[:], one(x_blocks[ds(b, 1)])).then_inc(S["x_loaded"], 16)
                with sp.Fori(0, ITEMS // 2) as pair:
                    for s in range(2):
                        sp.wait_ge(S["lo_split"], b * ITEMS + pair * 2 + (s + 1))
                        sp.dma_start(w_raw[s][:], w_stream[ds(pair * 2 + (s + 2), 1)]
                                     .rearrange("o p n -> (o p) n")).then_inc(w_loaded[s], 16)
            for s in range(2):
                sp.wait_ge(w_loaded[s], 16 * (BLOCKS * ITEMS // 2 + 1))

        @block.gpsimd
        def _(pool):
            pool.memset(exponent[:], -0.5).then_inc(S["pool_chain"], 1)
            pool.wait_ge(S["pool_chain"], 1)
            with pool.Fori(0, BLOCKS) as b:
                for which in range(2):
                    pool.wait_ge(S["var_ready"], b * 2 + (which + 1))
                    pool.tensor_tensor(rstd[:], var[:], exponent[:], ALU.pow).then_inc(S["powered"], 1)
                for t in range(TPB):
                    pool.wait_ge(S["final"], b * TPB + (t + 1))
                    pool.dma_start(out_blocks[ds(b, 1), :, t, :].rearrange("o p n -> (o p) n"),
                                   x_sum[:, t, :]).then_inc(S["stored"], 16)
            pool.wait_ge(S["stored"], 16 * BLOCKS * TPB)

        @block.scalar
        def _(act):
            def split_hi(b, j):
                s = j % 2
                act.wait_ge(w_loaded[s], b * (ITEMS // 2 * 16) + (j // 2 + 1) * 16)
                act.wait_ge(S["multiplied"], b * ITEMS + j)
                act.activation(w_hi[s][:], w_raw[s][:], ACT.Copy).then_inc(S["hi_split"], 1)

            def squares(b, which, source):
                for t in range(TPB):
                    act.wait_ge(S[source], b * (2 * TPB) + (TPB + t + 1))
                    if which or t:
                        act.wait_ge(S["squared"], b * (2 * TPB) + (which * TPB + t))
                    act.activation(junk, x_sum[:, t, :], ACT.Square, accum_out=sumsq[:, t:t + 1])\
                       .then_inc(S["squared"], 1)

            junk = act_hi[:, 0:2, :].rearrange("p a n -> p (a n)")
            act.preload_act_table_set("silu_and_others")
            split_hi(0, 0)
            act.wait_ge(S["consts"], 32)
            with act.Fori(0, BLOCKS) as b:
                for k in range(KC):
                    act.wait_ge(S["mix_turned"], b * KC + (k + 1))
                    act.activation(turned_hi[:, k, :], bank[k][:], ACT.Copy).then_inc(S["mix_hi"], 1)
                for j in range(OUT_ITEMS):
                    split_hi(b, j + 1)
                squares(b, 0, "x1_half")
                for k in range(KC):
                    act.wait_ge(S["h2_turned"], b * KC + (k + 1))
                    act.activation(turned_hi[:, k, :], bank[k][:], ACT.Copy, scale=g_ffn[:, k:k + 1])\
                       .then_inc(S["h2_hi"], 1)
                with act.Fori(0, FT // 2) as pair:
                    for e in range(2):
                        item = b * ITEMS + pair * 4 + (GATE_ITEM + 2 * e)
                        f = b * FT + pair * 2 + e
                        for n in (1, 2):
                            s = n % 2
                            loads = b * (ITEMS // 2 * 16) + pair * 32 + ((GATE_ITEM + 2 * e + n) // 2 + 1) * 16
                            act.wait_ge(w_loaded[s], loads)
                            act.wait_ge(S["multiplied"], item + n)
                            act.activation(w_hi[s][:], w_raw[s][:], ACT.Copy).then_inc(S["hi_split"], 1)
                            if n == 1:
                                act.wait_ge(S["multiplied"], item + 2)
                                act.wait_ge(S["act_lo"], f)
                                act.activation(gated[:, e, :], bank[2 * e][:], ACT.Silu)\
                                   .then_inc(S["silued"], 1)
                        act.wait_ge(S["producted"], f + 2)
                        act.activation(act_hi[:, ds(pair * 2 + e, 1), :].rearrange("p o n -> p (o n)"),
                                       gated[:, e, :], ACT.Copy).then_inc(S["act_hi"], 1)
                for j in range(DOWN_ITEM, ITEMS):
                    split_hi(b, j + 1)
                squares(b, 1, "x2_half")

        @block.vector
        def _(dve):
            def split_lo(s, number):
                dve.wait_ge(S["hi_split"], number + 1)
                dve.tensor_tensor(w_lo[s][:], w_raw[s][:], w_hi[s][:].bitcast(F32), ALU.subtract)\
                   .then_inc(S["lo_split"], 1)

            def add_half(b, item, half, first_bank, inc, source):
                cols = slice(half * HALF, (half + 1) * HALF)
                dve.wait_ge(S["multiplied"], done(b, item))
                for t in range(TPB):
                    dve.tensor_tensor(x_sum[:, t, cols], bank[first_bank + t][:], source[:, t, cols], ALU.add)\
                       .then_inc(S[inc], 1)

            def variance(b, which):
                dve.wait_ge(S["squared"], b * (2 * TPB) + (which + 1) * TPB)
                dve.wait_ge(S["powered"], b * 2 + which)
                dve.tensor_scalar(var[:], sumsq[:], 1.0 / D_MODEL, EPS, ALU.mult, ALU.add).then_inc(S["var_ready"], 1)
                dve.wait_ge(S["powered"], b * 2 + (which + 1))

            split_lo(0, 0)
            dve.sem_inc(S["producted"], 1)
            with dve.Fori(0, BLOCKS) as b:
                for k in range(KC):
                    dve.wait_ge(S["mix_hi"], b * KC + (k + 1))
                    dve.tensor_tensor(turned_lo[:, k, :], bank[k][:], turned_hi[:, k, :].bitcast(F32),
                                      ALU.subtract).then_inc(S["mix_lo"], 1)
                for j in range(OUT_ITEMS):
                    split_lo((j + 1) % 2, b * ITEMS + (j + 1))
                    if j == OUT_ITEMS // 2 - 1:
                        dve.wait_ge(S["x_loaded"], b * 16 + 16)
                        dve.wait_ge(S["stored"], b * (16 * TPB))
                    if j == OUT_ITEMS // 2:
                        add_half(b, OUT_ITEMS // 2 - 1, 0, 0, "x1_half", x_in)
                add_half(b, OUT_ITEMS - 1, 1, 4, "x1_half", x_in)
                variance(b, 0)
                for t in range(TPB):
                    dve.tensor_scalar(natural[:, t, :], x_sum[:, t, :], rstd[:, t:t + 1], None, ALU.mult)\
                       .then_inc(S["scaled"], 1)
                for k in range(KC):
                    dve.wait_ge(S["h2_hi"], b * KC + (k + 1))
                    dve.scalar_tensor_tensor(out=turned_lo[:, k, :], in0=bank[k][:], scalar=g_ffn[:, k:k + 1],
                                             in1=turned_hi[:, k, :].bitcast(F32), op0=ALU.mult,
                                             op1=ALU.subtract).then_inc(S["h2_lo"], 1)
                with dve.Fori(0, FT // 2) as pair:
                    for e in range(2):
                        item = b * ITEMS + pair * 4 + (GATE_ITEM + 2 * e)
                        f = b * FT + pair * 2 + e
                        split_lo(1, item + 1)
                        split_lo(0, item + 2)
                        dve.wait_ge(S["multiplied"], item + 3)
                        dve.wait_ge(S["silued"], f + 1 + 1)
                        dve.tensor_tensor(gated[:, e, :], bank[2 * e + 1][:], gated[:, e, :], ALU.mult)\
                           .then_inc(S["producted"], 1)
                        dve.wait_ge(S["act_hi"], f + 1)
                        here = (slice(None), ds(pair * 2 + e, 1), slice(None))
                        flat = lambda t: t.rearrange("p o n -> p (o n)")
                        dve.tensor_tensor(flat(act_lo[here]), gated[:, e, :], flat(act_hi[here]).bitcast(F32),
                                          ALU.subtract).then_inc(S["act_lo"], 1)
                for j in range(DOWN_ITEM, ITEMS):
                    split_lo((j + 1) % 2, b * ITEMS + (j + 1))
                    if j == DOWN_ITEM + FT // 2:
                        add_half(b, DOWN_ITEM + FT // 2 - 1, 0, 4, "x2_half", x_sum)
                add_half(b, ITEMS - 1, 1, 0, "x2_half", x_sum)
                variance(b, 1)
                for t in range(TPB):
                    dve.scalar_tensor_tensor(out=x_sum[:, t, :], in0=x_sum[:, t, :], scalar=rstd[:, t:t + 1],
                                             in1=g_final[:], op0=ALU.mult, op1=ALU.mult).then_inc(S["final"], 1)

        @block.tensor
        def _(pe):
            def passes(s, chunk, left_hi, left_lo, outs, start, stop):
                cols = slice(chunk * HALF, (chunk + 1) * HALF)
                for t in range(TPB):
                    tok = slice(t * P, (t + 1) * P)
                    for n, (a, w) in enumerate(((left_hi, w_hi), (left_lo, w_hi), (left_hi, w_lo))):
                        mm = pe.matmul(bank[outs + t][:], a[:, tok], w[s][:, cols],
                                       start=(start and n == 0), stop=(stop and n == 2))
                return mm

            pe.sem_inc(S["multiplied"], 1)
            pe.sem_inc(S["silued"], 1)
            with pe.Fori(0, BLOCKS) as b:
                pe.wait_ge(S["mix_loaded"], b * 16 + 16)
                pe.wait_ge(S["x2_half"], b * (2 * TPB))
                for k in range(KC):
                    for t in range(TPB):
                        mm = pe.transpose(bank[k][:, t * P:(t + 1) * P], natural[:, t, k * P:(k + 1) * P], ident[:])
                    mm.then_inc(S["mix_turned"], 1)
                for j in range(OUT_ITEMS):
                    pe.wait_ge(S["lo_split"], b * ITEMS + (j + 1))
                    if j in (0, 2):
                        pe.wait_ge(S["mix_lo"], b * KC + 4 * (j // 2 + 1))
                    half, first = divmod(j, OUT_ITEMS // 2)
                    for n in range(2):
                        c = 2 * first + n
                        mm = passes(j % 2, n, turned_hi[:, c, :], turned_lo[:, c, :], 4 * half, c == 0, c == KC - 1)
                    mm.then_inc(S["multiplied"], 1)
                for t in range(TPB):
                    pe.wait_ge(S["scaled"], b * TPB + (t + 1))
                    for k in range(KC):
                        mm = pe.transpose(bank[k][:, t * P:(t + 1) * P], natural[:, t, k * P:(k + 1) * P], ident[:])
                        if t == TPB - 1:
                            mm.then_inc(S["h2_turned"], 1)
                with pe.Fori(0, FT // 2) as pair:
                    for e in range(2):
                        f = b * FT + pair * 2 + e
                        for n in range(2):
                            pe.wait_ge(S["lo_split"], b * ITEMS + pair * 4 + (GATE_ITEM + 2 * e + n + 1))
                            pe.wait_ge(S["producted" if n else "silued"], f)
                            for c in range(KC):
                                if e == 0 and n == 0:
                                    pe.wait_ge(S["h2_lo"], b * KC + (c + 1))
                                w = slice(c * P, (c + 1) * P)
                                for m, (a, h) in enumerate(((w_hi, turned_hi), (w_lo, turned_hi), (w_hi, turned_lo))):
                                    mm = pe.matmul(bank[2 * e + n][:], a[n][:, w], h[:, c, :],
                                                   start=(c == 0 and m == 0), stop=(c == KC - 1 and m == 2))
                            mm.then_inc(S["multiplied"], 1)
                for j in range(DOWN_ITEM, ITEMS):
                    pe.wait_ge(S["lo_split"], b * ITEMS + (j + 1))
                    half, first = divmod(j - DOWN_ITEM, FT // 2)
                    if half == 0:
                        pe.wait_ge(S["act_lo"], b * FT + (2 * first + 2))
                    for n in range(2):
                        f = 2 * first + n
                        mm = passes(j % 2, n, act_hi[:, f, :], act_lo[:, f, :], 4 * (1 - half), f == 0, f == FT - 1)
                    mm.then_inc(S["multiplied"], 1)



def build_program(nc, D, out):
    qk_scratch = nc.dram_tensor("qk_scratch", [2, len(QK_ORDER) * GROUP, SEQ], F32).ap()
    v_scratch = nc.dram_tensor("v_scratch", [2, SEQ, GROUP], F32).ap()
    mix_scratch = nc.dram_tensor("mix_scratch", [SEQ, D_MODEL], F32).ap()
    ctx = ExitStack()
    with ctx:
        sb = lambda n, s, d=F32: ctx.enter_context(nc.sbuf_tensor(n, s, d))
        ident = sb("ident_sb", [P, P])
        loaded, cast = ctx.enter_context(nc.semaphore("m_loaded")), ctx.enter_context(nc.semaphore("m_cast"))
        with nc.sbuf_tensor("hT_hi", [P, KC, SEQ], F32R) as hT_hi, nc.sbuf_tensor("hT_lo", [P, KC, SEQ], F32R) as hT_lo:
            with nc.Block() as block:
                @block.sync
                def _(sp):
                    sp.dma_start(ident[:], D["ident"]).then_inc(loaded, 16)
                    sp.wait_ge(loaded, 16)
            phase_norm(nc, D["x"], D["g_attn"][0].partition_broadcast(P), ident, hT_hi, hT_lo)
            phase_qk(nc, D["w_qk"], D["positions"], D["inv_freq"], D["rotary"], hT_hi, hT_lo, qk_scratch)
            phase_v(nc, D["w_v"], hT_hi, hT_lo, v_scratch)
        with ExitStack() as masks:
            small = lambda n, d: masks.enter_context(nc.sbuf_tensor(n, [P, P], d))
            ident_bf, raw = small("ident_bf", BF16), small("mask_raw", F32)
            strict, causal = small("strict", F32), small("causal", BF16)
            with nc.Block() as block:
                @block.sync
                def _(sp):
                    sp.dma_start(raw[:], D["causal_mask"]).then_inc(loaded, 16)
                    sp.dma_start(strict[:], D["strict_mask"]).then_inc(loaded, 16)

                @block.vector
                def _(dve):
                    dve.wait_ge(loaded, 48)
                    dve.tensor_copy(ident_bf[:], ident[:]).then_inc(cast, 1)
                    dve.tensor_copy(causal[:], raw[:]).then_inc(cast, 1)
                    dve.wait_ge(cast, 2)
            phase_differential(nc, qk_scratch, v_scratch, D["lambdas"].partition_broadcast(P),
                               D["g_diff"][0].partition_broadcast(P), ident, ident_bf, causal, mix_scratch)
            phase_stick_breaking(nc, qk_scratch, v_scratch, D["g_stick"][0].partition_broadcast(P), ident,
                                 strict, mix_scratch)
        phase_ffn(nc, D["x"], mix_scratch, D["w_stream"], D["g_ffn"], D["g_final"][0].partition_broadcast(P),
                  ident, out)


def host_arrays(x, positions, norm_attn_g, w_in, lambda_q1, lambda_k1, lambda_q2, lambda_k2, diff_subln_g,
                sb_norm_g, w_out, norm_ffn_g, w_gate, w_up, w_down, final_norm_g):
    chunked = w_in[0].reshape(KC, P, -1)
    w_qk = np.stack([chunked[:, :, COL[kind] + f * P:COL[kind] + (f + 1) * P].transpose(1, 0, 2)
                     for kind in QK_ORDER for f in range(QK_TILES)])
    w_v = np.stack([chunked[:, :, COL[kind]:COL[kind] + GROUP] for kind in ("dv", "sv")])

    def natural(w):
        return w.reshape(-1, 2, P, 2, HALF).transpose(3, 0, 2, 1, 4).reshape(-1, P, D_MODEL)

    def by_tile(w):
        return w.reshape(KC, P, FT, P).transpose(2, 1, 0, 3).reshape(FT, P, D_MODEL)

    gate_up = np.stack([by_tile(w_gate[0]), by_tile(w_up[0])], 1).reshape(2 * FT, P, D_MODEL)
    items = [natural(w_out[0]), gate_up, natural(w_down[0])]
    w_stream = np.concatenate(items + [items[0][:2]])

    half = HEAD_DIM // 8
    inv_freq = np.zeros((P, 1), np.float32)
    rotary = np.zeros((P, P), np.float32)
    for first in range(0, P, HEAD_DIM):
        for i in range(half):
            inv_freq[first + i] = inv_freq[first + half + i] = np.float32(500000.0) ** np.float32(-i / half)
            rotary[first + half + i, first + i] = -1.0
            rotary[first + i, first + half + i] = 1.0
    row, col = np.arange(P)[:, None], np.arange(P)[None, :]
    return dict(
        x=x[0], positions=positions, g_attn=norm_attn_g, w_qk=w_qk, w_v=w_v, w_stream=w_stream,
        lambdas=np.concatenate([lambda_q1, lambda_k1, lambda_q2, lambda_k2]),
        g_diff=np.tile(diff_subln_g, (1, GROUP // (2 * HEAD_DIM))), g_stick=np.tile(sb_norm_g, (1, HEADS)),
        g_ffn=norm_ffn_g.reshape(KC, P).transpose(1, 0), g_final=final_norm_g.reshape(1, D_MODEL),
        inv_freq=inv_freq, rotary=rotary, ident=np.eye(P, dtype=np.float32),
        causal_mask=np.where(col > row, -1e30, 0.0).astype(np.float32),
        strict_mask=np.where(col >= row, -1e30, 0.0).astype(np.float32))


def kernel(**inputs):
    from concourse import bacc
    from concourse.bass_utils import run_bass_kernel_spmd

    arrays = {n: np.ascontiguousarray(a) for n, a in host_arrays(**{k: np.asarray(v) for k, v in inputs.items()}).items()}
    nc = bacc.Bacc("TRN2", target_bir_lowering=False, num_devices=1)
    dram = {n: nc.dram_tensor("in_" + n, a.shape, mybir.dt.from_np(a.dtype), kind="ExternalInput").ap() for n, a in arrays.items()}
    out = nc.dram_tensor("out", [SEQ, D_MODEL], F32, kind="ExternalOutput").ap()
    build_program(nc, dram, out)
    result = run_bass_kernel_spmd(nc, [{"in_" + n: a for n, a in arrays.items()}], core_ids=[0])
    return result.results[0]["out"].reshape(1, SEQ, D_MODEL)
```

```python
import math
from contextlib import ExitStack

import numpy as np
import concourse.bass as bass
from concourse import mybir

F32 = mybir.dt.float32
F32R = mybir.dt.float32r
BF16 = mybir.dt.bfloat16
I32 = mybir.dt.int32
ALU = mybir.AluOpType
ACT = mybir.ActivationFunctionType
AX = mybir.AxisListType
ds = bass.ds

P = 128
SEQ = 2048
D_MODEL = 1024
HEAD_DIM = 64
D_FF = 2816
EPS = 1e-5
KC = D_MODEL // P
TOK_TILES = SEQ // P
BLK = 512
BLOCKS = SEQ // BLK
TPB = BLK // P
GROUP = 512
HEADS = GROUP // HEAD_DIM
QK_TILES = GROUP // P
COL = {"dq": 0, "dk": 512, "dv": 1024, "sq": 1536, "sk": 2048, "sv": 2560}
SCALE = HEAD_DIM ** -0.5
LAMBDA_INIT = 0.8 - 0.6 * math.exp(-0.3 * 0)


MAGIC = 1.5 * 2 ** 23


def two_pi_parts():
    first = 6.28125
    second = math.floor((2 * math.pi - first) * 2 ** 19) / 2 ** 19
    return first, second, 2 * math.pi - first - second


TWO_PI = two_pi_parts()


def link(eng, sem, value, instruction):
    instruction.then_inc(sem, 1)
    eng.wait_ge(sem, value)


def phase_norm(nc, x, g_row_dram, ident, hT_hi, hT_lo, w_first, w_first_dram, w_first_loaded):
    ctx = ExitStack()
    with ctx:
        sb = lambda n, s, d=F32: ctx.enter_context(nc.sbuf_tensor(n, s, d))
        sem = lambda n: ctx.enter_context(nc.semaphore(n))
        xt = sb("a_x", [P, TOK_TILES, D_MODEL])
        g_row = sb("a_g", [P, D_MODEL])
        junk = sb("a_junk", [P, D_MODEL])
        sumsq = sb("a_sumsq", [P, TOK_TILES])
        var = sb("a_var", [P, TOK_TILES])
        lnv = sb("a_lnv", [P, TOK_TILES])
        y0 = sb("a_y0", [P, TOK_TILES])
        nt = sb("a_newton", [P, TOK_TILES])
        rstd = sb("a_rstd", [P, TOK_TILES])
        bank = [ctx.enter_context(nc.psum_tensor(f"a_ps{i}", [P, 512], F32)) for i in range(8)]
        x_loaded = [sem(f"a_x_loaded{g}") for g in range(BLOCKS)]
        g_loaded = sem("a_g_loaded")
        squared, var_ready, ln_ready, y0_ready = sem("a_squared"), sem("a_var"), sem("a_ln"), sem("a_y0")
        dve_chain, scaled, turned = sem("a_dve"), sem("a_scaled"), sem("a_turned")
        hi_ready, lo_ready, act_chain = sem("a_hi"), sem("a_lo"), sem("a_act")
        xs = x.rearrange("(g t p) n -> g p t n", t=TPB, p=P)
        block = ctx.enter_context(nc.Block())

        @block.sync
        def _(sp):
            for g in range(BLOCKS):
                sp.dma_start(xt[:, g * TPB:(g + 1) * TPB, :], xs[g]).then_inc(x_loaded[g], 16)
                if g == 0:
                    sp.dma_start(g_row[:], g_row_dram).then_inc(g_loaded, 16)
            sp.dma_start(w_first[:], w_first_dram).then_inc(w_first_loaded, 16)

        @block.scalar
        def _(act):
            def stats(g):
                act.wait_ge(x_loaded[g], 16)
                for t in range(g * TPB, (g + 1) * TPB):
                    if t:
                        act.wait_ge(squared, t)
                    act.activation(junk[:], xt[:, t, :], ACT.Square,
                                   accum_out=sumsq[:, t:t + 1]).then_inc(squared, 1)
                own = slice(g * TPB, (g + 1) * TPB)
                act.wait_ge(var_ready, g + 1)
                act.activation(lnv[:, own], var[:, own], ACT.Ln).then_inc(ln_ready, 1)
                act.wait_ge(ln_ready, g + 1)
                act.activation(y0[:, own], lnv[:, own], ACT.Exp, scale=-0.5).then_inc(y0_ready, 1)

            stats(0)
            for g in range(BLOCKS):
                if g + 1 < BLOCKS:
                    stats(g + 1)
                for u in range(2 * TPB):
                    t, half = g * TPB + u // 2, u % 2
                    act.wait_ge(turned, 2 * t + half + 1)
                    act.activation(hT_hi[:, 4 * half:4 * half + 4, t * P:(t + 1) * P],
                                   bank[u][:].rearrange("p (k t) -> p k t", k=4), ACT.Copy)\
                       .then_inc(hi_ready, 1)

        @block.vector
        def _(dve):
            n = [0]

            def chain(instruction):
                n[0] += 1
                link(dve, dve_chain, n[0], instruction)

            def scale_rows(g):
                own = slice(g * TPB, (g + 1) * TPB)
                dve.wait_ge(squared, (g + 1) * TPB)
                dve.tensor_scalar(var[:, own], sumsq[:, own], 1.0 / D_MODEL, EPS, ALU.mult, ALU.add)\
                   .then_inc(var_ready, 1)
                dve.wait_ge(y0_ready, g + 1)
                chain(dve.tensor_tensor(nt[:, own], y0[:, own], y0[:, own], ALU.mult))
                chain(dve.tensor_tensor(nt[:, own], nt[:, own], var[:, own], ALU.mult))
                chain(dve.tensor_scalar(nt[:, own], nt[:, own], -0.5, 1.5, ALU.mult, ALU.add))
                chain(dve.tensor_tensor(rstd[:, own], nt[:, own], y0[:, own], ALU.mult))
                if g == 0:
                    dve.wait_ge(g_loaded, 16)
                for t in range(g * TPB, (g + 1) * TPB):
                    dve.scalar_tensor_tensor(out=xt[:, t, :], in0=xt[:, t, :], scalar=rstd[:, t:t + 1],
                                             in1=g_row[:], op0=ALU.mult, op1=ALU.mult).then_inc(scaled, 1)

            scale_rows(0)
            for g in range(BLOCKS):
                if g + 1 < BLOCKS:
                    scale_rows(g + 1)
                for u in range(2 * TPB):
                    t, half = g * TPB + u // 2, u % 2
                    dst = (slice(None), slice(4 * half, 4 * half + 4), slice(t * P, (t + 1) * P))
                    dve.wait_ge(hi_ready, 2 * t + half + 1)
                    dve.tensor_tensor(hT_lo[dst], bank[u][:].rearrange("p (k t) -> p k t", k=4),
                                      hT_hi[dst].bitcast(F32), ALU.subtract).then_inc(lo_ready, 1)

        @block.tensor
        def _(pe):
            for t in range(TOK_TILES):
                pe.wait_ge(scaled, t + 1)
                for half in range(2):
                    u = (2 * t + half) % 8
                    if 2 * t + half >= 8:
                        pe.wait_ge(lo_ready, 2 * t + half - 7)
                    for k in range(4):
                        c = 4 * half + k
                        mm = pe.transpose(bank[u][:, k * P:(k + 1) * P], xt[:, t, c * P:(c + 1) * P], ident[:])
                    mm.then_inc(turned, 1)


QK_ORDER = ["sq", "sk", "dq", "dk"]
PAIRS = QK_TILES // 2
ALL_PAIRS = len(QK_ORDER) * PAIRS


def phase_qk(nc, w_qk, positions, invf_dram, perm_dram, hT_hi, hT_lo, qk_scratch, w_first, w_first_loaded,
             w_v, v_raw, v_loaded):
    ctx = ExitStack()
    with ctx:
        sb = lambda n, s, d=F32: ctx.enter_context(nc.sbuf_tensor(n, s, d))
        sem = lambda n: ctx.enter_context(nc.semaphore(n))
        w_raw = [w_first, sb("b_wraw1", [P, KC, P])]
        w_hi = [sb(f"b_whi{s}", [P, KC, P], F32R) for s in range(2)]
        w_lo = [sb(f"b_wlo{s}", [P, KC, P], F32R) for s in range(2)]
        out_hi = sb("b_ohi", [P, BLOCKS, BLK], F32R)
        out_lo = sb("b_olo", [P, BLOCKS, BLK], F32R)
        cosT, sinT = sb("b_cos", [P, SEQ]), sb("b_sin", [P, SEQ])
        raw_qk, turned = sb("b_rawqk", [P, 2, BLK]), sb("b_turned", [P, 2, BLK])
        turns, part = sb("b_turns", [P, SEQ // 2]), sb("b_part", [P, SEQ // 2])
        invf, perm = sb("b_invf", [P, 1]), sb("b_perm", [P, P])
        bank = [ctx.enter_context(nc.psum_tensor(f"b_ps{i}", [P, BLK], F32)) for i in range(BLOCKS)]
        rot_bank = [ctx.enter_context(nc.psum_tensor(f"b_rot{i}", [P, BLK], F32)) for i in range(2)]
        w_loaded = [w_first_loaded, sem("b_w_loaded1")]
        hi_split, lo_split = sem("b_hi_split"), sem("b_lo_split")
        projected = sem("b_projected")
        hi_out = sem("b_hi_out")
        unit_done = sem("b_unit_done")
        raw_copied, rotated, summed = sem("b_raw"), sem("b_rotated"), sem("b_summed")
        dve_chain, pool_chain = sem("b_dve"), sem("b_pool")
        stored = [sem(f"b_stored{b}") for b in range(BLOCKS)]
        consts, table_ready = sem("b_const"), sem("b_table")
        first_rot = 2 * QK_TILES * BLOCKS

        def kinds(eng, n, kind, body):
            if kind != QK_ORDER[-1]:
                with eng.Fori(0, PAIRS) as i:
                    for s in range(2):
                        pair = i + n * PAIRS
                        body(pair * 2 + s, pair, s, kind, False)
            else:
                for i in range(PAIRS):
                    for s in range(2):
                        pair = n * PAIRS + i
                        body(2 * pair + s, pair, s, kind, 2 * i + s == QK_TILES - 1)

        block = ctx.enter_context(nc.Block())

        @block.sync
        def _(sp):
            def store(n, b):
                sp.wait_ge(unit_done, n * BLOCKS + (b + 5))
                for part_no, src in ((0, out_hi), (1, out_lo)):
                    sp.dma_start(qk_scratch[part_no, ds(n * P, P), b * BLK:(b + 1) * BLK],
                                 src[:, b, :].bitcast(F32)).then_inc(stored[b], 16)

            sp.dma_start(w_raw[1][:], w_qk[1]).then_inc(w_loaded[1], 16)
            sp.dma_start(cosT[:].bitcast(I32), positions[0, :].partition_broadcast(P)).then_inc(consts, 16)
            sp.dma_start(invf[:], invf_dram).then_inc(consts, 16)
            sp.dma_start(perm[:], perm_dram).then_inc(consts, 16)
            for n, slot in enumerate(v_raw):
                sp.dma_start(slot[:], w_v[n // KC, n % KC]).then_inc(v_loaded[n], 16)
            with sp.Fori(0, ALL_PAIRS - 1) as pair:
                for s in range(2):
                    n = pair * 2 + s
                    sp.wait_ge(lo_split, n + 1)
                    sp.dma_start(w_raw[s][:], w_qk[ds(n + 2, 1)].rearrange("o p c n -> (o p) c n"))\
                      .then_inc(w_loaded[s], 16)
                    for b in range(BLOCKS):
                        store(n, b)
            for n in (2 * ALL_PAIRS - 2, 2 * ALL_PAIRS - 1):
                for b in range(BLOCKS):
                    store(n, b)
            for b in range(BLOCKS):
                sp.wait_ge(stored[b], (2 * ALL_PAIRS + 1) * 32)

        @block.gpsimd
        def _(pool):
            pool.wait_ge(consts, 48)
            step = [0]

            def chain(instruction):
                step[0] += 1
                link(pool, pool_chain, step[0], instruction)

            for cols in (slice(0, SEQ // 2), slice(SEQ // 2, SEQ)):
                cos, sin = cosT[:, cols], sinT[:, cols]
                chain(pool.tensor_copy(cos, cos.bitcast(I32)))
                chain(pool.tensor_scalar(cos, cos, invf[:, 0:1], 1.0, ALU.mult, ALU.mult))
                for table, quarter in ((sin, 0.0), (cos, 0.25)):
                    chain(pool.tensor_scalar(turns[:], cos, 1.0 / (2 * math.pi), quarter, ALU.mult, ALU.add))
                    chain(pool.tensor_scalar(turns[:], turns[:], MAGIC, -MAGIC, ALU.add, ALU.add))
                    chain(pool.tensor_scalar(part[:], turns[:], -TWO_PI[0], 1.0, ALU.mult, ALU.mult))
                    chain(pool.tensor_tensor(table, cos, part[:], ALU.add))
                    chain(pool.tensor_scalar(part[:], turns[:], -TWO_PI[1], 1.0, ALU.mult, ALU.mult))
                    chain(pool.tensor_tensor(table, table, part[:], ALU.add))
                    chain(pool.tensor_scalar(part[:], turns[:], -TWO_PI[2], quarter * 2 * math.pi,
                                             ALU.mult, ALU.add))
                    chain(pool.tensor_tensor(table, table, part[:], ALU.add))
                    chain(pool.tensor_scalar(table, table, 3.1415925, -3.1415925, ALU.min, ALU.max))

        @block.scalar
        def _(act):
            def split_hi(pair, s, tiles_done):
                act.wait_ge(w_loaded[s], pair * 16 + 16)
                act.wait_ge(projected, tiles_done * BLOCKS + 1)
                act.activation(w_hi[s][:], w_raw[s][:], ACT.Copy).then_inc(hi_split, 1)

            def evac(n, pair, s, kind, last):
                scale = SCALE if kind[1] == "q" else 1.0
                for b in range(BLOCKS):
                    if b == 1 and not last:
                        split_hi(pair + s, 1 - s, n)
                    act.wait_ge(projected, n * BLOCKS + (b + 2))
                    if kind[0] == "s":
                        act.wait_ge(stored[b], n * 32 + 32)
                        act.activation(out_hi[:, b, :], bank[b][:], ACT.Copy, scale=scale).then_inc(hi_out, 1)
                    else:
                        act.activation(raw_qk[:, b % 2, :], bank[b][:], ACT.Copy, scale=scale)\
                           .then_inc(raw_copied, 1)
                        act.wait_ge(summed, n * BLOCKS + (b + 1 - first_rot))
                        act.wait_ge(stored[b], n * 32 + 32)
                        act.activation(out_hi[:, b, :], turned[:, b % 2, :], ACT.Copy).then_inc(hi_out, 1)

            for b in range(BLOCKS):
                act.sem_inc(stored[b], 32)
            for n, kind in enumerate(QK_ORDER):
                if n == 0:
                    split_hi(0, 0, 0)
                if kind == "dq":
                    act.wait_ge(pool_chain, 20 * 2)
                    act.activation(sinT[:], sinT[:], ACT.Sin).then_inc(table_ready, 1)
                    act.activation(cosT[:], cosT[:], ACT.Sin).then_inc(table_ready, 1)
                kinds(act, n, kind, evac)

        @block.vector
        def _(dve):
            def split_lo(n, s):
                dve.wait_ge(hi_split, n + 1)
                dve.tensor_tensor(w_lo[s][:], w_raw[s][:], w_hi[s][:].bitcast(F32), ALU.subtract)\
                   .then_inc(lo_split, 1)

            def evac(n, pair, s, kind, last):
                scale = SCALE if kind[1] == "q" else 1.0
                for b in range(BLOCKS):
                    if b == 1 and not last:
                        split_lo(n + 1, 1 - s)
                    hi = out_hi[:, b, :].bitcast(F32)
                    if kind[0] == "s":
                        dve.wait_ge(stored[b], n * 32 + 32)
                        dve.wait_ge(hi_out, n * BLOCKS + (b + 1))
                        dve.scalar_tensor_tensor(out=out_lo[:, b, :], in0=bank[b][:], scalar=scale, in1=hi,
                                                 op0=ALU.mult, op1=ALU.subtract).then_inc(unit_done, 1)
                    else:
                        rot = n * BLOCKS + (b - first_rot)
                        sin, cos = sinT[:, b * BLK:(b + 1) * BLK], cosT[:, b * BLK:(b + 1) * BLK]
                        slot = (slice(None), b % 2, slice(None))
                        dve.wait_ge(rotated, rot + 1)
                        link(dve, dve_chain, rot * 2 + 1,
                             dve.tensor_tensor(turned[slot], rot_bank[b % 2][:], sin, ALU.mult))
                        link(dve, dve_chain, rot * 2 + 2,
                             dve.tensor_tensor(raw_qk[slot], raw_qk[slot], cos, ALU.mult))
                        dve.tensor_tensor(turned[slot], turned[slot], raw_qk[slot], ALU.add).then_inc(summed, 1)
                        dve.wait_ge(summed, rot + 1)
                        dve.wait_ge(stored[b], n * 32 + 32)
                        dve.wait_ge(hi_out, n * BLOCKS + (b + 1))
                        dve.tensor_tensor(out_lo[:, b, :], turned[slot], hi, ALU.subtract).then_inc(unit_done, 1)

            dve.sem_inc(unit_done, BLOCKS)
            for n, kind in enumerate(QK_ORDER):
                if n == 0:
                    split_lo(0, 0)
                if kind == "dq":
                    dve.wait_ge(table_ready, 2)
                kinds(dve, n, kind, evac)

        @block.tensor
        def _(pe):
            def rotate(n, b):
                rot = n * BLOCKS + (b - first_rot)
                pe.wait_ge(raw_copied, rot + 1)
                pe.matmul(rot_bank[b % 2][:], perm[:], raw_qk[:, b % 2, :], start=True, stop=True)\
                  .then_inc(rotated, 1)

            def project(n, pair, s, kind, last):
                pe.wait_ge(lo_split, n + 1)
                for b in range(BLOCKS):
                    pe.wait_ge(unit_done, n * BLOCKS + (b + 1))
                    cols = slice(b * BLK, (b + 1) * BLK)
                    for c in range(KC):
                        for w, h in ((w_hi, hT_hi), (w_lo, hT_hi), (w_hi, hT_lo)):
                            mm = pe.matmul(bank[b][:], w[s][:, c, :], h[:, c, cols],
                                           start=(c == 0 and w is w_hi and h is hT_hi),
                                           stop=(c == KC - 1 and h is hT_lo))
                        if c == 2 and b and kind[0] == "d":
                            rotate(n, b - 1)
                    mm.then_inc(projected, 1)
                if kind[0] == "d":
                    rotate(n, BLOCKS - 1)

            pe.sem_inc(projected, 1)
            for n, kind in enumerate(QK_ORDER):
                kinds(pe, n, kind, project)


V_AHEAD = 3
V_SLOTS = V_AHEAD + 2


def phase_v(nc, w_v, v_raw, v_loaded, w_first, hT_hi, hT_lo, v_scratch):
    ctx = ExitStack()
    with ctx:
        sb = lambda n, s, d=F32: ctx.enter_context(nc.sbuf_tensor(n, s, d))
        sem = lambda n: ctx.enter_context(nc.semaphore(n))
        halves = w_first[:].rearrange("p (s c) n -> p s (c n)", s=2)
        w_raw = [slot[:] for slot in v_raw] + [halves[:, s, :] for s in range(2)]
        w_hi, w_lo = sb("c_whi", [P, 2, KC, GROUP], F32R), sb("c_wlo", [P, 2, KC, GROUP], F32R)
        v_out = sb("c_out", [P, 2, GROUP])
        bank = [ctx.enter_context(nc.psum_tensor(f"c_ps{i}", [P, GROUP], F32)) for i in range(4)]
        w_loaded = v_loaded + [sem(f"c_w_loaded{s}") for s in range(V_AHEAD, V_SLOTS)]
        hi_split, lo_split = sem("c_hi_split"), sem("c_lo_split")
        projected, copied = sem("c_projected"), sem("c_copied")
        stored = [sem(f"c_stored{i}") for i in range(2)]
        block = ctx.enter_context(nc.Block())

        @block.sync
        def _(sp):
            for n in range(V_AHEAD, 2 * KC):
                if n >= V_SLOTS:
                    sp.wait_ge(lo_split, n - V_SLOTS + 1)
                sp.dma_start(w_raw[n % V_SLOTS], w_v[n // KC, n % KC]).then_inc(w_loaded[n % V_SLOTS], 16)
            with sp.Fori(0, 2) as group:
                for t in range(TOK_TILES):
                    sp.wait_ge(copied, group * TOK_TILES + (t + 5))
                    sp.dma_start(v_scratch[ds(group, 1), t * P:(t + 1) * P, :].rearrange("o p n -> (o p) n"),
                                 v_out[:, t % 2, :]).then_inc(stored[t % 2], 16)
            for i in range(2):
                sp.wait_ge(stored[i], 16 + 16 * 2 * TOK_TILES // 2)

        @block.vector
        def _(dve):
            for n in range(2 * KC):
                dve.wait_ge(hi_split, n + 1)
                dve.tensor_tensor(w_lo[:, n // KC, n % KC, :], w_raw[n % V_SLOTS],
                                  w_hi[:, n // KC, n % KC, :].bitcast(F32), ALU.subtract).then_inc(lo_split, 1)

        @block.scalar
        def _(act):
            act.sem_inc(copied, 4)
            for i in range(2):
                act.sem_inc(stored[i], 16)
            for n in range(2 * KC):
                act.wait_ge(w_loaded[n % V_SLOTS], 16 * (n // V_SLOTS + 1))
                act.activation(w_hi[:, n // KC, n % KC, :], w_raw[n % V_SLOTS], ACT.Copy).then_inc(hi_split, 1)
            with act.Fori(0, 2) as group:
                for t in range(TOK_TILES):
                    act.wait_ge(projected, group * TOK_TILES + (t + 1))
                    act.wait_ge(stored[t % 2], group * (16 * TOK_TILES // 2) + 16 * (t // 2 + 1))
                    act.activation(v_out[:, t % 2, :], bank[t % 4][:], ACT.Copy).then_inc(copied, 1)

        @block.tensor
        def _(pe):
            with pe.Fori(0, 2) as group:
                for t in range(TOK_TILES):
                    pe.wait_ge(copied, group * TOK_TILES + (t + 1))
                    for c in range(KC):
                        if t == 0:
                            pe.wait_ge(lo_split, group * KC + (c + 1))
                        for h, w in ((hT_hi, w_hi), (hT_lo, w_hi), (hT_hi, w_lo)):
                            mm = pe.matmul(bank[t % 4][:], h[:, c, t * P:(t + 1) * P],
                                           w[:, ds(group, 1), c, :].rearrange("p o n -> p (o n)"),
                                           start=(c == 0 and h is hT_hi and w is w_hi),
                                           stop=(c == KC - 1 and w is w_lo))
                    mm.then_inc(projected, 1)


CHUNK = 1024
CHUNK_TILES = CHUNK // P
KEY_PIECES = [0, 128, 384, 640, 1024, 1408, 2048]
PIECES = len(KEY_PIECES) - 1
PIECE_OF_TILE = [next(p for p in range(PIECES) if (i + 1) * P <= KEY_PIECES[p + 1]) for i in range(TOK_TILES)]


def chunks_of(i):
    first = i + 1 if i < CHUNK_TILES else (i + 1) // 2
    return [(0, first)] + ([(first, i + 1 - first)] if first <= i else [])


def load_keys_values(sp, k_st, v_sb, qk_scratch, v_scratch, k_row, group, kv_loaded, pieces):
    for piece in pieces:
        if piece:
            sp.wait_ge(kv_loaded[piece - 1], 48)
        a, b = KEY_PIECES[piece], KEY_PIECES[piece + 1]
        for part in range(2):
            sp.dma_start(k_st[part * HEAD_DIM:(part + 1) * HEAD_DIM, :, a:b].bitcast(F32),
                         qk_scratch[part, k_row:k_row + GROUP, a:b].rearrange("(h r) t -> r h t", r=HEAD_DIM))\
              .then_inc(kv_loaded[piece], 16)
        sp.dma_start(v_sb[:, a // P:b // P, :], v_scratch[group, a:b, :].rearrange("(k p) n -> p k n", p=P))\
          .then_inc(kv_loaded[piece], 16)


def load_query(sp, q_slot, qk_scratch, q_row, head, i, q_loaded):
    for half in range(2):
        sp.dma_start(q_slot[half * HEAD_DIM:(half + 1) * HEAD_DIM, :, :].bitcast(F32),
                     qk_scratch[:, ds(head * HEAD_DIM + q_row, HEAD_DIM), i * P:(i + 1) * P]
                     .rearrange("l r t -> r l t")).then_inc(q_loaded, 16)


def score_matmuls(pe, z, q_slot, k_st, head, key_tile, tiles, diagonal, ident_bf, mask_bf):
    for first in range(0, tiles, 4):
        n = min(4, tiles - first)
        cols = ds(head * SEQ + (key_tile + first) * P, n * P)
        keys = k_st[:].rearrange("p h t -> p (h t)")[:, cols]
        out = z[:, first * P:(first + n) * P]
        pe.matmul(out, q_slot[:, 0, :], keys, start=True, stop=False)
        if diagonal and first + n == tiles:
            pe.matmul(out[:, (n - 1) * P:n * P], ident_bf[:], mask_bf[:], start=False, stop=False)
        mm = pe.matmul(out, q_slot[:, 1, :], keys, start=False, stop=True)
    return mm


NORM_SEMS = ["o_copied", "squared", "summed", "pool_chain", "normed_ready", "g_loaded"]


def norm_tiles(pool, S, stored, heads_out, normed, squares, g_rep, sumsq, var, rstd, exponent, dim, factor,
               mix_scratch, mix_col):
    by_head = lambda t: t.rearrange("p (h d) -> p h d", d=dim)
    link(pool, S["pool_chain"], 1, pool.memset(exponent[:], -0.5))
    pool.wait_ge(S["g_loaded"], 16)
    link(pool, S["pool_chain"], 2, pool.tensor_scalar(g_rep[:], g_rep[:], factor, 1.0, ALU.mult, ALU.mult))
    n = 2
    for i in range(TOK_TILES):
        src, dst = heads_out[:, i % 2, :], normed[:, i % 2, :]
        pool.wait_ge(S["o_copied"], i + 1)
        if i >= 1:
            pool.wait_ge(S["summed"], i)
        pool.tensor_tensor(squares[:], src, src, ALU.mult).then_inc(S["squared"], 1)
        if i >= 2:
            pool.wait_ge(stored[i % 2], 16 * (i // 2))
        link(pool, S["pool_chain"], n + 1, pool.tensor_tensor(dst, src, g_rep[:], ALU.mult))
        pool.wait_ge(S["summed"], i + 1)
        link(pool, S["pool_chain"], n + 2,
             pool.tensor_scalar(var[:], sumsq[:], 1.0 / dim, EPS, ALU.mult, ALU.add))
        link(pool, S["pool_chain"], n + 3, pool.tensor_tensor(rstd[:], var[:], exponent[:], ALU.pow))
        n += 3
        pool.tensor_tensor(by_head(dst), by_head(dst), rstd[:].unsqueeze(2).to_broadcast([P, GROUP // dim, dim]),
                           ALU.mult).then_inc(S["normed_ready"], 1)
        pool.wait_ge(S["normed_ready"], i + 1)
        pool.dma_start(mix_scratch[i * P:(i + 1) * P, mix_col:mix_col + GROUP], dst).then_inc(stored[i % 2], 16)
    for s in range(2):
        pool.wait_ge(stored[s], 16 * (TOK_TILES // 2))


def sum_squares(dve, S, sumsq, squares, dim, i):
    dve.wait_ge(S["squared"], i + 1)
    if i >= 1:
        dve.wait_ge(S["normed_ready"], i)
    dve.tensor_reduce(sumsq[:], squares[:].rearrange("p (h d) -> p h d", d=dim), AX.X, ALU.add)\
       .then_inc(S["summed"], 1)


def copy_heads(act, S, heads_out, o_bank, applied, i):
    act.wait_ge(S["applied"], applied)
    if i >= 2:
        act.wait_ge(S["normed_ready"], i - 1)
    act.activation(heads_out[:, i % 2, :], o_bank[i % 2][:], ACT.Copy).then_inc(S["o_copied"], 1)


def phase_stick_breaking(nc, qk_scratch, v_scratch, g_rep_dram, ident, mask, mix_scratch, ffn_ahead, ffn_inputs):
    q_row, k_row = 0, GROUP
    dim = HEAD_DIM
    ctx = ExitStack()
    with ctx:
        sb = lambda n, s, d=F32: ctx.enter_context(nc.sbuf_tensor(n, s, d))
        sem = lambda n: ctx.enter_context(nc.semaphore(n))
        k_st = sb("e_k", [P, HEADS, SEQ], F32R)
        v_sb = sb("e_v", [P, TOK_TILES, GROUP])
        q_st = [sb(f"e_q{k}", [P, 2, P], F32R) for k in range(4)]
        work = [sb(f"e_work{s}", [P, CHUNK]) for s in range(2)]
        attn = [sb(f"e_attn{s}", [P, CHUNK]) for s in range(2)]
        attn_t = [sb(f"e_attn_t{s}", [P, CHUNK]) for s in range(2)]
        carry = sb("e_carry", [P, 1])
        heads_out, normed = sb("e_heads", [P, 2, GROUP]), sb("e_normed", [P, 2, GROUP])
        squares = sb("e_squares", [P, GROUP])
        g_rep = sb("e_g", [P, GROUP])
        sumsq, var, rstd, exponent = (sb(f"e_{n}", [P, HEADS]) for n in ("sumsq", "var", "rstd", "exponent"))
        z = [ctx.enter_context(nc.psum_tensor(f"e_z{s}", [P, CHUNK], F32)) for s in range(2)]
        t_bank = ctx.enter_context(nc.psum_tensor("e_t", [P, CHUNK], F32))
        o_bank = [ctx.enter_context(nc.psum_tensor(f"e_o{s}", [P, GROUP], F32)) for s in range(2)]
        kv_loaded = [sem(f"e_kv{p}") for p in range(PIECES)]
        q_loaded = [sem(f"e_q_loaded{k}") for k in range(4)]
        names = ["scored", "exped", "clipped_half", "clipped", "logged_half", "logged", "plused", "masked", "linked", "scanned", "attn_done",
                 "transposed", "evacuated", "applied", "var_ready", "powered"]
        S = {n: sem(f"e_{n}") for n in names + ["norm_chain", "o_copied", "normed_ready", "g_loaded", "pool_chain"]}
        stored = [sem(f"e_stored{s}") for s in range(2)]

        pairs_of = [HEADS // 2 * len(chunks_of(i)) for i in range(TOK_TILES)]
        first_step = [2 * sum(pairs_of[:i]) for i in range(TOK_TILES + 1)]

        split = first_step[CHUNK_TILES]

        FIRST_HALVED = 3
        halved_before = first_step[FIRST_HALVED]

        def step(i, pair, s, odd):
            chunks = chunks_of(i)
            two = len(chunks) == 2
            key_tile, tiles = chunks[1 - s] if two else chunks[0]
            return dict(i=i, s=s, odd=odd, q_slot=2 * odd + s, g=pair * 2 + (first_step[i] + s), pair=pair + first_step[i] // 2,
                        head=pair if two else pair * 2 + s, key_tile=key_tile, tiles=tiles, width=tiles * P,
                        diagonal=key_tile + tiles == i + 1,
                        peeled=isinstance(pair, int) and pair < 2,
                        half=tiles * P // 2 if i >= FIRST_HALVED else 0,
                        masks=(pair + (first_step[i] - split) // 2) + (split + 1) if two else
                        pair * 2 + (first_step[i] + s + 1), opens=not two or s == 0, closes=not two or s == 1,
                        first=(i == 0 and s == 0), two=two)

        def schedule(eng, body, tile_end):
            late = [None] * 4
            for i in range(TOK_TILES):
                loops = pairs_of[i] // 2 - 1
                for pair in range(2 if loops > 1 else pairs_of[i]):
                    for s in range(2):
                        now = step(i, pair, s, pair % 2)
                        body(now, *late)
                        late = [now] + late[:3]
                    if i and pair == 1:
                        tile_end(i - 1)
                if loops > 1:
                    with eng.Fori(1, loops + 1) as twice:
                        steps = [step(i, twice * 2 + k // 2, k % 2, k // 2 % 2) for k in range(-4, 4)]
                        for n in range(4):
                            body(*reversed(steps[n:n + 5]))
                    late = [step(i, pairs_of[i] + k // 2, k % 2, k // 2 % 2) for k in (-1, -2, -3, -4)]
            for n in range(4):
                body(*[None] * (n + 1), *late[:4 - n])
            tile_end(TOK_TILES - 1)

        block = ctx.enter_context(nc.Block())

        @block.sync
        def _(sp):
            def body(cur, prev, prev2, prev3, prev4):
                if cur is None:
                    return
                if prev4 is not None:
                    sp.wait_ge(S["scored"], cur["g"] - 3)
                load_query(sp, q_st[cur["q_slot"]], qk_scratch, q_row, cur["head"], cur["i"],
                           q_loaded[cur["q_slot"]])
                if cur["first"] and prev is None:
                    load_keys_values(sp, k_st, v_sb, qk_scratch, v_scratch, k_row, 1, kv_loaded, [0])
                    sp.dma_start(g_rep[:], g_rep_dram).then_inc(S["g_loaded"], 16)

            def tile_end(i):
                if i == TPB + 2:
                    for s in range(2):
                        sp.wait_ge(stored[s], 16 * (TPB // 2))
                    load_ahead(sp, ffn_ahead, *ffn_inputs)

            schedule(sp, body, tile_end)

        @block.tensor
        def _(pe):
            def body(cur, prev, prev2, prev3, prev4):
                if cur is not None:
                    if cur["s"] == 0 and (cur["i"] == 0 or PIECE_OF_TILE[cur["i"]] != PIECE_OF_TILE[cur["i"] - 1]) \
                            and (prev is None or prev["i"] != cur["i"]):
                        pe.wait_ge(kv_loaded[PIECE_OF_TILE[cur["i"]]], 48)
                    pe.wait_ge(q_loaded[cur["q_slot"]], cur["pair"] * 16 + (32 - 16 * cur["odd"]))
                    if prev2 is not None:
                        pe.wait_ge(S["scanned"], cur["g"] - 1)
                    score_matmuls(pe, z[cur["s"]], q_st[cur["q_slot"]], k_st, cur["head"], cur["key_tile"],
                                  cur["tiles"], False, None, None).then_inc(S["scored"], 1)
                if prev3 is not None:
                    pe.wait_ge(S["attn_done"], prev3["g"] + 1)
                    if prev4 is not None:
                        pe.wait_ge(S["evacuated"], prev3["g"])
                    for j in range(prev3["tiles"]):
                        mm = pe.transpose(t_bank[:, j * P:(j + 1) * P], attn[prev3["s"]][:, j * P:(j + 1) * P], ident[:])
                    mm.then_inc(S["transposed"], 1)
                if prev4 is not None:
                    o = o_bank[prev4["i"] % 2]
                    pe.wait_ge(S["evacuated"], prev4["g"] + 1)
                    if prev4["i"] >= 2 and prev4["s"] == 0:
                        pe.wait_ge(S["o_copied"], prev4["i"] - 1)
                    for j in range(prev4["tiles"]):
                        mm = pe.matmul(o[:, ds(prev4["head"] * dim, dim)], attn_t[prev4["s"]][:, j * P:(j + 1) * P],
                                       v_sb[:, prev4["key_tile"] + j, ds(prev4["head"] * dim, dim)],
                                       start=(prev4["opens"] and j == 0),
                                       stop=(prev4["closes"] and j == prev4["tiles"] - 1))
                    mm.then_inc(S["applied"], 1)

            schedule(pe, body, lambda i: None)

        @block.scalar
        def _(act):
            def body(cur, prev, prev2, prev3, prev4):
                if prev is not None:
                    w, h, t = prev["width"], prev["half"], work[prev["s"]]
                    if h:
                        act.wait_ge(S["clipped_half"], prev["g"] + 1 - halved_before)
                        act.activation(t[:, 0:h], t[:, 0:h], ACT.Ln, bias=1.0).then_inc(S["logged_half"], 1)
                    act.wait_ge(S["clipped"], prev["g"] + 1)
                    act.activation(t[:, h:w], t[:, h:w], ACT.Ln, bias=1.0).then_inc(S["logged"], 1)
                if prev2 is not None:
                    w, s = prev2["width"], prev2["s"]
                    act.wait_ge(S["scanned"], prev2["g"] + 1)
                    if prev4 is not None:
                        act.wait_ge(S["transposed"], prev2["g"] - 1)
                    act.activation(attn[s][:, 0:w], work[s][:, 0:w], ACT.Exp, scale=-1.0)\
                       .then_inc(S["attn_done"], 1)
                if cur is not None:
                    w, s = cur["width"], cur["s"]
                    act.wait_ge(S["scored"], cur["g"] + 1)
                    if prev2 is not None:
                        act.wait_ge(S["attn_done"], cur["g"] - 1)
                    act.activation(work[s][:, 0:w], z[s][:, 0:w], ACT.Exp, scale=-1.0).then_inc(S["exped"], 1)
                if prev3 is not None:
                    w, s = prev3["width"], prev3["s"]
                    act.wait_ge(S["transposed"], prev3["g"] + 1)
                    if not isinstance(prev3["g"], int) or prev3["g"] >= 2:
                        act.wait_ge(S["applied"], prev3["g"] - 1)
                    act.activation(attn_t[s][:, 0:w], t_bank[:, 0:w], ACT.Copy).then_inc(S["evacuated"], 1)

            def tile_end(i):
                copy_heads(act, S, heads_out, o_bank, first_step[i + 1], i)

            act.preload_act_table_set("natural_log_exp_and_others")
            schedule(act, body, tile_end)

        @block.vector
        def _(dve):
            by_head = lambda t: t.rearrange("p (h d) -> p h d", d=dim)

            def norm(i, stage):
                src, dst = heads_out[:, i % 2, :], normed[:, i % 2, :]
                chain = S["norm_chain"]
                if stage == 0:
                    dve.wait_ge(S["o_copied"], i + 1)
                    link(dve, chain, 4 * i + 1, dve.tensor_tensor(squares[:], src, src, ALU.mult))
                elif stage == 1:
                    link(dve, chain, 4 * i + 2, dve.tensor_reduce(sumsq[:], by_head(squares[:]), AX.X, ALU.add))
                    dve.tensor_scalar(var[:], sumsq[:], 1.0 / dim, EPS, ALU.mult, ALU.add)\
                       .then_inc(S["var_ready"], 1)
                elif stage == 2:
                    dve.wait_ge(S["powered"], i + 1)
                    link(dve, chain, 4 * i + 3,
                         dve.tensor_tensor(by_head(squares[:]), by_head(src),
                                           rstd[:].unsqueeze(2).to_broadcast([P, HEADS, dim]), ALU.mult))
                else:
                    if i == 0:
                        dve.wait_ge(S["g_loaded"], 16)
                    if i >= 2:
                        dve.wait_ge(stored[i % 2], 16 * (i // 2))
                    link(dve, chain, 4 * i + 4, dve.tensor_tensor(dst, squares[:], g_rep[:], ALU.mult))
                    dve.sem_inc(S["normed_ready"], 1)

            def body(cur, prev, prev2, prev3, prev4):
                if cur is None:
                    return
                s, w = cur["s"], cur["width"]
                t, scores = work[s], z[s]
                h = cur["half"]
                dve.wait_ge(S["exped"], cur["g"] + 1)
                if h:
                    dve.tensor_scalar(t[:, 0:h], t[:, 0:h], 2.0 ** 60, None, ALU.min).then_inc(S["clipped_half"], 1)
                dve.tensor_scalar(t[:, h:w], t[:, h:w], 2.0 ** 60, None, ALU.min).then_inc(S["clipped"], 1)
                if cur["diagonal"]:
                    own = scores[:, w - P:w]
                    link(dve, S["masked"], cur["masks"], dve.tensor_tensor(own, own, mask[:], ALU.add))
                def plus(cols):
                    return dve.scalar_tensor_tensor(out=t[:, cols], in0=scores[:, cols], scalar=-1.0, in1=t[:, cols],
                                                    op0=ALU.mult, op1=ALU.max)
                if h:
                    dve.wait_ge(S["logged_half"], cur["g"] + 1 - halved_before)
                    plus(slice(0, h))
                dve.wait_ge(S["logged"], cur["g"] + 1)
                plus(slice(h, w)).then_inc(S["plused"], 1)
                dve.wait_ge(S["plused"], cur["g"] + 1)
                links = (cur["pair"] - first_step[CHUNK_TILES] // 2) * 2
                last = t[:, w - 1:w]
                if cur["two"] and s == 1:
                    dve.wait_ge(S["scanned"], cur["g"])
                    link(dve, S["linked"], links + 2, dve.tensor_tensor(last, last, carry[:], ALU.add))
                back = t[:, 0:w - 1][:, ::-1]
                scan = dve.tensor_tensor_scan(back, scores[:, 1:w][:, ::-1], back, last, ALU.add, ALU.add)
                if cur["two"] and s == 0:
                    link(dve, S["linked"], links + 1, scan)
                    dve.tensor_tensor(carry[:], scores[:, 0:1], t[:, 0:1], ALU.add).then_inc(S["scanned"], 1)
                else:
                    scan.then_inc(S["scanned"], 1)
                if cur["i"] >= 2 and cur["peeled"]:
                    norm(cur["i"] - 2, cur["g"] - first_step[cur["i"]])

            schedule(dve, body, lambda i: None)
            for i in (TOK_TILES - 2, TOK_TILES - 1):
                for stage in range(4):
                    norm(i, stage)

        @block.gpsimd
        def _(pool):
            load_keys_values(pool, k_st, v_sb, qk_scratch, v_scratch, k_row, 1, kv_loaded, range(1, PIECES))
            link(pool, S["pool_chain"], 1, pool.memset(exponent[:], -0.5))

            def power(i):
                pool.wait_ge(S["var_ready"], i + 1)
                pool.tensor_tensor(rstd[:], var[:], exponent[:], ALU.pow).then_inc(S["powered"], 1)

            for i in range(TOK_TILES):
                power(i)
                pool.wait_ge(S["normed_ready"], i + 1)
                pool.dma_start(mix_scratch[i * P:(i + 1) * P, GROUP:2 * GROUP], normed[:, i % 2, :])\
                    .then_inc(stored[i % 2], 16)
            for s in range(2):
                pool.wait_ge(stored[s], 16 * (TOK_TILES // 2))


def phase_differential(nc, qk_scratch, v_scratch, lambdas_dram, g_rep_dram, ident, ident_bf, mask_bf, mix_scratch):
    q_row, k_row = 2 * GROUP, 3 * GROUP
    dim = 2 * HEAD_DIM
    ctx = ExitStack()
    with ctx:
        sb = lambda n, s, d=F32: ctx.enter_context(nc.sbuf_tensor(n, s, d))
        sem = lambda n: ctx.enter_context(nc.semaphore(n))
        k_st = sb("d_k", [P, HEADS, SEQ], F32R)
        v_sb = sb("d_v", [P, TOK_TILES, GROUP])
        q_st = [sb(f"d_q{k}", [P, 2, P], F32R) for k in range(4)]
        probs = [sb(f"d_probs{k}", [P, CHUNK]) for k in range(4)]
        attn = [sb(f"d_attn{u}", [P, CHUNK]) for u in range(2)]
        attn_t = [sb(f"d_attn_t{u}", [P, CHUNK]) for u in range(2)]
        neg_max, row_sum = sb("d_negmax", [P, 4]), sb("d_sum", [P, 4])
        neg_all, shift, weight = sb("d_negall", [P, 2]), sb("d_shift", [P, 4]), sb("d_weight", [P, 4])
        total, inverse, factor = sb("d_total", [P, 4]), sb("d_inverse", [P, 4]), sb("d_factor", [P, 4])
        sign = sb("d_sign", [P, 4])
        lambdas, lam_prod = sb("d_lambdas", [P, 4, HEAD_DIM]), sb("d_lamprod", [P, 2, HEAD_DIM])
        lam_dot, lam_exp = sb("d_lamdot", [P, 2]), sb("d_lamexp", [P, 2])
        heads_out, normed = sb("d_heads", [P, 2, GROUP]), sb("d_normed", [P, 2, GROUP])
        squares, g_rep = sb("d_squares", [P, GROUP]), sb("d_g", [P, GROUP])
        sumsq, var, rstd, exponent = (sb(f"d_{n}", [P, GROUP // dim]) for n in ("sumsq", "var", "rstd", "exponent"))
        z = [ctx.enter_context(nc.psum_tensor(f"d_z{s}", [P, CHUNK], F32)) for s in range(2)]
        t_bank = ctx.enter_context(nc.psum_tensor("d_t", [P, CHUNK], F32))
        o_bank = [ctx.enter_context(nc.psum_tensor(f"d_o{s}", [P, GROUP], F32)) for s in range(2)]
        kv_loaded = [sem(f"d_kv{p}") for p in range(PIECES)]
        q_loaded = [sem(f"d_q_loaded{k}") for k in range(4)]
        names = ["scored", "maxed", "exped", "shifted", "weighed", "stats_chain", "combined",
                 "transposed", "evacuated", "applied", "lambda_loaded", "lambda_ready", "lambda_chain"]
        S = {n: sem(f"d_{n}") for n in names + NORM_SEMS}
        stored = [sem(f"d_stored{s}") for s in range(2)]

        two = [len(chunks_of(i)) == 2 for i in range(TOK_TILES)]
        quads_of = [4 if two[i] else 2 for i in range(TOK_TILES)]
        first_quad = [sum(quads_of[:i]) for i in range(TOK_TILES + 1)]
        stat_steps = [8 if two[i] else 4 for i in range(TOK_TILES)]
        first_stat = [sum(stat_steps[j] * quads_of[j] for j in range(i)) for i in range(TOK_TILES)]

        def quad(i, q):
            return dict(i=i, q=q, n=q + first_quad[i])

        def step(Q, k):
            i = Q["i"]
            key_tile, tiles = chunks_of(i)[k % 2] if two[i] else chunks_of(i)[0]
            return dict(i=i, s=k % 2, g=Q["n"] * 4 + k, map=Q["q"] * 2 + k // 2 if two[i] else Q["q"] * 4 + k,
                        key_tile=key_tile, tiles=tiles, width=tiles * P, diagonal=key_tile + tiles == i + 1)

        def unit(Q, u):
            i = Q["i"]
            key_tile, tiles = chunks_of(i)[u] if two[i] else chunks_of(i)[0]
            return dict(i=i, u=u, a=Q["n"] * 2 + u, head=Q["q"] if two[i] else Q["q"] * 2 + u,
                        key_tile=key_tile, tiles=tiles, width=tiles * P,
                        maps=(u, 2 + u) if two[i] else (2 * u, 2 * u + 1),
                        opens=not two[i] or u == 0, closes=not two[i] or u == 1)

        def schedule(eng, body, tile_end):
            late = [None, None]
            for i in range(TOK_TILES):
                for q in range(2):
                    now = quad(i, q)
                    body(now, *late)
                    late = [now, late[0]]
                if i:
                    tile_end(i - 1)
                if quads_of[i] > 2:
                    with eng.Fori(2, quads_of[i]) as q:
                        body(*[quad(i, q - k) for k in range(3)])
                    late = [quad(i, quads_of[i] - 1 - k) for k in range(2)]
            body(None, *late)
            body(None, None, late[0])
            tile_end(TOK_TILES - 1)

        block = ctx.enter_context(nc.Block())

        @block.sync
        def _(sp):
            def body(cur, prev, prev2):
                if cur is None:
                    return
                for k in range(4):
                    t = step(cur, k)
                    if prev is not None:
                        sp.wait_ge(S["scored"], t["g"] - 3)
                    load_query(sp, q_st[k], qk_scratch, q_row, t["map"], t["i"], q_loaded[k])
                    if prev is None and k == 0:
                        load_keys_values(sp, k_st, v_sb, qk_scratch, v_scratch, k_row, 0, kv_loaded, [0])
                        sp.dma_start(lambdas[:], lambdas_dram).then_inc(S["lambda_loaded"], 16)
                        sp.dma_start(g_rep[:], g_rep_dram).then_inc(S["g_loaded"], 16)

            schedule(sp, body, lambda i: None)

        @block.tensor
        def _(pe):
            def scores(cur, k):
                t = step(cur, k)
                pe.wait_ge(q_loaded[k], cur["n"] * 32 + 32)
                if not isinstance(t["g"], int) or t["g"] >= 2:
                    pe.wait_ge(S["exped"], t["g"] - 1)
                score_matmuls(pe, z[t["s"]], q_st[k], k_st, t["map"], t["key_tile"], t["tiles"],
                              t["diagonal"], ident_bf, mask_bf).then_inc(S["scored"], 1)

            def turn(prev, n):
                t = unit(prev, n)
                pe.wait_ge(S["combined"], t["a"] + 1)
                pe.wait_ge(S["evacuated"], t["a"])
                for j in range(t["tiles"]):
                    mm = pe.transpose(t_bank[:, j * P:(j + 1) * P], attn[n][:, j * P:(j + 1) * P], ident[:])
                mm.then_inc(S["transposed"], 1)

            def apply(prev, n):
                t = unit(prev, n)
                o = o_bank[t["i"] % 2]
                pe.wait_ge(S["evacuated"], t["a"] + 1)
                if t["i"] >= 2 and n == 0:
                    pe.wait_ge(S["o_copied"], t["i"] - 1)
                for j in range(t["tiles"]):
                    mm = pe.matmul(o[:, ds(t["head"] * dim, dim)], attn_t[n][:, j * P:(j + 1) * P],
                                   v_sb[:, t["key_tile"] + j, ds(t["head"] * dim, dim)],
                                   start=(t["opens"] and j == 0), stop=(t["closes"] and j == t["tiles"] - 1))
                mm.then_inc(S["applied"], 1)

            def body(cur, prev, prev2):
                if cur is not None:
                    piece = PIECE_OF_TILE[cur["i"]]
                    if prev is None or (prev["i"] != cur["i"] and piece != PIECE_OF_TILE[prev["i"]]):
                        pe.wait_ge(kv_loaded[piece], 48)
                    scores(cur, 0)
                    scores(cur, 1)
                if prev2 is not None:
                    apply(prev2, 0)
                if prev is not None:
                    turn(prev, 0)
                if cur is not None:
                    scores(cur, 2)
                if prev2 is not None:
                    apply(prev2, 1)
                if cur is not None:
                    scores(cur, 3)
                if prev is not None:
                    turn(prev, 1)

            schedule(pe, body, lambda i: None)

        @block.scalar
        def _(act):
            def exponentials(cur, prev, k):
                t = step(cur, k)
                act.wait_ge(S["maxed"], t["g"] + 1)
                if prev is not None:
                    user = next(u for u in range(2) if k in unit(prev, u)["maps"])
                    act.wait_ge(S["combined"], prev["n"] * 2 + (user + 1))
                act.activation(probs[k][:, 0:t["width"]], z[t["s"]][:, 0:t["width"]], ACT.Exp,
                               bias=neg_max[:, k:k + 1], accum_out=row_sum[:, k:k + 1]).then_inc(S["exped"], 1)

            def evacuate(prev, n):
                t = unit(prev, n)
                act.wait_ge(S["transposed"], t["a"] + 1)
                if not isinstance(t["a"], int) or t["a"] >= 2:
                    act.wait_ge(S["applied"], t["a"] - 1)
                act.activation(attn_t[n][:, 0:t["width"]], t_bank[:, 0:t["width"]], ACT.Copy)\
                   .then_inc(S["evacuated"], 1)

            def body(cur, prev, prev2):
                if prev is not None and two[prev["i"]]:
                    number = prev["n"] + 1 - first_quad[CHUNK_TILES]
                    act.wait_ge(S["shifted"], number)
                    act.activation(weight[:], shift[:], ACT.Exp).then_inc(S["weighed"], 1)
                if prev2 is not None:
                    evacuate(prev2, 1)
                if cur is not None:
                    exponentials(cur, prev, 0)
                if prev is not None:
                    evacuate(prev, 0)
                if cur is not None:
                    for k in (1, 2, 3):
                        exponentials(cur, prev, k)

            act.preload_act_table_set("natural_log_exp_and_others")
            act.wait_ge(S["lambda_ready"], 1)
            act.activation(lam_exp[:], lam_dot[:], ACT.Exp).then_inc(S["lambda_ready"], 1)
            schedule(act, body, lambda i: copy_heads(act, S, heads_out, o_bank, 2 * first_quad[i + 1], i))

        @block.vector
        def _(dve):
            def maximum(cur, k):
                t = step(cur, k)
                dve.wait_ge(S["scored"], t["g"] + 1)
                dve.tensor_reduce(neg_max[:, k:k + 1], z[t["s"]][:, 0:t["width"]], AX.X, ALU.max, negate=True)\
                   .then_inc(S["maxed"], 1)

            def factors(cur, prev):
                i = prev["i"]
                base = prev["q"] * stat_steps[i] + first_stat[i]
                if not two[i]:
                    if cur is not None:
                        maximum(cur, 0)
                    dve.wait_ge(S["exped"], prev["n"] * 4 + 4)
                    link(dve, S["stats_chain"], base + 1, dve.reciprocal(inverse[:], row_sum[:]))
                    link(dve, S["stats_chain"], base + 2,
                         dve.tensor_tensor(factor[:], inverse[:], sign[:], ALU.mult))
                    return base + 2
                by_map = lambda t: t[:].rearrange("p (m c) -> p m c", c=2)
                wide = lambda t: t[:, 0:2].unsqueeze(2).to_broadcast([P, 2, 2])
                number = prev["n"] + 1 - first_quad[CHUNK_TILES]
                dve.wait_ge(S["maxed"], prev["n"] * 4 + 4)
                link(dve, S["stats_chain"], base + 1,
                     dve.tensor_tensor(neg_all[:], neg_max[:, 0:4:2], neg_max[:, 1:4:2], ALU.min))
                dve.tensor_tensor(by_map(shift), wide(neg_all), by_map(neg_max), ALU.subtract)\
                   .then_inc(S["shifted"], 1)
                dve.wait_ge(S["shifted"], number)
                if cur is not None:
                    maximum(cur, 0)
                dve.wait_ge(S["exped"], prev["n"] * 4 + 4)
                dve.wait_ge(S["weighed"], number)
                link(dve, S["stats_chain"], base + 2, dve.tensor_tensor(total[:], row_sum[:], weight[:], ALU.mult))
                link(dve, S["stats_chain"], base + 3,
                     dve.tensor_tensor(inverse[:, 0:2], total[:, 0:4:2], total[:, 1:4:2], ALU.add))
                link(dve, S["stats_chain"], base + 4, dve.reciprocal(inverse[:, 2:4], inverse[:, 0:2]))
                link(dve, S["stats_chain"], base + 5,
                     dve.tensor_tensor(inverse[:, 0:2], inverse[:, 2:4], sign[:, 0:2], ALU.mult))
                link(dve, S["stats_chain"], base + 6,
                     dve.tensor_tensor(by_map(factor), by_map(weight), wide(inverse), ALU.mult))
                return base + 6

            def combine(prev, n, count):
                t = unit(prev, n)
                w, (one, other) = t["width"], t["maps"]
                link(dve, S["stats_chain"], count + 1 + n,
                     dve.tensor_scalar(probs[other][:, 0:w], probs[other][:, 0:w],
                                       factor[:, other:other + 1], None, ALU.mult))
                if not isinstance(t["a"], int) or t["a"] >= 2:
                    dve.wait_ge(S["transposed"], t["a"] - 1)
                dve.scalar_tensor_tensor(out=attn[n][:, 0:w], in0=probs[one][:, 0:w],
                                         scalar=factor[:, one:one + 1], in1=probs[other][:, 0:w],
                                         op0=ALU.mult, op1=ALU.add).then_inc(S["combined"], 1)

            def body(cur, prev, prev2):
                count = None
                if prev is not None:
                    count = factors(cur, prev)
                    combine(prev, 0, count)
                elif cur is not None:
                    maximum(cur, 0)
                if cur is not None:
                    maximum(cur, 1)
                if prev is not None:
                    combine(prev, 1, count)
                if cur is not None:
                    maximum(cur, 2)
                    maximum(cur, 3)
                    if prev is not None and prev["i"] != cur["i"] and cur["i"] >= 2:
                        sum_squares(dve, S, sumsq, squares, dim, cur["i"] - 2)

            dve.wait_ge(S["lambda_loaded"], 16)
            pairs = lambdas[:].rearrange("p (m s) d -> p m s d", s=2)
            n = S["lambda_chain"]
            link(dve, n, 1, dve.memset(sign[:], 1.0))
            link(dve, n, 2, dve.tensor_tensor(lam_prod[:], pairs[:, :, 0, :], pairs[:, :, 1, :], ALU.mult))
            dve.tensor_reduce(lam_dot[:], lam_prod[:], AX.X, ALU.add).then_inc(S["lambda_ready"], 1)
            dve.wait_ge(S["lambda_ready"], 2)
            link(dve, n, 3, dve.tensor_tensor(lam_dot[:, 0:1], lam_exp[:, 1:2], lam_exp[:, 0:1], ALU.subtract))
            for k in (1, 3):
                link(dve, n, 3 + (k + 1) // 2,
                     dve.tensor_scalar(sign[:, k:k + 1], lam_dot[:, 0:1], -LAMBDA_INIT, None, ALU.add))
            schedule(dve, body, lambda i: None)
            for i in (TOK_TILES - 2, TOK_TILES - 1):
                sum_squares(dve, S, sumsq, squares, dim, i)

        @block.gpsimd
        def _(pool):
            load_keys_values(pool, k_st, v_sb, qk_scratch, v_scratch, k_row, 0, kv_loaded, range(1, PIECES))
            norm_tiles(pool, S, stored, heads_out, normed, squares, g_rep, sumsq, var, rstd, exponent,
                       dim, 1.0 - LAMBDA_INIT, mix_scratch, 0)


FT = D_FF // P
OUT_ITEMS = 2 * KC // 2
GATE_ITEM = OUT_ITEMS
DOWN_ITEM = OUT_ITEMS + 2 * FT
ITEMS = DOWN_ITEM + 2 * FT // 2
HALF = D_MODEL // 2


def ahead_buffers(nc, ctx):
    sb = lambda n, s, d=F32: ctx.enter_context(nc.sbuf_tensor(n, s, d))
    F = dict(w_raw=[sb(f"f_wraw{s}", [P, D_MODEL]) for s in range(2)],
             natural=sb("f_natural", [P, TPB, D_MODEL]),
             x_in=sb("f_xin", [P, TPB, D_MODEL]), g_final=sb("f_gfinal", [P, D_MODEL]), g_ffn=sb("f_gffn", [P, KC]),
             w_loaded=[ctx.enter_context(nc.semaphore(f"f_w_loaded{s}")) for s in range(2)])
    F.update({n: ctx.enter_context(nc.semaphore("f_" + n)) for n in ("consts", "mix_loaded", "x_loaded")})
    return F


def by_block(dram):
    return dram.rearrange("(b t p) n -> b p t n", t=TPB, p=P)


def load_ahead(eng, F, x, mix_scratch, w_stream, g_ffn_dram, g_final_dram):
    for s in range(2):
        eng.dma_start(F["w_raw"][s][:], w_stream[s]).then_inc(F["w_loaded"][s], 16)
    eng.dma_start(F["natural"][:], by_block(mix_scratch)[0]).then_inc(F["mix_loaded"], 16)
    eng.dma_start(F["x_in"][:], by_block(x)[0]).then_inc(F["x_loaded"], 16)
    eng.dma_start(F["g_final"][:], g_final_dram).then_inc(F["consts"], 16)
    eng.dma_start(F["g_ffn"][:], g_ffn_dram).then_inc(F["consts"], 16)


def phase_ffn(nc, F, x, mix_scratch, w_stream, ident, out):
    assert ITEMS % 2 == 0 and FT % 2 == 0
    ctx = ExitStack()
    with ctx:
        sb = lambda n, s, d=F32: ctx.enter_context(nc.sbuf_tensor(n, s, d))
        sem = lambda n: ctx.enter_context(nc.semaphore(n))
        w_raw, natural, x_in, w_loaded = F["w_raw"], F["natural"], F["x_in"], F["w_loaded"]
        g_final, g_ffn = F["g_final"], F["g_ffn"]
        w_hi = [sb(f"f_whi{s}", [P, D_MODEL], F32R) for s in range(2)]
        w_lo = [sb(f"f_wlo{s}", [P, D_MODEL], F32R) for s in range(2)]
        turned_hi, turned_lo = sb("f_thi", [P, KC, BLK], F32R), sb("f_tlo", [P, KC, BLK], F32R)
        x_sum = sb("f_xsum", [P, TPB, D_MODEL])
        act_hi, act_lo = sb("f_ahi", [P, FT, BLK], F32R), sb("f_alo", [P, FT, BLK], F32R)
        gated = sb("f_gated", [P, 2, BLK])
        sumsq, var, rstd, exponent = (sb(f"f_{n}", [P, TPB]) for n in ("sumsq", "var", "rstd", "exponent"))
        bank = [ctx.enter_context(nc.psum_tensor(f"f_ps{i}", [P, BLK], F32)) for i in range(8)]
        names = ["mix_turned", "mix_hi", "mix_lo", "hi_split", "lo_split",
                 "multiplied", "x1_half", "squared", "var_ready", "powered", "scaled", "h2_turned", "h2_hi",
                 "h2_lo", "silued", "producted", "act_hi", "act_lo", "x2_half", "final", "stored", "pool_chain"]
        S = {n: sem(f"f_{n}") for n in names}
        S.update({n: F[n] for n in ("consts", "mix_loaded", "x_loaded")})
        x_blocks, mix_blocks, out_blocks = by_block(x), by_block(mix_scratch), by_block(out)
        one = lambda ap: ap.rearrange("o p t n -> (o p) t n")
        done = lambda b, j: b * ITEMS + (j + 2)
        is_first = lambda b: isinstance(b, int) and b == 0

        def rounds(eng, project, feed_forward, final_norm):
            project(0)
            with eng.Fori(0, BLOCKS - 1) as b:
                feed_forward(b)
                project(b + 1)
            feed_forward(BLOCKS - 1)
            final_norm(BLOCKS - 1)

        block = ctx.enter_context(nc.Block())

        @block.sync
        def _(sp):
            def load(b):
                if not is_first(b):
                    sp.wait_ge(S["h2_turned"], b * KC)
                    sp.dma_start(natural[:], one(mix_blocks[ds(b, 1)])).then_inc(S["mix_loaded"], 16)
                    sp.wait_ge(S["x1_half"], b * (2 * TPB))
                    sp.dma_start(x_in[:], one(x_blocks[ds(b, 1)])).then_inc(S["x_loaded"], 16)
                with sp.Fori(0, ITEMS // 2) as pair:
                    for s in range(2):
                        sp.wait_ge(S["lo_split"], b * ITEMS + pair * 2 + (s + 1))
                        sp.dma_start(w_raw[s][:], w_stream[ds(pair * 2 + (s + 2), 1)]
                                     .rearrange("o p n -> (o p) n")).then_inc(w_loaded[s], 16)

            load(0)
            with sp.Fori(1, BLOCKS) as b:
                load(b)
            for s in range(2):
                sp.wait_ge(w_loaded[s], 16 * (BLOCKS * ITEMS // 2 + 1))

        @block.gpsimd
        def _(pool):
            pool.memset(exponent[:], -0.5).then_inc(S["pool_chain"], 1)
            pool.wait_ge(S["pool_chain"], 1)
            with pool.Fori(0, BLOCKS) as b:
                for which in range(2):
                    pool.wait_ge(S["var_ready"], b * 2 + (which + 1))
                    pool.tensor_tensor(rstd[:], var[:], exponent[:], ALU.pow).then_inc(S["powered"], 1)
                for t in range(TPB):
                    pool.wait_ge(S["final"], b * TPB + (t + 1))
                    pool.dma_start(out_blocks[ds(b, 1), :, t, :].rearrange("o p n -> (o p) n"),
                                   x_sum[:, t, :]).then_inc(S["stored"], 16)
            pool.wait_ge(S["stored"], 16 * BLOCKS * TPB)

        @block.scalar
        def _(act):
            def split_hi(b, j):
                s = j % 2
                act.wait_ge(w_loaded[s], b * (ITEMS // 2 * 16) + (j // 2 + 1) * 16)
                act.wait_ge(S["multiplied"], b * ITEMS + j)
                act.activation(w_hi[s][:], w_raw[s][:], ACT.Copy).then_inc(S["hi_split"], 1)

            def squares(b, which, source, t):
                act.wait_ge(S[source], b * (2 * TPB) + (TPB + t + 1))
                if which or t or not is_first(b):
                    act.wait_ge(S["squared"], b * (2 * TPB) + (which * TPB + t))
                act.activation(junk, x_sum[:, t, :], ACT.Square, accum_out=sumsq[:, t:t + 1])\
                   .then_inc(S["squared"], 1)

            def project(b):
                for k in range(KC):
                    act.wait_ge(S["mix_turned"], b * KC + (k + 1))
                    act.activation(turned_hi[:, k, :], bank[(k + 4) % 8][:], ACT.Copy).then_inc(S["mix_hi"], 1)
                for j in range(OUT_ITEMS):
                    split_hi(b, j + 1)
                    if not is_first(b) and j < 2:
                        squares(b - 1, 1, "x2_half", 2 * j)
                        squares(b - 1, 1, "x2_half", 2 * j + 1)
                for t in range(TPB):
                    squares(b, 0, "x1_half", t)

            junk = act_hi[:, 0:2, :].rearrange("p a n -> p (a n)")
            act.preload_act_table_set("silu_and_others")
            split_hi(0, 0)
            act.wait_ge(S["consts"], 32)

            def feed_forward(b):
                for k in range(KC):
                    act.wait_ge(S["h2_turned"], b * KC + (k + 1))
                    act.activation(turned_hi[:, k, :], bank[k][:], ACT.Copy, scale=g_ffn[:, k:k + 1])\
                       .then_inc(S["h2_hi"], 1)
                with act.Fori(0, FT // 2) as pair:
                    for e in range(2):
                        item = b * ITEMS + pair * 4 + (GATE_ITEM + 2 * e)
                        f = b * FT + pair * 2 + e
                        for n in (1, 2):
                            s = n % 2
                            loads = b * (ITEMS // 2 * 16) + pair * 32 + ((GATE_ITEM + 2 * e + n) // 2 + 1) * 16
                            act.wait_ge(w_loaded[s], loads)
                            act.wait_ge(S["multiplied"], item + n)
                            act.activation(w_hi[s][:], w_raw[s][:], ACT.Copy).then_inc(S["hi_split"], 1)
                            if n == 1:
                                act.wait_ge(S["multiplied"], item + 2)
                                act.wait_ge(S["act_lo"], f + 1)
                                act.activation(gated[:, e, :], bank[2 * e][:], ACT.Silu)\
                                   .then_inc(S["silued"], 1)
                        act.wait_ge(S["producted"], f + 3)
                        act.activation(act_hi[:, ds(pair * 2 + e, 1), :].rearrange("p o n -> p (o n)"),
                                       gated[:, e, :], ACT.Copy).then_inc(S["act_hi"], 1)
                for j in range(DOWN_ITEM, ITEMS):
                    if isinstance(b, int) and j == ITEMS - 1:
                        break
                    split_hi(b, j + 1)

            def final_norm(b):
                for t in range(TPB):
                    squares(b, 1, "x2_half", t)

            rounds(act, project, feed_forward, final_norm)

        @block.vector
        def _(dve):
            def split_lo(s, number):
                dve.wait_ge(S["hi_split"], number + 1)
                dve.tensor_tensor(w_lo[s][:], w_raw[s][:], w_hi[s][:].bitcast(F32), ALU.subtract)\
                   .then_inc(S["lo_split"], 1)

            def add_half(b, item, half, first_bank, inc, source):
                cols = slice(half * HALF, (half + 1) * HALF)
                dve.wait_ge(S["multiplied"], done(b, item))
                for t in range(TPB):
                    dve.tensor_tensor(x_sum[:, t, cols], bank[first_bank + t][:], source[:, t, cols], ALU.add)\
                       .then_inc(S[inc], 1)

            def variance(b, which):
                dve.wait_ge(S["squared"], b * (2 * TPB) + (which + 1) * TPB)
                if which or not is_first(b):
                    dve.wait_ge(S["powered"], b * 2 + which)
                dve.tensor_scalar(var[:], sumsq[:], 1.0 / D_MODEL, EPS, ALU.mult, ALU.add).then_inc(S["var_ready"], 1)
                dve.wait_ge(S["powered"], b * 2 + (which + 1))

            def scale_out(b):
                for t in range(TPB):
                    dve.scalar_tensor_tensor(out=x_sum[:, t, :], in0=x_sum[:, t, :], scalar=rstd[:, t:t + 1],
                                             in1=g_final[:], op0=ALU.mult, op1=ALU.mult).then_inc(S["final"], 1)

            def project(b):
                for k in range(KC):
                    dve.wait_ge(S["mix_hi"], b * KC + (k + 1))
                    dve.tensor_tensor(turned_lo[:, k, :], bank[(k + 4) % 8][:], turned_hi[:, k, :].bitcast(F32),
                                      ALU.subtract).then_inc(S["mix_lo"], 1)
                for j in range(OUT_ITEMS):
                    split_lo((j + 1) % 2, b * ITEMS + (j + 1))
                    if not is_first(b) and j == 1:
                        variance(b - 1, 1)
                    if not is_first(b) and j == 2:
                        scale_out(b - 1)
                    if j == OUT_ITEMS // 2 - 1:
                        dve.wait_ge(S["x_loaded"], b * 16 + 16)
                        if not is_first(b):
                            dve.wait_ge(S["stored"], b * (16 * TPB))
                    if j == OUT_ITEMS // 2:
                        add_half(b, OUT_ITEMS // 2 - 1, 0, 4, "x1_half", x_in)
                add_half(b, OUT_ITEMS - 1, 1, 0, "x1_half", x_in)
                variance(b, 0)
                for t in range(TPB):
                    dve.tensor_scalar(natural[:, t, :], x_sum[:, t, :], rstd[:, t:t + 1], None, ALU.mult)\
                       .then_inc(S["scaled"], 1)

            def feed_forward(b):
                for k in range(KC):
                    dve.wait_ge(S["h2_hi"], b * KC + (k + 1))
                    dve.scalar_tensor_tensor(out=turned_lo[:, k, :], in0=bank[k][:], scalar=g_ffn[:, k:k + 1],
                                             in1=turned_hi[:, k, :].bitcast(F32), op0=ALU.mult,
                                             op1=ALU.subtract).then_inc(S["h2_lo"], 1)
                with dve.Fori(0, FT // 2) as pair:
                    for e in range(2):
                        item = b * ITEMS + pair * 4 + (GATE_ITEM + 2 * e)
                        f = b * FT + pair * 2 + e
                        split_lo(1, item + 1)
                        split_lo(0, item + 2)
                        dve.wait_ge(S["multiplied"], item + 3)
                        dve.wait_ge(S["silued"], f + 1 + 2)
                        dve.tensor_tensor(gated[:, e, :], bank[2 * e + 1][:], gated[:, e, :], ALU.mult)\
                           .then_inc(S["producted"], 1)
                        dve.wait_ge(S["act_hi"], f + 1)
                        here = (slice(None), ds(pair * 2 + e, 1), slice(None))
                        flat = lambda t: t.rearrange("p o n -> p (o n)")
                        dve.tensor_tensor(flat(act_lo[here]), gated[:, e, :], flat(act_hi[here]).bitcast(F32),
                                          ALU.subtract).then_inc(S["act_lo"], 1)
                for j in range(DOWN_ITEM, ITEMS):
                    if not (isinstance(b, int) and j == ITEMS - 1):
                        split_lo((j + 1) % 2, b * ITEMS + (j + 1))
                    if j == DOWN_ITEM + FT // 2:
                        add_half(b, DOWN_ITEM + FT // 2 - 1, 0, 4, "x2_half", x_sum)
                add_half(b, ITEMS - 1, 1, 0, "x2_half", x_sum)

            def final_norm(b):
                variance(b, 1)
                scale_out(b)

            split_lo(0, 0)
            dve.sem_inc(S["producted"], 2)
            dve.sem_inc(S["act_lo"], 2)
            rounds(dve, project, feed_forward, final_norm)

        @block.tensor
        def _(pe):
            def passes(s, chunk, left_hi, left_lo, outs, start, stop):
                cols = slice(chunk * HALF, (chunk + 1) * HALF)
                for t in range(TPB):
                    tok = slice(t * P, (t + 1) * P)
                    for n, (a, w) in enumerate(((left_hi, w_hi), (left_lo, w_hi), (left_hi, w_lo))):
                        mm = pe.matmul(bank[outs + t][:], a[:, tok], w[s][:, cols],
                                       start=(start and n == 0), stop=(stop and n == 2))
                return mm

            pe.sem_inc(S["multiplied"], 1)
            pe.sem_inc(S["silued"], 2)

            def project(b):
                pe.wait_ge(S["mix_loaded"], b * 16 + 16)
                for k in range(KC):
                    if k in (0, 4) and not is_first(b):
                        pe.wait_ge(S["x2_half"], b * (2 * TPB) + (k - 4))
                    for t in range(TPB):
                        mm = pe.transpose(bank[(k + 4) % 8][:, t * P:(t + 1) * P],
                                          natural[:, t, k * P:(k + 1) * P], ident[:])
                    mm.then_inc(S["mix_turned"], 1)
                for j in range(OUT_ITEMS):
                    pe.wait_ge(S["lo_split"], b * ITEMS + (j + 1))
                    if j in (0, 2):
                        pe.wait_ge(S["mix_lo"], b * KC + 4 * (j // 2 + 1))
                    half, first = divmod(j, OUT_ITEMS // 2)
                    for n in range(2):
                        c = 2 * first + n
                        mm = passes(j % 2, n, turned_hi[:, c, :], turned_lo[:, c, :],
                                    4 * (1 - half), c == 0, c == KC - 1)
                    mm.then_inc(S["multiplied"], 1)

            def feed_forward(b):
                for t in range(TPB):
                    pe.wait_ge(S["scaled"], b * TPB + (t + 1))
                    for k in range(KC):
                        mm = pe.transpose(bank[k][:, t * P:(t + 1) * P], natural[:, t, k * P:(k + 1) * P], ident[:])
                        if t == TPB - 1:
                            mm.then_inc(S["h2_turned"], 1)
                with pe.Fori(0, FT // 2) as pair:
                    for e in range(2):
                        f = b * FT + pair * 2 + e
                        for n in range(2):
                            pe.wait_ge(S["lo_split"], b * ITEMS + pair * 4 + (GATE_ITEM + 2 * e + n + 1))
                            pe.wait_ge(S["producted" if n else "silued"], f + 1)
                            for c in range(KC):
                                if e == 0 and n == 0:
                                    pe.wait_ge(S["h2_lo"], b * KC + (c + 1))
                                w = slice(c * P, (c + 1) * P)
                                for m, (a, h) in enumerate(((w_hi, turned_hi), (w_lo, turned_hi), (w_hi, turned_lo))):
                                    mm = pe.matmul(bank[2 * e + n][:], a[n][:, w], h[:, c, :],
                                                   start=(c == 0 and m == 0), stop=(c == KC - 1 and m == 2))
                            mm.then_inc(S["multiplied"], 1)
                for j in range(DOWN_ITEM, ITEMS):
                    pe.wait_ge(S["lo_split"], b * ITEMS + (j + 1))
                    half, first = divmod(j - DOWN_ITEM, FT // 2)
                    if half == 0:
                        pe.wait_ge(S["act_lo"], b * FT + (2 * first + 4))
                    for n in range(2):
                        f = 2 * first + n
                        mm = passes(j % 2, n, act_hi[:, f, :], act_lo[:, f, :], 4 * (1 - half), f == 0, f == FT - 1)
                    mm.then_inc(S["multiplied"], 1)

            rounds(pe, project, feed_forward, lambda b: None)


def build_program(nc, D, out):
    qk_scratch = nc.dram_tensor("qk_scratch", [2, len(QK_ORDER) * GROUP, SEQ], F32).ap()
    v_scratch = nc.dram_tensor("v_scratch", [2, SEQ, GROUP], F32).ap()
    mix_scratch = nc.dram_tensor("mix_scratch", [SEQ, D_MODEL], F32).ap()
    ctx = ExitStack()
    with ctx:
        sb = lambda n, s, d=F32: ctx.enter_context(nc.sbuf_tensor(n, s, d))
        ident = sb("ident_sb", [P, P])
        loaded, cast = ctx.enter_context(nc.semaphore("m_loaded")), ctx.enter_context(nc.semaphore("m_cast"))
        with nc.sbuf_tensor("hT_hi", [P, KC, SEQ], F32R) as hT_hi, nc.sbuf_tensor("hT_lo", [P, KC, SEQ], F32R) as hT_lo:
            with nc.Block() as block:
                @block.sync
                def _(sp):
                    sp.dma_start(ident[:], D["ident"]).then_inc(loaded, 16)
                    sp.wait_ge(loaded, 16)
            with ExitStack() as ahead:
                w_first = ahead.enter_context(nc.sbuf_tensor("w_first", [P, KC, P], F32))
                w_first_loaded = ahead.enter_context(nc.semaphore("w_first_loaded"))
                phase_norm(nc, D["x"], D["g_attn"][0].partition_broadcast(P), ident, hT_hi, hT_lo,
                           w_first, D["w_qk"][0], w_first_loaded)
                v_raw = [ahead.enter_context(nc.sbuf_tensor(f"v_raw{s}", [P, GROUP], F32)) for s in range(V_AHEAD)]
                v_loaded = [ahead.enter_context(nc.semaphore(f"v_loaded{s}")) for s in range(V_AHEAD)]
                phase_qk(nc, D["w_qk"], D["positions"], D["inv_freq"], D["rotary"], hT_hi, hT_lo, qk_scratch,
                         w_first, w_first_loaded, D["w_v"], v_raw, v_loaded)
                phase_v(nc, D["w_v"], v_raw, v_loaded, w_first, hT_hi, hT_lo, v_scratch)
        with ExitStack() as masks:
            small = lambda n, d: masks.enter_context(nc.sbuf_tensor(n, [P, P], d))
            ident_bf, raw = small("ident_bf", BF16), small("mask_raw", F32)
            strict, causal = small("strict", F32), small("causal", BF16)
            with nc.Block() as block:
                @block.sync
                def _(sp):
                    sp.dma_start(raw[:], D["causal_mask"]).then_inc(loaded, 16)
                    sp.dma_start(strict[:], D["strict_mask"]).then_inc(loaded, 16)

                @block.vector
                def _(dve):
                    dve.wait_ge(loaded, 48)
                    dve.tensor_copy(ident_bf[:], ident[:]).then_inc(cast, 1)
                    dve.tensor_copy(causal[:], raw[:]).then_inc(cast, 1)
                    dve.wait_ge(cast, 2)
            phase_differential(nc, qk_scratch, v_scratch, D["lambdas"].partition_broadcast(P),
                               D["g_diff"][0].partition_broadcast(P), ident, ident_bf, causal, mix_scratch)
            ahead = ahead_buffers(nc, masks)
            phase_stick_breaking(nc, qk_scratch, v_scratch, D["g_stick"][0].partition_broadcast(P), ident,
                                 strict, mix_scratch, ahead,
                                 (D["x"], mix_scratch, D["w_stream"], D["g_ffn"], D["g_final"][0].partition_broadcast(P)))
            phase_ffn(nc, ahead, D["x"], mix_scratch, D["w_stream"], ident, out)


def host_arrays(x, positions, norm_attn_g, w_in, lambda_q1, lambda_k1, lambda_q2, lambda_k2, diff_subln_g,
                sb_norm_g, w_out, norm_ffn_g, w_gate, w_up, w_down, final_norm_g):
    chunked = w_in[0].reshape(KC, P, -1)
    w_qk = np.stack([chunked[:, :, COL[kind] + f * P:COL[kind] + (f + 1) * P].transpose(1, 0, 2)
                     for kind in QK_ORDER for f in range(QK_TILES)])
    w_v = np.stack([chunked[:, :, COL[kind]:COL[kind] + GROUP] for kind in ("dv", "sv")])

    def natural(w):
        return w.reshape(-1, 2, P, 2, HALF).transpose(3, 0, 2, 1, 4).reshape(-1, P, D_MODEL)

    def by_tile(w):
        return w.reshape(KC, P, FT, P).transpose(2, 1, 0, 3).reshape(FT, P, D_MODEL)

    gate_up = np.stack([by_tile(w_gate[0]), by_tile(w_up[0])], 1).reshape(2 * FT, P, D_MODEL)
    items = [natural(w_out[0]), gate_up, natural(w_down[0])]
    w_stream = np.concatenate(items + [items[0][:2]])

    half = HEAD_DIM // 8
    inv_freq = np.zeros((P, 1), np.float32)
    rotary = np.zeros((P, P), np.float32)
    for first in range(0, P, HEAD_DIM):
        for i in range(half):
            inv_freq[first + i] = inv_freq[first + half + i] = np.float32(500000.0) ** np.float32(-i / half)
            rotary[first + half + i, first + i] = -1.0
            rotary[first + i, first + half + i] = 1.0
    row, col = np.arange(P)[:, None], np.arange(P)[None, :]
    return dict(
        x=x[0], positions=positions, g_attn=norm_attn_g, w_qk=w_qk, w_v=w_v, w_stream=w_stream,
        lambdas=np.concatenate([lambda_q1, lambda_k1, lambda_q2, lambda_k2]),
        g_diff=np.tile(diff_subln_g, (1, GROUP // (2 * HEAD_DIM))), g_stick=np.tile(sb_norm_g, (1, HEADS)),
        g_ffn=norm_ffn_g.reshape(KC, P).transpose(1, 0), g_final=final_norm_g.reshape(1, D_MODEL),
        inv_freq=inv_freq, rotary=rotary, ident=np.eye(P, dtype=np.float32),
        causal_mask=np.where(col > row, -1e30, 0.0).astype(np.float32),
        strict_mask=np.where(col >= row, -1e30, 0.0).astype(np.float32))


def kernel(**inputs):
    from concourse import bacc
    from concourse.bass_utils import run_bass_kernel_spmd

    arrays = {n: np.ascontiguousarray(a) for n, a in host_arrays(**{k: np.asarray(v) for k, v in inputs.items()}).items()}
    nc = bacc.Bacc("TRN2", target_bir_lowering=False, num_devices=1)
    dram = {n: nc.dram_tensor("in_" + n, a.shape, mybir.dt.from_np(a.dtype), kind="ExternalInput").ap() for n, a in arrays.items()}
    out = nc.dram_tensor("out", [SEQ, D_MODEL], F32, kind="ExternalOutput").ap()
    build_program(nc, dram, out)
    result = run_bass_kernel_spmd(nc, [{"in_" + n: a for n, a in arrays.items()}], core_ids=[0])
    return result.results[0]["out"].reshape(1, SEQ, D_MODEL)
```
